# Optimizing a Trainium2 kernel written in Bass

```python
import math
import jax, jax.numpy as jnp
from jax import lax
import numpy as np
import jax
import jax.numpy as jnp

D_MODEL = 1024
BATCH = 1
SEQ = 256
DEPTH = 2

N_A_LAYERS = DEPTH // 2
N_B_LAYERS = DEPTH - N_A_LAYERS
POOL_WINDOWS = (2, 4, 8, 16)
N_POOL_GROUPS = len(POOL_WINDOWS)
POOL_GROUP = D_MODEL // N_POOL_GROUPS
HEAD_DIM = 64
N_HEADS = D_MODEL // HEAD_DIM
MOBA_BLOCK = 256
MOBA_TOPK = 3
Q_BLOCK = 128
NUM_BUCKETS = 32
MAX_DISTANCE = 128
D_FF = -(-8 * D_MODEL // (3 * 256)) * 256
EPS = 1e-6


def rmsnorm(x, g):
    xf = x.astype(jnp.float32)
    y = xf * lax.rsqrt(jnp.mean(xf * xf, axis=-1, keepdims=True) + EPS)
    return (y * g.astype(jnp.float32)).astype(x.dtype)

def pool_mixer(h, w, scale):
    B, T, D = h.shape
    hf = h.astype(jnp.float32)
    csum = jnp.concatenate([jnp.zeros((B, 1, D), jnp.float32), jnp.cumsum(hf, axis=1)], axis=1)
    t = jnp.arange(T)
    outs = []
    for g, win in enumerate(POOL_WINDOWS):
        sl = slice(g * POOL_GROUP, (g + 1) * POOL_GROUP)
        start = jnp.maximum(t + 1 - win, 0)
        cnt = (t + 1 - start).astype(jnp.float32)
        window_sum = csum[:, 1:, sl] - jnp.take(csum[:, :, sl], start, axis=1)
        outs.append(window_sum / cnt[None, :, None] - hf[:, :, sl])
    d = jnp.stack(outs, axis=2).astype(h.dtype)
    y = jnp.einsum('btgc,gce->btge', d, w).reshape(B, T, D)
    return y * scale

def swiglu(h, w_gate_up, w_down):
    gu = h @ w_gate_up
    gate, up = jnp.split(gu, 2, axis=-1)
    return (jax.nn.silu(gate) * up) @ w_down

def rel_bucket(n):
    max_exact = NUM_BUCKETS // 2
    nf = jnp.maximum(n, max_exact).astype(jnp.float32)
    large = max_exact + (jnp.log(nf / max_exact) / math.log(MAX_DISTANCE / max_exact)
                         * (NUM_BUCKETS - max_exact)).astype(jnp.int32)
    large = jnp.minimum(large, NUM_BUCKETS - 1)
    return jnp.where(n < max_exact, n, large)

def shared_kv(x, g, w_kv):
    B, T, D = x.shape
    h = rmsnorm(x, g)
    kv = h @ w_kv
    k, v = jnp.split(kv, 2, axis=-1)
    n_blocks = -(-T // MOBA_BLOCK)
    pad = n_blocks * MOBA_BLOCK - T

    def to_blocks(a):
        a = a.reshape(B, T, N_HEADS, HEAD_DIM).transpose(0, 2, 1, 3)
        a = jnp.pad(a, ((0, 0), (0, 0), (0, pad), (0, 0)))
        return a.reshape(B, N_HEADS, n_blocks, MOBA_BLOCK, HEAD_DIM)

    k_blocks = to_blocks(k)
    v_blocks = to_blocks(v)
    k_mean = jnp.mean(k_blocks.astype(jnp.float32), axis=3).astype(k_blocks.dtype)
    return k_blocks, v_blocks, k_mean

def moba_attention(q, k_blocks, v_blocks, k_mean, rel_bias):
    B, T = q.shape[0], q.shape[1]
    n_q = T // Q_BLOCK
    n_blocks = k_blocks.shape[2]
    topk = min(MOBA_TOPK, n_blocks)
    scale = HEAD_DIM ** -0.5
    h_idx = jnp.arange(N_HEADS)[:, None, None]
    bias_t = rel_bias.T.astype(jnp.float32)
    q_blocks = q.transpose(0, 2, 1, 3).reshape(B, N_HEADS, n_q, Q_BLOCK, HEAD_DIM)
    q_blocks = q_blocks.transpose(0, 2, 1, 3, 4).reshape(B * n_q, N_HEADS, Q_BLOCK, HEAD_DIM)
    b_idx = jnp.repeat(jnp.arange(B), n_q)
    qb_idx = jnp.tile(jnp.arange(n_q), B)
    j_blk = jnp.arange(MOBA_BLOCK)

    def step(args):
        qblk, b, qb = args
        kb = k_blocks[b]
        vb = v_blocks[b]
        km = k_mean[b]
        qs = qb * Q_BLOCK
        own = qs // MOBA_BLOCK
        qpos = qs + jnp.arange(Q_BLOCK)
        gate = jnp.einsum('hqd,hnd->hqn', qblk, km).astype(jnp.float32)
        gate = jnp.where(jnp.arange(n_blocks)[None, None, :] < own, gate, -jnp.inf)
        _, sel = lax.top_k(gate, topk)
        sel_valid = jnp.arange(topk) < jnp.minimum(own, topk)
        k_sel = kb[h_idx, sel]
        v_sel = vb[h_idx, sel]
        s_sel = jnp.einsum('hqd,hqkjd->hqkj', qblk, k_sel).astype(jnp.float32) * scale
        kpos_sel = sel[..., None] * MOBA_BLOCK + j_blk
        k_own = lax.dynamic_index_in_dim(kb, own, axis=1, keepdims=False)
        v_own = lax.dynamic_index_in_dim(vb, own, axis=1, keepdims=False)
        s_own = jnp.einsum('hqd,hjd->hqj', qblk, k_own).astype(jnp.float32) * scale
        kpos_own = own * MOBA_BLOCK + j_blk
        L_sel = topk * MOBA_BLOCK
        s = jnp.concatenate([s_sel.reshape(N_HEADS, Q_BLOCK, L_sel), s_own], axis=-1)
        kpos = jnp.concatenate([kpos_sel.reshape(N_HEADS, Q_BLOCK, L_sel),
                                jnp.broadcast_to(kpos_own[None, None, :], (N_HEADS, Q_BLOCK, MOBA_BLOCK))], axis=-1)
        valid_sel = jnp.broadcast_to(sel_valid[None, None, :, None], (N_HEADS, Q_BLOCK, topk, MOBA_BLOCK)).reshape(N_HEADS, Q_BLOCK, L_sel)
        valid_own = jnp.broadcast_to(kpos_own[None, None, :] <= qpos[None, :, None], (N_HEADS, Q_BLOCK, MOBA_BLOCK))
        valid = jnp.concatenate([valid_sel, valid_own], axis=-1)
        bucket = rel_bucket(jnp.maximum(qpos[None, :, None] - kpos, 0))
        bias = bias_t[h_idx, bucket]
        s = jnp.where(valid, s + bias, -jnp.inf)
        p = jax.nn.softmax(s, axis=-1).astype(vb.dtype)
        p_sel = p[..., :L_sel].reshape(N_HEADS, Q_BLOCK, topk, MOBA_BLOCK)
        p_own = p[..., L_sel:]
        return (jnp.einsum('hqkj,hqkjd->hqd', p_sel, v_sel)
                + jnp.einsum('hqj,hjd->hqd', p_own, v_own))

    o = lax.map(step, (q_blocks, b_idx, qb_idx))
    o = o.reshape(B, n_q, N_HEADS, Q_BLOCK, HEAD_DIM).transpose(0, 1, 3, 2, 4)
    return o.reshape(B, T, D_MODEL)

def first_inputs(seed: int = 0) -> dict:
    key = jax.random.key(seed)
    ks = jax.random.split(key, 14)
    f32 = jnp.float32
    nrm = lambda k, shape: jax.random.normal(k, shape, f32)
    x = nrm(ks[0], (BATCH, SEQ, D_MODEL))
    norm_mixer = 1.0 + 0.05 * nrm(ks[1], (DEPTH, D_MODEL))
    norm_ffn = 1.0 + 0.05 * nrm(ks[2], (DEPTH, D_MODEL))
    pool_w = nrm(ks[3], (N_A_LAYERS, N_POOL_GROUPS, POOL_GROUP, POOL_GROUP)) * POOL_GROUP ** -0.5
    pool_scale = 1.0 + 0.05 * nrm(ks[4], (N_A_LAYERS, D_MODEL))
    kv_norm = 1.0 + 0.05 * nrm(ks[5], (D_MODEL,))
    w_kv = nrm(ks[6], (D_MODEL, 2 * D_MODEL)) * D_MODEL ** -0.5
    w_q = nrm(ks[7], (N_B_LAYERS, D_MODEL, D_MODEL)) * D_MODEL ** -0.5
    w_o = nrm(ks[8], (N_B_LAYERS, D_MODEL, D_MODEL)) * D_MODEL ** -0.5
    rel_bias = 0.5 * nrm(ks[9], (NUM_BUCKETS, N_HEADS))
    w_gate_up = nrm(ks[10], (DEPTH, D_MODEL, 2 * D_FF)) * D_MODEL ** -0.5
    w_down = nrm(ks[11], (DEPTH, D_FF, D_MODEL)) * D_FF ** -0.5
    final_norm = 1.0 + 0.05 * nrm(ks[12], (D_MODEL,))
    return {'x': x, 'norm_mixer': norm_mixer, 'norm_ffn': norm_ffn, 'pool_w': pool_w,
            'pool_scale': pool_scale, 'kv_norm': kv_norm, 'w_kv': w_kv, 'w_q': w_q, 'w_o': w_o,
            'rel_bias': rel_bias, 'w_gate_up': w_gate_up, 'w_down': w_down, 'final_norm': final_norm}

def first_block(x, norm_mixer, norm_ffn, pool_w, pool_scale, kv_norm, w_kv, w_q, w_o,
              rel_bias, w_gate_up, w_down, final_norm):
    B, T, D = x.shape
    k_blocks = v_blocks = k_mean = None
    for layer in range(DEPTH):
        if layer < N_A_LAYERS:
            x = x + pool_mixer(rmsnorm(x, norm_mixer[layer]), pool_w[layer], pool_scale[layer])
        else:
            j = layer - N_A_LAYERS
            if j == 0:
                k_blocks, v_blocks, k_mean = shared_kv(x, kv_norm, w_kv)
            h = rmsnorm(x, norm_mixer[layer])
            q = (h @ w_q[j]).reshape(B, T, N_HEADS, HEAD_DIM)
            o = moba_attention(q, k_blocks, v_blocks, k_mean, rel_bias)
            x = x + o @ w_o[j]
        x = x + swiglu(rmsnorm(x, norm_ffn[layer]), w_gate_up[layer], w_down[layer])
    return rmsnorm(x, final_norm)


DEPTH_2 = 1

CTX_LEN = 256
GRID_W = 64

HG_HEADS = 4
HG_DK = 128
HG_DV = 128
HG_KEY_WIDTH = HG_HEADS * HG_DK
HG_WIDTH = HG_HEADS * HG_DV
HG_CHUNK = 16

CM_CHUNK = 128
CM_GROUPS = 4
CM_WIDTH = 512
CM_GROUP_DIM = CM_WIDTH // CM_GROUPS
ROWS_PER_CHUNK = CM_CHUNK // GRID_W

SPLIT_IDX = (HG_KEY_WIDTH, 2 * HG_KEY_WIDTH, 3 * HG_KEY_WIDTH, 3 * HG_KEY_WIDTH + HG_WIDTH,
             3 * HG_KEY_WIDTH + 2 * HG_WIDTH, 3 * HG_KEY_WIDTH + 2 * HG_WIDTH + 2 * CM_WIDTH)
D_IN = 3 * HG_KEY_WIDTH + 2 * HG_WIDTH + 2 * CM_WIDTH + 2 * D_MODEL

N_EXPERTS = 64
TOP_K = 8
N_EXPERT_GROUPS = 8
TOPK_GROUPS = 4
D_EXPERT = 256
D_SHARED = 256
ROUTED_SCALE = 2.5
MOE_BLOCK = 256


def rms_norm(x, g):
    x32 = x.astype(jnp.float32)
    y = x32 * lax.rsqrt(jnp.mean(x32 * x32, axis=-1, keepdims=True) + EPS)
    return (y * g.astype(jnp.float32)).astype(x.dtype)

def layer_norm(x, g, b):
    x32 = x.astype(jnp.float32)
    xc = x32 - jnp.mean(x32, axis=-1, keepdims=True)
    y = xc * lax.rsqrt(jnp.mean(xc * xc, axis=-1, keepdims=True) + EPS)
    return (y * g.astype(jnp.float32) + b.astype(jnp.float32)).astype(x.dtype)

def hgrn2_gates(z, lb):
    B, T, _ = z.shape
    z = z.astype(jnp.float32).reshape(B, T, HG_HEADS, HG_DK)
    lb = lb.reshape(HG_HEADS, HG_DK)
    log_f = jnp.log(lb + (1.0 - lb) * jax.nn.sigmoid(z))
    k = (1.0 - lb) * jax.nn.sigmoid(-z)
    return k, log_f

def gla_chunk_scan(q, k, v, log_f, s0, readout):
    B, T, H, DK = k.shape
    DV = v.shape[-1]
    n = T // HG_CHUNK

    def to_chunks(a):
        return a.astype(jnp.float32).reshape(B, n, HG_CHUNK, H, a.shape[-1]).transpose(1, 0, 3, 2, 4)

    kc, vc = to_chunks(k), to_chunks(v)
    bc = jnp.cumsum(to_chunks(log_f), axis=3)
    tri = jnp.tril(jnp.ones((HG_CHUNK, HG_CHUNK), dtype=bool))
    mid = HG_CHUNK // 2 - 1

    def step(S, xs):
        k_, v_, b_ = xs[0], xs[1], xs[2]
        b_last = b_[:, :, -1:, :]
        S_new = jnp.exp(b_last[:, :, 0, :, None]) * S + jnp.einsum('bhsd,bhsv->bhdv', k_ * jnp.exp(b_last - b_), v_)
        if not readout:
            return S_new, None
        q_ = xs[3]
        b_mid = b_[:, :, mid:mid + 1, :]
        A = jnp.einsum('bhtd,bhsd->bhts', q_ * jnp.exp(b_ - b_mid), k_ * jnp.exp(b_mid - b_))
        A = jnp.where(tri, A, 0.0)
        o = jnp.einsum('bhts,bhsv->bhtv', A, v_) + jnp.einsum('bhtd,bhdv->bhtv', q_ * jnp.exp(b_), S)
        return S_new, o

    xs = (kc, vc, bc, to_chunks(q)) if readout else (kc, vc, bc)
    S_fin, o = lax.scan(step, s0, xs)
    if readout:
        o = o.transpose(1, 0, 3, 2, 4).reshape(B, T, H, DV)
    return o, S_fin

def chunk_spatial_gating(p, n_chunks, ln_g, ln_b, w_s, b_s):
    a = jax.nn.gelu(p)
    u, v = jnp.split(a, 2, axis=-1)
    v = layer_norm(v, ln_g, ln_b)
    B, T, _ = v.shape
    v = v.reshape(B, n_chunks, CM_CHUNK, CM_GROUPS, CM_GROUP_DIM)
    z = jnp.einsum('gpq,bnqgc->bnpgc', w_s, v) + b_s[None, None, :, :, None]
    return u * z.reshape(B, T, CM_WIDTH)

def token_mixer(h_lat, h_ctx, w_in, lb, g_out, ln_g, ln_b, w_s, b_s, w_a, w_b, w_o,
                n_lat_chunks, n_ctx_chunks, need_ctx):
    B, T, _ = h_lat.shape
    L = h_ctx.shape[1]
    p_lat = h_lat @ w_in
    p_ctx = h_ctx @ w_in
    ql, fl_fwd, fl_bwd, il, gl, cml, gtl = jnp.split(p_lat, SPLIT_IDX, axis=-1)
    qc, fc_fwd, fc_bwd, ic, gc, cmc, gtc = jnp.split(p_ctx, SPLIT_IDX, axis=-1)

    q_lat = jax.nn.silu(ql).reshape(B, T, HG_HEADS, HG_DK)
    v_lat = il.reshape(B, T, HG_HEADS, HG_DV)
    q_ctx = jax.nn.silu(qc).reshape(B, L, HG_HEADS, HG_DK) if need_ctx else None
    v_ctx = ic.reshape(B, L, HG_HEADS, HG_DV)
    s0 = jnp.zeros((B, HG_HEADS, HG_DK, HG_DV), jnp.float32)

    lat_outs, ctx_outs = [], []
    for d, (f_lat, f_ctx) in enumerate(((fl_fwd, fc_fwd), (fl_bwd, fc_bwd))):
        rev = (lambda a: a[:, ::-1]) if d == 1 else (lambda a: a)
        k_l, lf_l = hgrn2_gates(f_lat, lb[d])
        k_c, lf_c = hgrn2_gates(f_ctx, lb[d])
        q_c = rev(q_ctx) if need_ctx else None
        oc, s_ctx = gla_chunk_scan(q_c, rev(k_c), rev(v_ctx), rev(lf_c), s0, need_ctx)
        ol, _ = gla_chunk_scan(rev(q_lat), rev(k_l), rev(v_lat), rev(lf_l), s_ctx, True)
        lat_outs.append(rev(ol))
        if need_ctx:
            ctx_outs.append(rev(oc))

    def merge(o, g, cm, gt, n_chunks, dtype):
        n_tok = o.shape[1]
        g = g.reshape(B, n_tok, HG_HEADS, HG_DV).astype(jnp.float32)
        a = (rms_norm(o, g_out) * jax.nn.silu(g)).reshape(B, n_tok, HG_WIDTH).astype(dtype)
        bm = chunk_spatial_gating(cm, n_chunks, ln_g, ln_b, w_s, b_s)
        ga, gb = jnp.split(gt, 2, axis=-1)
        y = jax.nn.sigmoid(ga) * (a @ w_a) + jax.nn.sigmoid(gb) * (bm @ w_b)
        return y @ w_o

    y_lat = merge(lat_outs[0] + lat_outs[1], gl, cml, gtl, n_lat_chunks, h_lat.dtype)
    y_ctx = merge(ctx_outs[0] + ctx_outs[1], gc, cmc, gtc, n_ctx_chunks, h_ctx.dtype) if need_ctx else None
    return y_lat, y_ctx

def swiglu_2(h, w_gu, w_down):
    gate, up = jnp.split(h @ w_gu, 2, axis=-1)
    return (jax.nn.silu(gate) * up) @ w_down

def moe_ffn(h, w_router, b_router, w_gu, w_down, w_sh_gu, w_sh_down):
    N, D = h.shape
    scores = jax.nn.sigmoid((h @ w_router).astype(jnp.float32))
    sel = scores + b_router.astype(jnp.float32)
    grp = sel.reshape(N, N_EXPERT_GROUPS, N_EXPERTS // N_EXPERT_GROUPS)
    grp_score = jnp.sum(lax.top_k(grp, 2)[0], axis=-1)
    _, top_g = lax.top_k(grp_score, TOPK_GROUPS)
    gmask = jnp.any(top_g[:, :, None] == jnp.arange(N_EXPERT_GROUPS)[None, None, :], axis=1)
    sel = jnp.where(jnp.repeat(gmask, N_EXPERTS // N_EXPERT_GROUPS, axis=1), sel, -jnp.inf)
    _, top_e = lax.top_k(sel, TOP_K)
    w = jnp.take_along_axis(scores, top_e, axis=1)
    w = w / jnp.sum(w, axis=-1, keepdims=True) * ROUTED_SCALE

    M = N * TOP_K
    flat_e = top_e.reshape(M).astype(jnp.int32)
    flat_tok = jnp.repeat(jnp.arange(N, dtype=jnp.int32), TOP_K)
    flat_w = w.reshape(M)
    counts = jnp.bincount(flat_e, length=N_EXPERTS).astype(jnp.int32)
    padded = (counts + MOE_BLOCK - 1) // MOE_BLOCK * MOE_BLOCK
    pad_end = jnp.cumsum(padded)
    pad_start = pad_end - padded
    start = jnp.cumsum(counts) - counts
    order = jnp.argsort(flat_e)
    se, stok, sw = flat_e[order], flat_tok[order], flat_w[order]
    dest = pad_start[se] + jnp.arange(M, dtype=jnp.int32) - start[se]
    NB = -(-M // MOE_BLOCK) + N_EXPERTS
    row_tok = jnp.full((NB * MOE_BLOCK,), N, jnp.int32).at[dest].set(stok)
    row_w = jnp.zeros((NB * MOE_BLOCK,), jnp.float32).at[dest].set(sw)
    block_e = jnp.clip(jnp.searchsorted(pad_end, jnp.arange(NB, dtype=jnp.int32) * MOE_BLOCK, side='right'),
                       0, N_EXPERTS - 1)
    h_pad = jnp.concatenate([h, jnp.zeros((1, D), h.dtype)], axis=0)

    def expert_block(acc, blk):
        tok, wts, e = blk
        out = swiglu_2(h_pad[tok], w_gu[e], w_down[e])
        return acc.at[tok].add(out * wts[:, None].astype(out.dtype)), None

    acc, _ = lax.scan(expert_block, jnp.zeros((N + 1, D), h.dtype),
                      (row_tok.reshape(NB, MOE_BLOCK), row_w.reshape(NB, MOE_BLOCK), block_e))
    return acc[:N] + swiglu_2(h, w_sh_gu, w_sh_down)

def second_inputs(seed: int = 0) -> dict:
    key = jax.random.key(seed)
    ks = jax.random.split(key, 26)

    def nrm(k, shape, scale):
        return jax.random.normal(k, shape, jnp.float32) * scale

    def gain(k, shape):
        return 1.0 + nrm(k, shape, 0.05)

    D = D_MODEL
    return {
        'x': nrm(ks[0], (BATCH, SEQ, D), 1.0),
        'c': nrm(ks[1], (BATCH, D), 1.0),
        'ctx': nrm(ks[2], (BATCH, CTX_LEN, D), 1.0),
        'c_ctx': nrm(ks[3], (D,), 1.0),
        'w_ada': nrm(ks[4], (DEPTH_2, D, 6 * D), 0.5 * D ** -0.5),
        'b_ada': nrm(ks[5], (DEPTH_2, 6 * D), 0.02),
        'g_pre_mix': gain(ks[6], (DEPTH_2, D)),
        'g_post_mix': gain(ks[7], (DEPTH_2, D)),
        'g_pre_ffn': gain(ks[8], (DEPTH_2, D)),
        'g_post_ffn': gain(ks[9], (DEPTH_2, D)),
        'w_in': nrm(ks[10], (DEPTH_2, D, D_IN), D ** -0.5),
        'lb_logits': nrm(ks[11], (2, DEPTH_2 + 1, HG_KEY_WIDTH), 0.1),
        'g_hgrn_out': gain(ks[12], (DEPTH_2, HG_DV)),
        'cm_ln_g': gain(ks[13], (DEPTH_2, CM_WIDTH)),
        'cm_ln_b': nrm(ks[14], (DEPTH_2, CM_WIDTH), 0.02),
        'w_spatial': nrm(ks[15], (DEPTH_2, CM_GROUPS, CM_CHUNK, CM_CHUNK), CM_CHUNK ** -0.5),
        'b_spatial': 1.0 + nrm(ks[16], (DEPTH_2, CM_CHUNK, CM_GROUPS), 0.1),
        'w_branch_a': nrm(ks[17], (DEPTH_2, HG_WIDTH, D), HG_WIDTH ** -0.5),
        'w_branch_b': nrm(ks[18], (DEPTH_2, CM_WIDTH, D), CM_WIDTH ** -0.5),
        'w_out': nrm(ks[19], (DEPTH_2, D, D), D ** -0.5),
        'w_router': nrm(ks[20], (DEPTH_2, D, N_EXPERTS), D ** -0.5),
        'b_router': nrm(ks[21], (DEPTH_2, N_EXPERTS), 0.01),
        'w_expert_gu': nrm(ks[22], (DEPTH_2, N_EXPERTS, D, 2 * D_EXPERT), D ** -0.5),
        'w_expert_down': nrm(ks[23], (DEPTH_2, N_EXPERTS, D_EXPERT, D), D_EXPERT ** -0.5),
        'w_shared_gu': nrm(ks[24], (DEPTH_2, D, 2 * D_SHARED), D ** -0.5),
        'w_shared_down': nrm(ks[25], (DEPTH_2, D_SHARED, D), D_SHARED ** -0.5),
    }

def second_block(x, c, ctx, c_ctx, w_ada, b_ada, g_pre_mix, g_post_mix, g_pre_ffn, g_post_ffn, w_in,
              lb_logits, g_hgrn_out, cm_ln_g, cm_ln_b, w_spatial, b_spatial, w_branch_a, w_branch_b,
              w_out, w_router, b_router, w_expert_gu, w_expert_down, w_shared_gu, w_shared_down):
    B, T, D = x.shape
    L = ctx.shape[1]
    rows = T // GRID_W
    n_lat_chunks = rows // ROWS_PER_CHUNK
    n_ctx_chunks = L // CM_CHUNK
    lower_bounds = jnp.cumsum(jax.nn.softmax(lb_logits.astype(jnp.float32), axis=1), axis=1)
    silu_c = jax.nn.silu(c)
    silu_cc = jax.nn.silu(c_ctx)
    x_lat, x_ctx = x, ctx
    for l in range(DEPTH_2):
        need_ctx = l < DEPTH_2 - 1
        mod_lat = (silu_c @ w_ada[l] + b_ada[l])[:, None, :]
        mod_ctx = silu_cc @ w_ada[l] + b_ada[l]
        sh1, sc1, gt1, sh2, sc2, gt2 = jnp.split(mod_lat, 6, axis=-1)
        csh1, csc1, cgt1, csh2, csc2, cgt2 = jnp.split(mod_ctx, 6, axis=-1)

        h_lat = rms_norm(x_lat, g_pre_mix[l]) * (1.0 + sc1) + sh1
        h_ctx = rms_norm(x_ctx, g_pre_mix[l]) * (1.0 + csc1) + csh1
        y_lat, y_ctx = token_mixer(h_lat, h_ctx, w_in[l], lower_bounds[:, l], g_hgrn_out[l], cm_ln_g[l],
                                   cm_ln_b[l], w_spatial[l], b_spatial[l], w_branch_a[l], w_branch_b[l],
                                   w_out[l], n_lat_chunks, n_ctx_chunks, need_ctx)
        x_lat = x_lat + gt1 * rms_norm(y_lat, g_post_mix[l])
        if need_ctx:
            x_ctx = x_ctx + cgt1 * rms_norm(y_ctx, g_post_mix[l])

        h2_lat = (rms_norm(x_lat, g_pre_ffn[l]) * (1.0 + sc2) + sh2).reshape(B * T, D)
        if need_ctx:
            h2_ctx = (rms_norm(x_ctx, g_pre_ffn[l]) * (1.0 + csc2) + csh2).reshape(B * L, D)
            f_all = moe_ffn(jnp.concatenate([h2_lat, h2_ctx], axis=0), w_router[l], b_router[l],
                            w_expert_gu[l], w_expert_down[l], w_shared_gu[l], w_shared_down[l])
            f_lat, f_ctx = f_all[:B * T], f_all[B * T:]
            x_ctx = x_ctx + cgt2 * rms_norm(f_ctx.reshape(B, L, D), g_post_ffn[l])
        else:
            f_lat = moe_ffn(h2_lat, w_router[l], b_router[l], w_expert_gu[l], w_expert_down[l],
                            w_shared_gu[l], w_shared_down[l])
        x_lat = x_lat + gt2 * rms_norm(f_lat.reshape(B, T, D), g_post_ffn[l])
    return x_lat


def setup_inputs(seed=0):
    out = dict(first_inputs(seed))
    for name, value in second_inputs(seed + 1).items():
        if name != "x":
            out[name + "_2"] = value
    return out


def reference(
    x, norm_mixer, norm_ffn, pool_w, pool_scale, kv_norm, w_kv, w_q, w_o, rel_bias, w_gate_up,
    w_down, final_norm, c_2, ctx_2, c_ctx_2, w_ada_2, b_ada_2, g_pre_mix_2, g_post_mix_2,
    g_pre_ffn_2, g_post_ffn_2, w_in_2, lb_logits_2, g_hgrn_out_2, cm_ln_g_2, cm_ln_b_2,
    w_spatial_2, b_spatial_2, w_branch_a_2, w_branch_b_2, w_out_2, w_router_2, b_router_2,
    w_expert_gu_2, w_expert_down_2, w_shared_gu_2, w_shared_down_2,
):
    x = first_block(
        x, norm_mixer, norm_ffn, pool_w, pool_scale, kv_norm, w_kv, w_q, w_o, rel_bias,
        w_gate_up, w_down, final_norm,
    )
    return second_block(
        x, c_2, ctx_2, c_ctx_2, w_ada_2, b_ada_2, g_pre_mix_2, g_post_mix_2, g_pre_ffn_2,
        g_post_ffn_2, w_in_2, lb_logits_2, g_hgrn_out_2, cm_ln_g_2, cm_ln_b_2, w_spatial_2,
        b_spatial_2, w_branch_a_2, w_branch_b_2, w_out_2, w_router_2, b_router_2, w_expert_gu_2,
        w_expert_down_2, w_shared_gu_2, w_shared_down_2,
    )


_drawn_inputs = setup_inputs


def setup_inputs(seed=0):
    import zlib

    import numpy as np

    out = dict(_drawn_inputs(seed))
    spreads = {}
    factors = {'ctx_2': 4.952,
     'c_ctx_2': 5.013,
     'g_post_ffn_2': 4.032,
     'lb_logits_2': 6.733,
     'g_hgrn_out_2': 2.775,
     'cm_ln_b_2': 5.651}
    for name, (base, spread) in spreads.items():
        noise = np.random.default_rng([zlib.crc32(name.encode()), seed]).standard_normal(out[name].shape)
        drawn = base * np.exp(spread * noise) if base else spread * noise
        out[name] = jnp.asarray(drawn.astype(out[name].dtype))
    for name, factor in factors.items():
        out[name] = (out[name] * factor).astype(out[name].dtype)
    return out
```

```python
import math
from contextlib import ExitStack, contextmanager

import numpy as np

import concourse.bass as bass
from concourse import mybir

P = 128
T = 256
NT = T // P
D = 1024
KD = D // P
D_FF = 2816
HID = 256
FFN_UNITS = D_FF // HID
EXPERTS = 64
MOE_UNITS = EXPERTS + 1
GROUPS = 8
HEADS = 16
DH = 64
BUCKETS = 32
MAX_DISTANCE = 128
WINDOWS = (2, 4, 8, 16)
GLA_HEADS = 4
CHUNK = 16
CM = 512
ADA_CHUNKS = 12
EPS = 1e-6
BIG = 1e30
ROUTED_SCALE = 2.5

PIECE = 1024
RAW = 12
RING = 4

FEAT = {}
_at = 0
for _name, _n in (("norm_mixer0", 8), ("norm_mixer1", 8), ("norm_ffn0", 8), ("norm_ffn1", 8), ("kv_norm", 8),
                  ("g_pre_mix", 8), ("g_pre_ffn", 8), ("g_hgrn", 1), ("b_ada", 48), ("b_spatial", 4), ("c", 16)):
    FEAT[_name] = (_at, _at + _n)
    _at += _n
NFEAT = _at
ROWS = {}
_at = 0
for _name, _n in (("pool_scale", 1024), ("final_norm", 1024), ("gt1_b", 1024), ("gt2_b", 1024), ("g_post_mix", 1024),
                  ("g_post_ffn", 1024), ("ln_g", 512), ("ln_b", 512), ("lb", 2048), ("b_router", 64)):
    ROWS[_name] = (_at, _at + _n)
    _at += _n
NROWS = _at
CONST = {}
_at = 0
for _name, _n in (("ident", 128), ("flip", 128), ("prefix", 128), ("after", 128), ("before", 128), ("ones", 128),
                  ("levels", 512), ("sel_sum", 2), ("sel_lat", 128)):
    CONST[_name] = (_at, _at + _n)
    _at += _n
NCONST = _at


def constants():
    u, t = np.arange(P)[:, None], np.arange(P)[None, :]
    c = np.zeros((P, NCONST), np.float32)

    def put(name, value):
        a, b = CONST[name]
        c[:value.shape[0], a:b] = value

    put("ident", (u == t).astype(np.float32))
    put("flip", (u == P - 1 - t).astype(np.float32))
    put("prefix", (u <= t).astype(np.float32))
    put("after", (u > t).astype(np.float32))
    put("before", (u < t).astype(np.float32))
    put("ones", np.ones((P, P), np.float32))
    mid = t // CHUNK * CHUNK + CHUNK // 2 - 1
    inner = ((u > mid) & (u <= t)).astype(np.float32) - ((u > t) & (u <= mid)).astype(np.float32)
    levels = [inner]
    for half in (CHUNK, 2 * CHUNK, 4 * CHUNK):
        m = t // (2 * half) * 2 * half + half
        levels.append(np.where(t < m, (u > t) & (u < m), (u >= m) & (u <= t)).astype(np.float32))
    put("levels", np.concatenate(levels, axis=1))
    r = np.arange(4)[:, None]
    put("sel_sum", (r % 2 == np.arange(2)[None, :]).astype(np.float32))
    put("sel_lat", np.repeat((r % 2 == 0).astype(np.float32), P, axis=1))
    s, q = np.arange(T)[:, None], np.arange(T)[None, :]
    pools = []
    for w in WINDOWS:
        cnt = np.minimum(q + 1, w)
        pools.append(((s <= q) & (s > q - w)) / cnt.astype(np.float32) - (s == q))
    pool = np.stack(pools, 1).astype(np.float32)
    pool = np.concatenate([pool[:P].reshape(P, 4 * T), pool[P:, :, P:].reshape(P, 4 * P)], axis=1)
    causal = np.repeat((u <= t).astype(np.int32)[:, None, :], GLA_HEADS, axis=1).reshape(P, GLA_HEADS * P)
    n = 255 - np.arange(384)
    exact = BUCKETS // 2
    far = np.maximum(n, exact).astype(np.float32)
    large = exact + (np.log(far / exact) / math.log(MAX_DISTANCE / exact) * (BUCKETS - exact)).astype(np.int32)
    bucket = np.where(n < exact, n, np.minimum(large, BUCKETS - 1))
    buckets = ((np.arange(BUCKETS)[:, None] == bucket[None, :]) & (n >= 0)[None, :]).astype(np.float32)
    return c, pool, causal, buckets


class Pos:

    def __init__(self):
        self.n, self.i, self.per = {}, None, {}

    def __call__(self, name, extra=0):
        v = self.n.get(name, 0) + extra
        return v if self.i is None else v + self.i * self.per.get(name, 0)

    def add(self, name, k=1):
        self.n[name] = self.n.get(name, 0) + k

    @contextmanager
    def loop(self, eng, times, per):
        start = dict(self.n)
        with eng.Fori(0, times) as i:
            self.i, self.per = i, per
            yield i
            self.i = None
        for name, v in self.n.items():
            d = v - start.get(name, 0)
            assert d == per.get(name, 0), (name, d)
            self.n[name] = v + d * (times - 1)


def program(nc, stream, x, ctx, feat, rows, consts, pool_c, causal_c, buckets_c, rel_bias, w_router, w_spatial, out):
    f32, f32r, i32 = mybir.dt.float32, mybir.dt.float32r, mybir.dt.int32
    ALU, ACT = mybir.AluOpType, mybir.ActivationFunctionType
    AXX = mybir.AxisListType.X
    es = ExitStack()
    with es:
        size = 207 * 1024
        es.enter_context(nc.sbuf_tensor("slab", [P, size // 4], f32))
        slab_at = nc.sbuf_base - size

        def place(start, *wanted):
            made = []
            for name, shape, *dt in wanted:
                n = 4 * int(np.prod(shape[1:]))
                assert start + n <= size, (name, start, n)
                made.append(nc.alloc_sbuf_tensor_at(name, shape, dt[0] if dt else f32, offset=slab_at + start))
                start += (n + 31) // 32 * 32
            return (*made, start)

        (raw, w_hi, w_lo, x_tok, x_hi, x_lo, xn, cst, causal, ft, eps, zero, ss, rms, rstd, mod, gains, phase) = place(
            0, ("raw", [P, RAW, PIECE]), ("w_hi", [P, RING, PIECE], f32r), ("w_lo", [P, RING, PIECE], f32r),
            ("x_tok", [P, NT, D]), ("x_hi", [P, KD, T], f32r), ("x_lo", [P, KD, T], f32r), ("xn", [P, NT, D]),
            ("cst", [P, NCONST]), ("causal", [P, GLA_HEADS, P], i32), ("ft", [P, NFEAT]), ("eps", [P, 1]),
            ("zero", [P, P], f32r), ("ss", [P, 2]), ("rms", [P, 2]), ("rstd", [P, 2]), ("mod", [P, 48, 2]),
            ("gains", [P, 3, KD]))
        a_hi, a_lo, a_tok, sg, unit_end = place(
            phase, ("a_hi", [P, NT, HID], f32r), ("a_lo", [P, NT, HID], f32r), ("a_tok", [P, NT, HID]),
            ("sg", [P, NT, HID]))
        pool_m, pool_s, oneh, rb, rv, _ = place(
            unit_end, ("pool_m", [P, 4 * T + 4 * P]), ("pool_s", [P, D]), ("oneh", [BUCKETS, 384]),
            ("rb", [BUCKETS, HEADS]), ("rv", [HEADS, 384]))
        q_even, q_odd, kT, v_tok, h2_hi, h2_lo, pt0, pt1, pr_odd, mx, rs, rr, _ = place(
            phase, ("q_even", [P, KD, T]), ("q_odd", [P, KD, T]), ("kT", [P, KD, T]), ("v_tok", [P, NT, D]), ("h2_hi", [P, KD, T], f32r),
            ("h2_lo", [P, KD, T], f32r), ("pt0", [P, 4, T]), ("pt1", [P, 4, P]), ("pr_odd", [P, 12 * P]),
            ("mx", [P, 2, 8]), ("rs", [P, 2, 8]), ("rr", [P, 8]))
        bias, _ = place(size - 4 * HEADS * T, ("bias", [P, HEADS, T]))
        fin_g, _ = place(unit_end, ("fin_g", [P, D]))
        tail = (size - 4 * (2 * 512 + 2 * D + NT * MOE_UNITS) - 64) // 32 * 32
        s0, gt1, gt2, comb, _ = place(
            tail, ("s0", [P, 2, 512]), ("gt1", [P, D]), ("gt2", [P, D]), ("comb", [P, NT, MOE_UNITS]))
        ctx_tok, _ = place(tail - 4 * NT * D, ("ctx_tok", [P, NT, D]))
        lb, oml, lbend = place(phase, ("lb", [P, 2, 512]), ("oml", [P, 2, 512]))
        ada_out, ad, csil, lbr, gate_rows, end = place(
            lbend, ("ada_out", [4, 6 * D]), ("ad", [P, KD, P], f32r), ("csil", [P, KD, 2]),
            ("lbr", [P, 2, 2, 512]), ("gate_rows", [P, 4, D]))
        assert end <= tail - 4 * NT * D
        zk, zf, zv, zq, ex, ki, qp, ats, kh, s1, dt, o_dir, end = place(
            lbend, ("zk", [P, 2, NT, 512]), ("zf", [P, 2, NT, 512]), ("zv", [P, 2, NT, 512]),
            ("zq", [P, 2, NT, 512]), ("ex", [P, 4, GLA_HEADS, P]), ("ki", [P, GLA_HEADS, P]),
            ("qp", [P, GLA_HEADS, P]), ("ats", [P, GLA_HEADS, P]), ("kh", [P, 512]), ("s1", [P, GLA_HEADS, P]),
            ("dt", [P, GLA_HEADS, 1]), ("o_dir", [P, 2, NT, 512]))
        assert end <= tail
        sgl, u_tok, vl, ga, gb, g_hi, g_lo, ln_g, ln_b, wst, sq, st8, st8b, mean, end = place(
            phase, ("sgl", [P, NT, 512]), ("u_tok", [P, NT, CM]), ("vl", [P, NT, CM]), ("ga", [P, NT, D]),
            ("gb", [P, NT, D]), ("g_hi", [P, KD, T], f32r), ("g_lo", [P, KD, T], f32r), ("ln_g", [P, CM]),
            ("ln_b", [P, CM]), ("wst", [P, GLA_HEADS, P]), ("sq", [P, NT, CM]), ("st8", [P, 8]), ("st8b", [P, 8]),
            ("mean", [P, 2]))
        assert end <= lbend + 4 * (8 * 1024 + 9 * 512)
        (wr, wr_hi, wr_lo, br, sc, sel, best, gsc, gm8, gkeep, gkeep2, t64, wsum, _) = place(
            unit_end, ("wr", [P, KD, EXPERTS]), ("wr_hi", [P, KD, EXPERTS], f32r), ("wr_lo", [P, KD, EXPERTS], f32r),
            ("br", [P, EXPERTS]), ("sc", [P, NT, EXPERTS]), ("sel", [P, NT, EXPERTS]), ("best", [P, NT, 8, 8]),
            ("gsc", [P, NT, 8]), ("gm8", [P, NT, 8]), ("gkeep", [P, NT, 8]), ("gkeep2", [P, NT, 8]),
            ("t64", [P, NT, EXPERTS]), ("wsum", [P, NT]))
        ps = es.enter_context(nc.psum_tensor("ps", [P, 8, 512], f32))
        scratch = nc.dram_tensor("bias_scratch", (HEADS, P, 384), f32, kind="Internal").ap()

        def const(name, rows_=P):
            a, b = CONST[name]
            return cst[0:rows_, a:b]

        def vec(name):
            a, b = FEAT[name]
            return ft[:, a:b]

        ident = const("ident")

        def probs(b):
            if b % 2:
                return (pr_odd[:, 0:512].rearrange("p (h k) -> p h k", h=4),
                        pr_odd[:, 512:1536].rearrange("p (h k) -> p h k", h=4))
            return (xn[:, 0, 0:512].rearrange("p (h k) -> p h k", h=4),
                    xn[:, 1, :].rearrange("p (h k) -> p h k", h=4))

        names = set()

        def sem(name):
            assert name not in names
            names.add(name)
            return es.enter_context(nc.semaphore(name))

        loaded = [sem(f"loaded{i}") for i in range(RAW // 2)]
        hi_ready, lo_ready, piece_used = sem("hi_ready"), sem("lo_ready"), sem("piece_used")
        g_free = sem("g_free")
        x_ready, rms_ready, xn_ready = sem("x_ready"), sem("rms_ready"), sem("xn_ready")
        t_done, h_hi, h_lo = sem("t_done"), sem("h_hi"), sem("h_lo")
        silu_ready, act_ready, act_t, act_hi = sem("silu_ready"), sem("act_ready"), sem("act_t"), sem("act_hi")
        dve_step, act_step = sem("dve_step"), sem("act_step")
        in_first, in_fin, in_gate, in_ctx, in_merge, in_router = (
            sem("in_first"), sem("in_fin"), sem("in_gate"), sem("in_ctx"), sem("in_merge"), sem("in_router"))
        bias_mm, bias_rows, bias_out, bias_in = sem("bias_mm"), sem("bias_rows"), sem("bias_out"), sem("bias_in")
        q_zero = sem("q_zero")
        s_done, p_raw, p_exp, p_ready, pt_done, pt0_ready, pt1_ready, pv_done, o_hi, o_lo = (
            sem("s_done"), sem("p_raw"), sem("p_exp"), sem("p_ready"), sem("pt_done"), sem("pt0_ready"),
            sem("pt1_ready"), sem("pv_done"), sem("o_hi"), sem("o_lo"))
        lb_max, lb_exp = sem("lb_max"), sem("lb_exp")
        c_silu, ad_ready, ada_free, mod_mm, gate_mm, mod_ready = (
            sem("c_silu"), sem("ad_ready"), [sem(f"ada_free{i}") for i in range(3)], sem("mod_mm"), sem("gate_mm"),
            sem("mod_ready"))
        sig_ready, f_ready, log_ready, k_ready = (
            sem("sig_ready"), sem("f_ready"), sem("log_ready"), sem("k_ready"))
        flip_mm, flip_ready = sem("flip_mm"), sem("flip_ready")
        cx_r, cx_exp, cx_k, cx_s, cx_ready = sem("cx_r"), sem("cx_exp"), sem("cx_k"), sem("cx_s"), sem("cx_ready")
        (sc_e, sc_t, sc_x, sc_m, sc_at, sc_ats, sc_r, sc_kh, sc_kk, sc_u, sc_o, sc_end, sc_flip, sc_sum) = (
            sem(n) for n in ("sc_e", "sc_t", "sc_x", "sc_m", "sc_at", "sc_ats", "sc_r", "sc_kh", "sc_kk", "sc_u",
                             "sc_o", "sc_end", "sc_flip", "sc_sum"))
        silu_g, gelu_r, gate_r = sem("silu_g"), sem("gelu_r"), sem("gate_r")
        (m_ms, m_rms, m_a, m_at, m_ahi, m_alo, m_v, m_z, m_b, m_bt, m_bhi, m_blo) = (
            sem(n) for n in ("m_ms", "m_rms", "m_a", "m_at", "m_ahi", "m_alo", "m_v", "m_z", "m_b", "m_bt", "m_bhi",
                             "m_blo"))
        zero_ready, ats_zero = sem("zero_ready"), sem("ats_zero")
        r_w, r_mm, r_sig = sem("r_w"), sem("r_mm"), sem("r_sig")
        res_ready, stored = sem("res_ready"), sem("stored")

        XR_POOL, XR_FFN0, XR_WO, XR_FFN1, XR_FIN, XR_MIX = 2, 4, 6, 8, 10, 12
        LOADS = stream.shape[0]
        N_PIECES = 2 * LOADS
        Z0 = 2 * FFN_UNITS + 6

        UNITS_PER = {"piece": 12, "pe": 12, "fill": 2, "act": 4, "t": 2}

        def kc(d, t):
            return ex[:, 2 * d + t, :, :].rearrange("p h n -> p (h n)")

        block = es.enter_context(nc.Block())

        @block.sync
        def _(sp):
            def load(l, slot, free_at):
                if free_at is not None:
                    sp.wait_ge(lo_ready, free_at)
                sp.dma_start(raw[:, 2 * slot:2 * slot + 2, :].rearrange("p a b -> p (a b)"),
                             stream[l]).then_inc(loaded[slot], 16)

            half = RAW // 2
            for l in range(2 * half):
                load(l, l % half, None if l < half else 2 * (l - half) + 2)
            whole = (LOADS - 2 * half) // half
            with sp.Fori(0, whole) as i:
                for j in range(half):
                    load(i * half + (2 * half + j), j, i * RAW + (RAW + 2 * j + 2))
            for l in range((2 + whole) * half, LOADS):
                load(l, l % half, 2 * (l - half) + 2)
            sp.wait_ge(res_ready, 2)
            sp.dma_start(out.rearrange("(t p) d -> p t d", p=P), x_tok[:, :, :]).then_inc(stored, 16)
            sp.wait_ge(stored, 16)

        @block.gpsimd
        def _(pool):
            def row(dst, name):
                a, b = ROWS[name]
                return pool.dma_start(dst, rows[0:1, a:b].partition_broadcast(P))

            nc.gpsimd.memset(eps[:, :], EPS).then_inc(zero_ready, 1)
            nc.gpsimd.memset(zero[:, :].bitcast(f32), 0.0).then_inc(zero_ready, 1)
            pool.dma_start(x_tok[:, :, :], x.rearrange("(t p) d -> p t d", p=P)).then_inc(in_first, 16)
            pool.dma_start(cst[:, :], consts).then_inc(in_first, 16)
            pool.dma_start(ft[:, :], feat).then_inc(in_first, 16)
            pool.dma_start(pool_m[:, :], pool_c).then_inc(in_first, 16)
            row(pool_s[:, :], "pool_scale").then_inc(in_first, 16)
            pool.dma_start(oneh[:, :], buckets_c).then_inc(in_first, 16)
            pool.dma_start(rb[:, :], rel_bias).then_inc(in_first, 16)
            pool.dma_start(causal[:, :, :].rearrange("p h k -> p (h k)"), causal_c).then_inc(in_first, 16)
            pool.wait_ge(bias_rows, 1)
            pool.dma_start(scratch, rv[:, :].unsqueeze(1).to_broadcast([HEADS, P, 384])).then_inc(bias_out, 16)
            pool.wait_ge(bias_out, 16)
            shifted = bass.AP(tensor=scratch.tensor, offset=scratch.offset + P - 1,
                              ap=[[384 - 1, P], [P * 384, HEADS], [1, T]])
            pool.dma_start(bias[:, :, :], shifted).then_inc(bias_in, 16)
            pool.wait_ge(x_ready, XR_FFN0)
            nc.gpsimd.memset(q_even[DH:, :, :], 0.0).then_inc(q_zero, 1)
            nc.gpsimd.memset(q_odd[0:DH, :, :], 0.0).then_inc(q_zero, 1)
            pool.wait_ge(x_ready, XR_WO)
            row(fin_g[:, :], "final_norm").then_inc(in_fin, 16)
            pool.wait_ge(x_ready, XR_FIN)
            for k, name in enumerate(("gt1_b", "gt2_b", "g_post_mix", "g_post_ffn")):
                row(gate_rows[:, k, :], name).then_inc(in_gate, 16)
            row(lbr[:, :, :, :].rearrange("p a b c -> p (a b c)"), "lb").then_inc(in_gate, 16)
            pool.dma_start(ctx_tok[:, :, :], ctx.rearrange("(t p) d -> p t d", p=P)).then_inc(in_ctx, 16)
            nc.gpsimd.memset(ad[:, :, :].bitcast(f32), 0.0).then_inc(zero_ready, 1)
            pool.wait_ge(cx_ready, 2)
            nc.gpsimd.memset(ats[:, :, :], 0.0).then_inc(ats_zero, 1)
            pool.wait_ge(sc_sum, 2)
            row(ln_g[:, :], "ln_g").then_inc(in_merge, 16)
            row(ln_b[:, :], "ln_b").then_inc(in_merge, 16)
            pool.dma_start(wst[:, :, :].rearrange("p g q -> p (g q)"), w_spatial).then_inc(in_merge, 16)
            pool.wait_ge(x_ready, XR_MIX)
            pool.dma_start(wr[:, :, :].rearrange("p k e -> p (k e)"), w_router).then_inc(in_router, 16)
            row(br[:, :], "b_router").then_inc(in_router, 16)

        @block.tensor
        def _(pe):
            pos = Pos()

            def three(o, l_hi, l_lo, r_hi, r_lo, start, stop, shared=False):
                pe.matmul(o, l_hi, r_hi, start=start, stop=False, skip_group_check=shared)
                pe.matmul(o, l_lo, r_hi, start=False, stop=False, skip_group_check=shared)
                return pe.matmul(o, l_hi, r_lo, start=False, stop=stop, skip_group_check=shared)

            def piece():
                pe.wait_ge(lo_ready, pos("piece", 1))
                return pos.n.get("piece", 0) % RING

            def done(last):
                last.then_inc(piece_used, 1)
                pos.add("piece")

            def wait_h(k):
                pe.wait_ge(h_lo, pos("h", k + 1))

            def tok(k, t):
                return (slice(None), k, slice(t * P, (t + 1) * P))

            def free_fill():
                if pos.i is not None or pos.n.get("fill", 0) >= 2:
                    pe.wait_ge(g_free, pos("fill", -1))

            def chunk(hi, lo, kts=tuple(range(KD)), banks=None, waits=True):
                if banks is None:
                    free_fill()
                    b = pos.n.get("fill", 0) % 2
                    banks = (2 * b, 2 * b + 1)
                    pos.add("fill")
                for j in range(len(kts) // 2):
                    slot = piece()
                    for jj in range(2):
                        k = kts[2 * j + jj]
                        if waits:
                            wait_h(k)
                        for t in range(NT):
                            c = slice(jj * 512, (jj + 1) * 512)
                            last = three(ps[:, banks[t], :], hi[tok(k, t)], lo[tok(k, t)], w_hi[:, slot, c],
                                         w_lo[:, slot, c], k == kts[0], k == kts[-1])
                    done(last)

            def chunk_t(hi, lo):
                free_fill()
                b = pos.n["fill"] % 2
                pos.add("fill")
                for j in range(KD // 2):
                    slot = piece()
                    for jj in range(2):
                        k = 2 * j + jj
                        wait_h(k)
                        for m in range(4):
                            c = slice(jj * 512 + m * P, jj * 512 + (m + 1) * P)
                            o = ps[:, 2 * b + m // 2, (m % 2) * T:(m % 2 + 1) * T]
                            start = k == 0 and m % 2 == 0
                            pe.matmul(o, w_hi[:, slot, c], hi[:, k, :], start=start, stop=False, skip_group_check=True)
                            pe.matmul(o, w_lo[:, slot, c], hi[:, k, :], start=False, stop=False, skip_group_check=True)
                            last = pe.matmul(o, w_hi[:, slot, c], lo[:, k, :], start=False, stop=k == KD - 1,
                                             skip_group_check=True)
                    done(last)

            def norm_t():
                for j in range(4):
                    for kk in range(2):
                        for t in range(NT):
                            if j == 0 and kk == 0:
                                pe.wait_ge(xn_ready, pos("xn", t + 1))
                            k = 2 * j + kk
                            last = pe.transpose(ps[:, 4 + j, kk * T + t * P:kk * T + (t + 1) * P],
                                                xn[:, t, k * P:(k + 1) * P], ident)
                    last.then_inc(t_done, 1)
                pos.add("xn", 2)

            def gu(j):
                if j == 0:
                    free_fill()
                b = pos.n["fill"] % 2
                slot = piece()
                for jj in range(2):
                    k = 2 * j + jj
                    for t in range(NT):
                        c = slice(jj * 512, (jj + 1) * 512)
                        last = three(ps[:, 2 * b + t, :], x_hi[tok(k, t)], x_lo[tok(k, t)], w_hi[:, slot, c],
                                     w_lo[:, slot, c], k == 0, k == KD - 1)
                done(last)
                if j == 3:
                    pos.add("fill")

            def unit_t(b):
                pe.wait_ge(act_ready, pos("act", 2))
                pos.add("act", 2)
                for j in range(2):
                    for t in range(NT):
                        last = pe.transpose(ps[:, 2 * b, j * T + t * P:j * T + (t + 1) * P],
                                            a_tok[:, t, j * P:(j + 1) * P], ident)
                last.then_inc(act_t, 1)

            def down(fills, stop=False):
                for j in range(2):
                    slot = piece()
                    pe.wait_ge(g_free, pos("fill", -fills))
                    for t in range(NT):
                        for h in range(2):
                            c = slice(h * 512, (h + 1) * 512)
                            last = three(ps[:, 4 + 2 * t + h, :], a_hi[tok(j, t)], a_lo[tok(j, t)],
                                         w_hi[:, slot, c], w_lo[:, slot, c], False, stop and j == 1, True)
                    done(last)

            def unit_step():
                for j in range(3):
                    gu(j)
                unit_t((pos.n["fill"] - 1) % 2)
                gu(3)
                down(1)

            def units(loops, peeled):
                for k in range(KD):
                    wait_h(k)
                for j in range(4):
                    gu(j)
                for b in range(4):
                    pe.matmul(ps[:, 4 + b, :], zero[:, :], x_hi[:, 0:2, :].rearrange("p k t -> p (k t)"),
                              start=True, stop=False, skip_group_check=True)
                for _ in range(peeled):
                    unit_step()
                with pos.loop(pe, loops, UNITS_PER | {"h": 0, "xn": 0}):
                    for _ in range(2):
                        unit_step()
                unit_t((pos.n["fill"] - 1) % 2)
                down(0, True)

            pe.wait_ge(in_first, 128)
            pe.wait_ge(zero_ready, 2)
            pm0 = pool_m[:, 0:4 * T].rearrange("p (w t) -> p w t", w=4)
            pm1 = pool_m[:, 4 * T:].rearrange("p (w t) -> p w t", w=4)
            pe.matmul(ps[0:HEADS, 0, 0:384], rb[:, :], oneh[:, :], start=True, stop=True).then_inc(bias_mm, 1)
            pe.wait_ge(xn_ready, 2)
            for j in range(4):
                for kk in range(2):
                    k = 2 * j + kk
                    o = ps[:, 4 + j, kk * T:(kk + 1) * T]
                    pe.matmul(o, xn[:, 0, k * P:(k + 1) * P], pm0[:, j, :], start=True, stop=False)
                    last = pe.matmul(ps[:, 4 + j, kk * T + P:(kk + 1) * T], xn[:, 1, k * P:(k + 1) * P],
                                     pm1[:, j, :], start=False, stop=True)
                last.then_inc(t_done, 1)
            pos.add("xn", 2)
            pe.wait_ge(bias_rows, 1)
            for j in range(2):
                slot = piece()
                for g in range(2):
                    grp = 2 * j + g
                    for kk in range(2):
                        wait_h(2 * grp + kk)
                        for t in range(NT):
                            c = slice(g * 512 + kk * 256, g * 512 + (kk + 1) * 256)
                            last = three(ps[:, 2 * t + j, g * 256:(g + 1) * 256], x_hi[tok(2 * grp + kk, t)],
                                         x_lo[tok(2 * grp + kk, t)], w_hi[:, slot, c], w_lo[:, slot, c],
                                         kk == 0, kk == 1)
                done(last)
            pos.add("h", 8)
            pos.n["fill"] = 0
            norm_t()
            units(4, 2)
            pos.add("h", 8)
            norm_t()
            for _ in range(2):
                chunk_t(h2_hi, h2_lo)
            for _ in range(2):
                chunk(h2_hi, h2_lo)
            pos.add("h", 8)
            for _ in range(2):
                chunk_t(x_hi, x_lo)
            pos.add("h", 8)
            pe.wait_ge(g_free, pos("fill"))

            pe.wait_ge(q_zero, 2)

            def scores(b):
                if b >= 2:
                    pe.wait_ge(pt0_ready, b - 1)
                    pe.wait_ge(pt1_ready, b - 1)
                base = 3 * (b % 2)
                for i in range(4):
                    h = 4 * b + i
                    q = (q_even, q_odd)[h % 2]
                    pe.matmul(ps[:, base, i * P:(i + 1) * P], q[:, h // 2, 0:P], kT[:, h // 2, 0:P],
                              start=True, stop=True)
                    last = pe.matmul(ps[:, base + 1 + i // 2, (i % 2) * T:(i % 2 + 1) * T], q[:, h // 2, P:T],
                                     kT[:, h // 2, :], start=True, stop=True)
                last.then_inc(s_done, 1)

            def attend(b):
                base = 3 * (b % 2)
                p0, p1 = probs(b)
                pe.wait_ge(p_ready, b + 1)
                for i in range(4):
                    o = base + 1 + i // 2
                    c = (i % 2) * T
                    pe.transpose(ps[:, o, c:c + P], p0[:, i, :], ident)
                    pe.transpose(ps[:, o, c + P:c + T], p1[:, i, 0:P], ident)
                    last = pe.transpose(ps[:, base, i * P:(i + 1) * P], p1[:, i, P:T], ident)
                last.then_inc(pt_done, 1)
                pe.wait_ge(pt0_ready, b + 1)
                pe.wait_ge(pt1_ready, b + 1)
                if b >= 2:
                    pe.wait_ge(o_lo, b - 1)
                for i in range(4):
                    h = 4 * b + i
                    rows_ = slice(DH * (h % 2), DH * (h % 2) + DH)
                    c = (i // 2) * T
                    pe.matmul(ps[rows_, 6 + b % 2, c:c + T], v_tok[:, 0, h * DH:(h + 1) * DH], pt0[:, i, :],
                              start=True, stop=False)
                    last = pe.matmul(ps[rows_, 6 + b % 2, c + P:c + T], v_tok[:, 1, h * DH:(h + 1) * DH],
                                     pt1[:, i, :], start=False, stop=True)
                last.then_inc(pv_done, 1)

            scores(0)
            scores(1)
            attend(0)
            scores(2)
            attend(1)
            scores(3)
            attend(2)
            attend(3)
            pe.wait_ge(o_lo, 4)
            for c in range(2):
                chunk(x_hi, x_lo, banks=(4 + c, 6 + c), waits=False)
            norm_t()
            units(5, 0)
            pos.add("h", 8)
            pe.wait_ge(ad_ready, 1)
            pe.wait_ge(x_ready, XR_FFN1)

            def modulation(copied):
                for j in range(3):
                    if copied is not None:
                        pe.wait_ge(ada_free[j], copied)
                    for k in range(KD):
                        if k % 2 == 0:
                            slot = piece()
                        c = slice((k % 2) * 512, (k % 2 + 1) * 512)
                        pe.matmul(ps[:, 4 + j, :], ad[:, k, :], w_hi[:, slot, c], start=k == 0, stop=False)
                        last = pe.matmul(ps[:, 4 + j, :], ad[:, k, :], w_lo[:, slot, c], start=False, stop=k == KD - 1)
                        if k % 2:
                            done(last)

            modulation(None)
            with pos.loop(pe, ADA_CHUNKS // 3 - 1, {"piece": 12}) as i:
                modulation(i + 1)
            for j in range(3):
                pe.wait_ge(ada_free[j], ADA_CHUNKS // 3)
            for m in range(48):
                last = pe.matmul(ps[:, 7, 2 * m:2 * m + 2], ada_out[:, m * P:(m + 1) * P], const("sel_sum", 4),
                                 start=True, stop=True)
            last.then_inc(mod_mm, 1)
            for g, first in enumerate((2 * D, 5 * D)):
                for c in range(2):
                    last = pe.matmul(ps[:, 2 * g + c, :], const("sel_lat", 4),
                                     ada_out[:, first + c * 512:first + (c + 1) * 512], start=True, stop=True)
            last.then_inc(gate_mm, 1)
            pe.wait_ge(mod_ready, 1)
            norm_t()
            for _ in range(3):
                chunk(x_hi, x_lo)
            pos.add("h", 8)
            pe.wait_ge(g_free, pos("fill"))
            pe.wait_ge(log_ready, 2)
            for d, near in enumerate(("after", "before")):
                for t in range(NT):
                    o = ps[:, 2 * d + t, :]
                    outer = t == d
                    last = pe.matmul(o, const(near), zf[:, d, t, :], start=True, stop=not outer)
                    if outer:
                        last = pe.matmul(o, const("ones"), zf[:, d, 1 - t, :], start=False, stop=True)
                last.then_inc(cx_r, 1)
            for d in range(2):
                pe.wait_ge(cx_k, 2 * (d + 1))
                for h in range(GLA_HEADS):
                    c = slice(h * P, (h + 1) * P)
                    for t in range(NT):
                        last = pe.matmul(ps[:, 4 + d, c], kc(d, t)[:, c], zv[:, 0, t, c], start=t == 0, stop=t == 1)
                last.then_inc(cx_s, 1)
            pe.wait_ge(cx_ready, 2)
            norm_t()
            for _ in range(4):
                chunk(x_hi, x_lo)
            pe.wait_ge(g_free, pos("fill"))
            for r, (src, at) in enumerate(((xn, 1), (zv, 1), (zq, 2))):
                pe.wait_ge(g_free, Z0 + 7)
                if at == 2:
                    pe.wait_ge(silu_g, 1)
                for t in range(NT):
                    s_ = xn[:, t, 0:512] if r == 0 else src[:, 0, t, :]
                    last = pe.matmul(ps[:, 2 * r + 1 - t, :], const("flip"), s_, start=True, stop=True)
                last.then_inc(flip_mm, 1)
            pe.wait_ge(flip_ready, 3)
            for g in range(4):
                d, a = g // 2, g % 2
                if g:
                    pe.wait_ge(sc_end, g)
                pe.wait_ge(log_ready, 3 + d)
                pe.wait_ge(k_ready, 3 + d)
                for h in range(GLA_HEADS):
                    pe.matmul(ps[:, 2 + h, :], zf[:, d, a, h * P:(h + 1) * P], const("levels"), start=True,
                              stop=True).then_inc(sc_e, 1)
                for h in range(GLA_HEADS):
                    last = pe.matmul(ps[:, 6, h * P:(h + 1) * P], zf[:, d, a, h * P:(h + 1) * P], const("prefix"),
                                     start=True, stop=True)
                last.then_inc(sc_e, 1)
                for h in range(GLA_HEADS):
                    c = slice(h * P, (h + 1) * P)
                    pe.transpose(ps[:, 0, c], zq[:, d, a, c], ident)
                    last = pe.transpose(ps[:, 1, c], zk[:, d, a, c], ident)
                last.then_inc(sc_t, 1)
                if a == 0:
                    pe.wait_ge(sc_x, 9 * (g + 1))
                    pe.matmul(ps[:, 2, :], const("after"), zf[:, d, 0, :], start=True, stop=True).then_inc(sc_r, 1)
                pe.wait_ge(sc_m, 9 * (g + 1))
                for h in range(GLA_HEADS):
                    c0 = h * P
                    last = pe.matmul(ps[:, 7, c0:c0 + P], ki[:, h, :], ex[:, 0, h, :], start=True, stop=True,
                                     skip_group_check=True)
                    for lev, half in enumerate((CHUNK, 2 * CHUNK, 4 * CHUNK), 1):
                        for s in range(0, P, 2 * half):
                            last = pe.matmul(ps[s:s + half, 7, c0 + s + half:c0 + s + 2 * half],
                                             ex[:, lev, h, s:s + half], ex[:, lev, h, s + half:s + 2 * half],
                                             start=True, stop=True, skip_group_check=True)
                last.then_inc(sc_at, 1)
                if a == 0:
                    pe.wait_ge(sc_kk, d + 1)
                    for h in range(GLA_HEADS):
                        c = slice(h * P, (h + 1) * P)
                        last = pe.matmul(ps[:, 3, c], kh[:, c], zv[:, d, 0, c], start=True, stop=True)
                    last.then_inc(sc_u, 1)
                pe.wait_ge(sc_ats, g + 1)
                for h in range(GLA_HEADS):
                    c = slice(h * P, (h + 1) * P)
                    pe.matmul(ps[:, 4, c], ats[:, h, :], zv[:, d, a, c], start=True, stop=False)
                    state = s0[:, d, c] if a == 0 else s1[:, h, :]
                    last = pe.matmul(ps[:, 4, c], qp[:, h, :], state, start=False, stop=True)
                last.then_inc(sc_o, 1)
            pe.wait_ge(sc_end, 4)
            for t in range(NT):
                last = pe.matmul(ps[:, 5 + 1 - t, :], const("flip"), o_dir[:, 1, t, :], start=True, stop=True)
            last.then_inc(sc_flip, 1)
            pe.wait_ge(sc_sum, 2)
            for _ in range(7):
                chunk(x_hi, x_lo)
            pos.add("h", 8)
            pe.wait_ge(g_free, pos("fill"))
            pe.wait_ge(m_a, 1)
            for t in range(NT):
                for h in range(GLA_HEADS):
                    last = pe.transpose(ps[:, h // 2, (h % 2) * T + t * P:(h % 2) * T + (t + 1) * P],
                                        o_dir[:, 0, t, h * P:(h + 1) * P], ident)
            last.then_inc(m_at, 1)
            pe.wait_ge(in_merge, 48)
            pe.wait_ge(m_v, 1)
            for t in range(NT):
                for g in range(GLA_HEADS):
                    c = slice(g * P, (g + 1) * P)
                    last = pe.matmul(ps[:, 2 + t, c], wst[:, g, :], vl[:, t, c], start=True, stop=True)
            last.then_inc(m_z, 1)
            pe.wait_ge(m_b, 1)
            for t in range(NT):
                for h in range(GLA_HEADS):
                    last = pe.transpose(ps[:, 4 + h // 2, (h % 2) * T + t * P:(h % 2) * T + (t + 1) * P],
                                        u_tok[:, t, h * P:(h + 1) * P], ident)
            last.then_inc(m_bt, 1)
            pe.wait_ge(m_alo, 1)
            pe.wait_ge(m_blo, 1)
            for c in range(2):
                chunk(g_hi, g_lo, (0, 1, 2, 3), (4 + c, 6 + c), waits=False)
            for c in range(2):
                chunk(g_hi, g_lo, (4, 5, 6, 7), (c, 2 + c), waits=False)
            norm_t()
            for k in range(KD):
                wait_h(k)
            for c in range(2):
                chunk(x_hi, x_lo, banks=(4 + c, 6 + c), waits=False)
            pos.add("h", 8)
            norm_t()
            pe.wait_ge(r_w, 2)
            for k in range(KD):
                wait_h(k)
            for t in range(NT):
                for k in range(KD):
                    last = three(ps[:, t, 0:EXPERTS], x_hi[tok(k, t)], x_lo[tok(k, t)], wr_hi[:, k, :],
                                 wr_lo[:, k, :], k == 0, k == KD - 1)
            last.then_inc(r_mm, 1)
            pe.wait_ge(r_sig, 1)
            units(32, 0)

        @block.scalar
        def _(act):
            pos = Pos()

            def step(ins):
                ins.then_inc(act_step, 1)
                pos.add("step")
                act.wait_ge(act_step, pos("step"))

            def prep(k):
                for _ in range(k):
                    n = pos.n.get("piece", 0)
                    if n % 2 == 0:
                        at = n // 2 % (RAW // 2)
                        times = n // RAW
                        full = 16 * (times + 1)
                        if pos.i is not None:
                            full = full + pos.i * 16
                        act.wait_ge(loaded[at], full)
                    if pos.i is not None or n >= RING:
                        act.wait_ge(piece_used, pos("piece", 1 - RING))
                    nc.scalar.activation(w_hi[:, n % RING, :], raw[:, n % RAW, :], ACT.Copy).then_inc(hi_ready, 1)
                    pos.add("piece")

            def ahead():
                prep(min(pos.n.get("pe", 0) + RING, N_PIECES) - pos.n.get("piece", 0))

            def root(parts, version=None, div=D):
                for t in range(NT):
                    if version is not None:
                        act.wait_ge(x_ready, version - 1 + t)
                    step(nc.scalar.activation(xn[:, t, :], parts[t], ACT.Square, accum_out=ss[:, t:t + 1]))
                nc.scalar.activation(rms[:, :], ss[:, :], ACT.Sqrt, scale=1.0 / div, bias=eps[:, :]).then_inc(
                    rms_ready, 1)

            def norm_hi(targets):
                for n, (dst, gain, shift) in enumerate(targets):
                    for j in range(4):
                        if n == 0:
                            act.wait_ge(t_done, pos("t_done", j + 1))
                        else:
                            act.wait_ge(h_lo, pos("h", -8 + 2 * j + 2))
                        for k in (2 * j, 2 * j + 1):
                            src = ps[:, 4 + j, (k % 2) * T:(k % 2 + 1) * T]
                            if gain is None:
                                ins = nc.scalar.activation(dst[:, k, :], src, ACT.Copy)
                            elif shift is None:
                                ins = nc.scalar.activation(dst[:, k, :], src, ACT.Copy, scale=gain[:, k:k + 1])
                            else:
                                ins = nc.scalar.activation(dst[:, k, :], src, ACT.Identity, scale=gain[:, k:k + 1],
                                                           bias=shift[:, k:k + 1])
                            ins.then_inc(h_hi, 1)
                    pos.add("h", 8)
                pos.add("t_done", 4)

            def unit_silu(b):
                act.wait_ge(piece_used, pos("pe"))
                if pos.i is not None or pos.n.get("act", 0) > 0:
                    act.wait_ge(act_ready, pos("act"))
                for t in range(NT):
                    nc.scalar.activation(sg[:, t, :], ps[:, 2 * b + t, 0:HID], ACT.Silu).then_inc(silu_ready, 1)
                pos.add("act", 2)

            def unit_hi(b):
                act.wait_ge(act_t, pos("t", 1))
                pos.add("t")
                nc.scalar.activation(a_hi[:, :, :], ps[:, 2 * b, :].rearrange("p (j t) -> p j t", j=2),
                                     ACT.Copy).then_inc(act_hi, 1)

            def unit_step():
                b = pos.n.get("fill", 0) % 2
                prep(2)
                unit_silu(b)
                prep(3)
                unit_hi(b)
                prep(1)
                pos.add("fill")
                pos.add("pe", 6)

            def units(loops, peeled):
                pos.add("pe", 4)
                for _ in range(peeled):
                    unit_step()
                with pos.loop(act, loops, UNITS_PER):
                    for _ in range(2):
                        unit_step()
                b = pos.n["fill"] % 2
                unit_silu(b)
                prep(2)
                unit_hi(b)
                pos.add("fill")
                pos.add("pe", 2)

            def gates(d, z):
                act.wait_ge(g_free, Z0 + z)
                step(nc.scalar.activation(zk[:, d, :, :], zf[:, d, :, :], ACT.Sigmoid, scale=-1.0))
                nc.scalar.activation(zf[:, d, :, :], zf[:, d, :, :], ACT.Sigmoid).then_inc(sig_ready, 1)

            def log(d, n):
                act.wait_ge(f_ready, n)
                nc.scalar.activation(zf[:, d, :, :], zf[:, d, :, :], ACT.Ln).then_inc(log_ready, 1)

            act.wait_ge(in_first, 128)
            act.wait_ge(zero_ready, 2)
            root([x_tok[:, t, :] for t in range(NT)])
            ahead()
            norm_hi([(x_hi, vec("norm_mixer0"), None)])
            pos.add("pe", 2)
            ahead()
            root([x_tok[:, t, :] for t in range(NT)], XR_POOL)
            norm_hi([(x_hi, vec("norm_ffn0"), None)])
            units(4, 2)
            ahead()
            root([x_tok[:, t, :] for t in range(NT)], XR_FFN0)
            norm_hi([(h2_hi, vec("kv_norm"), None), (x_hi, vec("norm_mixer1"), None)])
            for _ in range(6):
                pos.add("pe", 4)
                ahead()

            def exps(b):
                p0, p1 = probs(b)
                act.wait_ge(p_raw, 2 * b + 2)
                for n, pr in enumerate((p0, p1)):
                    for i in range(4):
                        c = 4 * n + i
                        nc.scalar.activation(pr[:, i, :], pr[:, i, :], ACT.Exp, bias=mx[:, b % 2, c:c + 1],
                                             accum_out=rs[:, b % 2, c:c + 1]).then_inc(p_exp, 1)

            exps(0)
            for b in range(4):
                if b < 3:
                    exps(b + 1)
                act.wait_ge(pt_done, b + 1)
                if b:
                    act.wait_ge(pv_done, b)
                base = 3 * (b % 2)
                nc.scalar.activation(pt0[:, :, :], ps[:, base + 1:base + 3, :].rearrange("p a (h q) -> p (a h) q", h=2),
                                     ACT.Copy).then_inc(pt0_ready, 1)
                act.wait_ge(pv_done, b + 1)
                nc.scalar.activation(x_hi[:, 2 * b:2 * b + 2, :],
                                     ps[:, 6 + b % 2, :].rearrange("p (k t) -> p k t", k=2), ACT.Copy).then_inc(o_hi, 1)
            for _ in range(2):
                pos.add("pe", 4)
                ahead()
            root([x_tok[:, t, :] for t in range(NT)], XR_WO)
            norm_hi([(x_hi, vec("norm_ffn1"), None)])
            units(5, 0)
            ahead()
            root([x_tok[:, t, :] for t in range(NT)], XR_FFN1)
            act.wait_ge(x_ready, XR_FIN)
            nc.scalar.activation(csil[:, :, :].rearrange("p k c -> p (k c)"), vec("c"), ACT.Silu).then_inc(c_silu, 1)
            act.wait_ge(lb_max, 1)
            nc.scalar.activation(lbr[:, :, :, :].rearrange("p a b c -> p (a b c)"),
                                 lbr[:, :, :, :].rearrange("p a b c -> p (a b c)"), ACT.Exp).then_inc(lb_exp, 1)
            with pos.loop(act, ADA_CHUNKS // 3, {"piece": 12}):
                prep(12)
            pos.add("pe", 48)
            act.wait_ge(in_ctx, 16)
            root([ctx_tok[:, t, :] for t in range(NT)])
            act.wait_ge(mod_ready, 1)
            norm_hi([(x_hi, gains[:, 1, :], mod[:, :, 1])])
            for _ in range(3):
                pos.add("pe", 4)
                ahead()
            gates(0, 2)
            gates(1, 2)
            log(0, 1)
            log(1, 2)
            for d in range(2):
                act.wait_ge(cx_r, d + 1)
                for t in range(NT):
                    nc.scalar.activation(kc(d, t), ps[:, 2 * d + t, :], ACT.Exp).then_inc(cx_exp, 1)
            root([x_tok[:, t, :] for t in range(NT)], XR_FIN)
            norm_hi([(x_hi, gains[:, 0, :], mod[:, :, 0])])
            for _ in range(4):
                pos.add("pe", 4)
                ahead()
            gates(0, 7)
            nc.scalar.activation(zq[:, 0, :, :], zq[:, 0, :, :], ACT.Silu).then_inc(silu_g, 1)
            log(0, 3)
            act.wait_ge(flip_ready, 1)
            step(nc.scalar.activation(zk[:, 1, :, :], zf[:, 1, :, :], ACT.Sigmoid, scale=-1.0))
            nc.scalar.activation(zf[:, 1, :, :], zf[:, 1, :, :], ACT.Sigmoid).then_inc(sig_ready, 1)
            log(1, 4)
            for g in range(4):
                d, a = g // 2, g % 2
                if g:
                    act.wait_ge(sc_end, g)
                for h in range(GLA_HEADS):
                    act.wait_ge(sc_e, 5 * g + h + 1)
                    nc.scalar.activation(ex[:, :, h, :], ps[:, 2 + h, :].rearrange("p (l t) -> p l t", l=4),
                                         ACT.Exp).then_inc(sc_x, 1)
                    nc.scalar.activation(ki[:, h, :], ps[:, 2 + h, 0:P], ACT.Exp, scale=-1.0).then_inc(sc_x, 1)
                act.wait_ge(sc_e, 5 * g + 5)
                nc.scalar.activation(qp[:, :, :], ps[:, 6, :].rearrange("p (h t) -> p h t", h=4),
                                     ACT.Exp).then_inc(sc_x, 1)
                if a == 0:
                    act.wait_ge(sc_r, d + 1)
                    nc.scalar.activation(kh[:, :], ps[:, 2, :], ACT.Exp).then_inc(sc_kh, 1)
            act.wait_ge(sc_sum, 2)
            for c, (dst, fn, ready) in enumerate((
                    (sgl[:, :, :], ACT.Silu, silu_g), (u_tok[:, :, :], ACT.Gelu_apprx_tanh, gelu_r),
                    (vl[:, :, :], ACT.Gelu_apprx_tanh, gelu_r), (ga[:, :, 0:512], ACT.Sigmoid, gate_r),
                    (ga[:, :, 512:], ACT.Sigmoid, gate_r), (gb[:, :, 0:512], ACT.Sigmoid, gate_r),
                    (gb[:, :, 512:], ACT.Sigmoid, gate_r))):
                pos.add("pe", 4)
                ahead()
                act.wait_ge(g_free, Z0 + 8 + c)
                nc.scalar.activation(dst, dst, fn).then_inc(ready, 1)
            act.wait_ge(m_ms, 1)
            nc.scalar.activation(st8b[:, :], st8[:, :], ACT.Sqrt, scale=1.0 / P, bias=eps[:, :]).then_inc(m_rms, 1)
            act.wait_ge(m_at, 1)
            ga_, _ = FEAT["g_hgrn"]
            nc.scalar.activation(g_hi[:, 0:4, :], ps[:, 0:2, :].rearrange("p a (h t) -> p (a h) t", h=2), ACT.Copy,
                                 scale=ft[:, ga_:ga_ + 1]).then_inc(m_ahi, 1)
            act.wait_ge(m_ms, 2)
            nc.scalar.activation(rms[:, :], ss[:, :], ACT.Sqrt, scale=1.0 / CM, bias=eps[:, :]).then_inc(m_rms, 1)
            act.wait_ge(m_bt, 1)
            nc.scalar.activation(g_hi[:, 4:8, :], ps[:, 4:6, :].rearrange("p a (h t) -> p (a h) t", h=2),
                                 ACT.Copy).then_inc(m_bhi, 1)
            for _ in range(4):
                pos.add("pe", 2)
                ahead()
            norm_hi([(x_hi, None, None)])
            for _ in range(2):
                pos.add("pe", 4)
                ahead()
            act.wait_ge(piece_used, pos("pe"))
            root([ps[:, 4 + 2 * t:6 + 2 * t, :].rearrange("p a b -> p (a b)") for t in range(NT)])
            root([x_tok[:, t, :] for t in range(NT)], XR_MIX)
            norm_hi([(x_hi, gains[:, 2, :], mod[:, 24:, 0])])
            act.wait_ge(r_mm, 1)
            nc.scalar.activation(sc[:, :, :], ps[:, 0:2, 0:EXPERTS], ACT.Sigmoid).then_inc(r_sig, 1)
            units(32, 0)
            act.wait_ge(piece_used, pos("pe"))
            root([ps[:, 4 + 2 * t:6 + 2 * t, :].rearrange("p a b -> p (a b)") for t in range(NT)])

        @block.vector
        def _(dve):
            pos = Pos()

            def step(ins):
                ins.then_inc(dve_step, 1)
                pos.add("step")
                dve.wait_ge(dve_step, pos("step"))

            def prep(k):
                for _ in range(k):
                    n = pos.n.get("piece", 0)
                    dve.wait_ge(hi_ready, pos("piece", 1))
                    nc.vector.tensor_tensor(w_lo[:, n % RING, :], raw[:, n % RAW, :],
                                            w_hi[:, n % RING, :].bitcast(f32), ALU.subtract).then_inc(lo_ready, 1)
                    pos.add("piece")

            def ahead():
                prep(min(pos.n.get("pe", 0) + RING, N_PIECES) - pos.n.get("piece", 0))

            def inverse():
                dve.wait_ge(rms_ready, pos("rms", 1))
                pos.add("rms")
                step(nc.vector.reciprocal(rstd[:, :], rms[:, :]))

            def norm_x(src):
                inverse()
                for t in range(NT):
                    nc.vector.tensor_scalar(xn[:, t, :], src[:, t, :], rstd[:, t:t + 1], None,
                                            ALU.mult).then_inc(xn_ready, 1)

            def norm_lo(targets):
                for dst_hi, dst, gain, shift in targets:
                    for k in range(KD):
                        dve.wait_ge(h_hi, pos("h", 2 * (k // 2) + 2))
                        src = ps[:, 4 + k // 2, (k % 2) * T:(k % 2 + 1) * T]
                        high = dst_hi[:, k, :].bitcast(f32)
                        if gain is None:
                            ins = nc.vector.tensor_tensor(dst[:, k, :], src, high, ALU.subtract)
                        elif shift is None:
                            ins = nc.vector.scalar_tensor_tensor(dst[:, k, :], src, gain[:, k:k + 1], high, ALU.mult,
                                                                 ALU.subtract)
                        else:
                            tmp = xn[:, 0, 0:T]
                            if k:
                                dve.wait_ge(h_lo, pos("h", k))
                            step(nc.vector.tensor_scalar(tmp, src, gain[:, k:k + 1], shift[:, k:k + 1], ALU.mult,
                                                         ALU.add))
                            ins = nc.vector.tensor_tensor(dst[:, k, :], tmp, high, ALU.subtract)
                        ins.then_inc(h_lo, 1)
                    pos.add("h", 8)

            def wide(t):
                return ps[:, 4 + 2 * t:6 + 2 * t, :].rearrange("p a b -> p (a b)")

            def add_residual():
                dve.wait_ge(piece_used, pos("pe"))
                for t in range(NT):
                    nc.vector.tensor_tensor(x_tok[:, t, :], x_tok[:, t, :], wide(t), ALU.add).then_inc(x_ready, 1)

            def unit_act(b, weight):
                for t in range(NT):
                    dve.wait_ge(silu_ready, pos("act", t + 1))
                    up = ps[:, 2 * b + t, HID:2 * HID]
                    if weight is None:
                        ins = nc.vector.tensor_tensor(a_tok[:, t, :], sg[:, t, :], up, ALU.mult)
                    else:
                        ins = nc.vector.scalar_tensor_tensor(a_tok[:, t, :], sg[:, t, :], comb[:, t, weight], up,
                                                             ALU.mult, ALU.mult)
                    ins.then_inc(act_ready, 1)
                pos.add("act", 2)

            def unit_lo(b):
                dve.wait_ge(act_hi, pos("t", 1))
                pos.add("t")
                nc.vector.tensor_tensor(a_lo[:, :, :], ps[:, 2 * b, :].rearrange("p (j t) -> p j t", j=2),
                                        a_hi[:, :, :].bitcast(f32), ALU.subtract).then_inc(g_free, 1)

            def unit_step(weight):
                b = pos.n.get("fill", 0) % 2
                prep(2)
                unit_act(b, weight)
                prep(3)
                unit_lo(b)
                prep(1)
                pos.add("fill")
                pos.add("pe", 6)

            def units(loops, peeled, routed=False):
                pos.add("pe", 4)
                for _ in range(peeled):
                    unit_step(None)
                with pos.loop(dve, loops, UNITS_PER) as i:
                    for e in range(2):
                        unit_step(bass.ds(i * 2 + e, 1) if routed else None)
                b = pos.n["fill"] % 2
                unit_act(b, slice(MOE_UNITS - 1, MOE_UNITS) if routed else None)
                prep(2)
                unit_lo(b)
                pos.add("fill")
                pos.add("pe", 2)

            def copy_queries(c):
                b = pos.n["fill"] % 2
                pos.add("fill")
                dve.wait_ge(piece_used, pos("pe"))
                k = slice(4 * c, 4 * c + 4)
                for r, dst in ((slice(0, DH), q_even), (slice(DH, P), q_odd)):
                    ins = nc.vector.tensor_copy(dst[r, k, :], ps[r, 2 * b:2 * b + 2, :].rearrange(
                        "p a (k t) -> p (a k) t", k=2))
                    if r.start:
                        ins.then_inc(g_free, 1)
                    else:
                        step(ins)

            def copy_fill(dst, transposed=False):
                b = pos.n["fill"] % 2
                pos.add("fill")
                dve.wait_ge(piece_used, pos("pe"))
                src = ps[:, 2 * b:2 * b + 2, :]
                if transposed:
                    src = src.rearrange("p a (k t) -> p (a k) t", k=2)
                nc.vector.tensor_copy(dst, src).then_inc(g_free, 1)

            dve.wait_ge(in_first, 128)
            norm_x(x_tok)
            dve.wait_ge(bias_mm, 1)
            step(nc.vector.tensor_copy(rv[:, :], ps[0:HEADS, 0, 0:384]))
            nc.vector.memset(rv[:, 256:384], -BIG).then_inc(bias_rows, 1)
            ahead()
            norm_lo([(x_hi, x_lo, vec("norm_mixer0"), None)])
            pos.add("pe", 2)
            ahead()
            dve.wait_ge(piece_used, pos("pe"))
            for t in range(NT):
                step(nc.vector.tensor_tensor(xn[:, t, :], ps[:, 2 * t:2 * t + 2, :].rearrange("p a b -> p (a b)"),
                                             pool_s[:, :], ALU.mult))
                nc.vector.tensor_tensor(x_tok[:, t, :], x_tok[:, t, :], xn[:, t, :], ALU.add).then_inc(x_ready, 1)
            norm_x(x_tok)
            norm_lo([(x_hi, x_lo, vec("norm_ffn0"), None)])
            units(4, 2)
            add_residual()
            ahead()
            norm_x(x_tok)
            norm_lo([(h2_hi, h2_lo, vec("kv_norm"), None), (x_hi, x_lo, vec("norm_mixer1"), None)])
            dve.wait_ge(bias_in, 16)
            for dst, transposed in ((kT[:, 0:4, :], True), (kT[:, 4:8, :], True), (v_tok[:, :, 0:512], False),
                                    (v_tok[:, :, 512:], False)):
                pos.add("pe", 4)
                ahead()
                copy_fill(dst, transposed=transposed)
            for c in range(2):
                pos.add("pe", 4)
                ahead()
                copy_queries(c)

            def raw_scores(b):
                p0, p1 = probs(b)
                base = 3 * (b % 2)
                dve.wait_ge(s_done, b + 1)
                if b >= 2:
                    dve.wait_ge(pt_done, b - 1)
                for n, (pr, src, rel) in enumerate((
                        (p0, ps[:, base, :].rearrange("p (h k) -> p h k", h=4), bias[:, 4 * b:4 * b + 4, P:T]),
                        (p1, ps[:, base + 1:base + 3, :].rearrange("p a (h k) -> p (a h) k", h=2),
                         bias[:, 4 * b:4 * b + 4, :]))):
                    step(nc.vector.scalar_tensor_tensor(pr, src, DH ** -0.5, rel, ALU.mult, ALU.add))
                    nc.vector.reduce_max(mx[:, b % 2, 4 * n:4 * n + 4], pr, AXX, negate=True).then_inc(p_raw, 1)

            raw_scores(0)
            for b in range(4):
                p0, p1 = probs(b)
                if b < 3:
                    raw_scores(b + 1)
                dve.wait_ge(p_exp, 8 * (b + 1))
                step(nc.vector.reciprocal(rr[:, :], rs[:, b % 2, :]))
                step(nc.vector.tensor_tensor(p0, p0, rr[:, 0:4].unsqueeze(2).to_broadcast([P, 4, P]), ALU.mult))
                nc.vector.tensor_tensor(p1, p1, rr[:, 4:8].unsqueeze(2).to_broadcast([P, 4, T]),
                                        ALU.mult).then_inc(p_ready, 1)
                dve.wait_ge(pt_done, b + 1)
                if b:
                    dve.wait_ge(pv_done, b)
                nc.vector.tensor_copy(pt1[:, :, :], ps[:, 3 * (b % 2), :].rearrange("p (h q) -> p h q", h=4)
                                      ).then_inc(pt1_ready, 1)
                dve.wait_ge(o_hi, b + 1)
                nc.vector.tensor_tensor(x_lo[:, 2 * b:2 * b + 2, :],
                                        ps[:, 6 + b % 2, :].rearrange("p (k t) -> p k t", k=2),
                                        x_hi[:, 2 * b:2 * b + 2, :].bitcast(f32), ALU.subtract).then_inc(o_lo, 1)
            for _ in range(2):
                pos.add("pe", 4)
                ahead()
            add_residual()
            norm_x(x_tok)
            norm_lo([(x_hi, x_lo, vec("norm_ffn1"), None)])
            units(5, 0)
            ahead()
            add_residual()
            inverse()
            dve.wait_ge(in_fin, 16)
            for t in range(NT):
                nc.vector.scalar_tensor_tensor(x_tok[:, t, :], x_tok[:, t, :], rstd[:, t:t + 1], fin_g[:, :],
                                               ALU.mult, ALU.mult).then_inc(x_ready, 1)
            dve.wait_ge(zero_ready, 3)
            dve.wait_ge(c_silu, 1)
            step(nc.vector.tensor_copy(ad[:, :, 0:2], csil[:, :, :]))
            nc.vector.tensor_tensor(ad[:, :, 2:4], csil[:, :, :], ad[:, :, 0:2].bitcast(f32),
                                    ALU.subtract).then_inc(ad_ready, 1)
            dve.wait_ge(in_gate, 80)
            step(nc.vector.tensor_tensor(lb[:, :, :], lbr[:, :, 0, :], lbr[:, :, 1, :], ALU.max))
            step(nc.vector.tensor_tensor(lbr[:, :, 0, :], lbr[:, :, 0, :], lb[:, :, :], ALU.subtract))
            nc.vector.tensor_tensor(lbr[:, :, 1, :], lbr[:, :, 1, :], lb[:, :, :], ALU.subtract).then_inc(lb_max, 1)
            dve.wait_ge(lb_exp, 1)
            step(nc.vector.tensor_tensor(oml[:, :, :], lbr[:, :, 0, :], lbr[:, :, 1, :], ALU.add))
            step(nc.vector.reciprocal(oml[:, :, :], oml[:, :, :]))
            step(nc.vector.tensor_tensor(lb[:, :, :], lbr[:, :, 0, :], oml[:, :, :], ALU.mult))
            step(nc.vector.tensor_scalar(oml[:, :, :], lb[:, :, :], -1.0, 1.0, ALU.mult, ALU.add))
            with pos.loop(dve, ADA_CHUNKS // 3, {"piece": 12, "pe": 12, "step": 0}) as i:
                for j in range(3):
                    pos.add("pe", 4)
                    prep(4)
                    dve.wait_ge(piece_used, pos("pe"))
                    nc.vector.tensor_copy(ada_out[:, bass.ds(i * 1536 + j * 512, 512)],
                                          ps[0:4, 4 + j, :]).then_inc(ada_free[j], 1)
            dve.wait_ge(mod_mm, 1)
            a, b_ = FEAT["b_ada"]
            step(nc.vector.tensor_tensor(mod[:, :, :], ps[:, 7, 0:96].rearrange("p (m c) -> p m c", c=2),
                                         ft[:, a:b_].unsqueeze(2).to_broadcast([P, 48, 2]), ALU.add))
            for n, (g, m, c) in enumerate((("g_pre_mix", 8, 0), ("g_pre_mix", 8, 1), ("g_pre_ffn", 32, 0))):
                step(nc.vector.scalar_tensor_tensor(gains[:, n, :], mod[:, m:m + 8, c], 1.0, vec(g), ALU.add, ALU.mult))
            dve.wait_ge(gate_mm, 1)
            for g, dst in enumerate((gt1, gt2)):
                step(nc.vector.tensor_tensor(dst[:, :], ps[:, 2 * g:2 * g + 2, :].rearrange("p a b -> p (a b)"),
                                             gate_rows[:, g, :], ALU.add))
                ins = nc.vector.tensor_tensor(dst[:, :], dst[:, :], gate_rows[:, 2 + g, :], ALU.mult)
                if g == 0:
                    step(ins)
                else:
                    ins.then_inc(mod_ready, 1)
            ahead()
            dve.wait_ge(in_ctx, 16)
            norm_x(ctx_tok)
            norm_lo([(x_hi, x_lo, gains[:, 1, :], mod[:, :, 1])])

            def take(dst):
                pos.add("pe", 4)
                ahead()
                b = pos.n["fill"] % 2
                pos.add("fill")
                dve.wait_ge(piece_used, pos("pe"))
                nc.vector.tensor_copy(dst, ps[:, 2 * b:2 * b + 2, :]).then_inc(g_free, 1)

            def forget(d, n):
                dve.wait_ge(sig_ready, n)
                for t in range(NT):
                    nc_ = nc.vector.tensor_tensor(zk[:, d, t, :], zk[:, d, t, :], oml[:, d, :], ALU.mult)
                    if t == 0:
                        step(nc_)
                    else:
                        nc_.then_inc(k_ready, 1)
                    step(nc.vector.tensor_tensor(zf[:, d, t, :], zf[:, d, t, :], oml[:, d, :], ALU.mult))
                    f = nc.vector.tensor_tensor(zf[:, d, t, :], zf[:, d, t, :], lb[:, d, :], ALU.add)
                    if t == 0:
                        step(f)
                    else:
                        f.then_inc(f_ready, 1)

            for dst in (zf[:, 0, :, :], zf[:, 1, :, :], zv[:, 0, :, :]):
                take(dst)
            forget(0, 1)
            forget(1, 2)
            for d in range(2):
                for t in range(NT):
                    dve.wait_ge(cx_exp, 2 * d + t + 1)
                    nc.vector.tensor_tensor(kc(d, t), kc(d, t), zk[:, d, t, :], ALU.mult).then_inc(cx_k, 1)
                dve.wait_ge(cx_s, d + 1)
                nc.vector.tensor_copy(s0[:, d, :], ps[:, 4 + d, :]).then_inc(cx_ready, 1)
            norm_x(x_tok)
            norm_lo([(x_hi, x_lo, gains[:, 0, :], mod[:, :, 0])])
            for dst in (zf[:, 0, :, :], xn[:, :, 0:512], zv[:, 0, :, :], zq[:, 0, :, :]):
                take(dst)
            forget(0, 3)
            for r, dst in enumerate((zf, zv, zq)):
                dve.wait_ge(flip_mm, r + 1)
                nc.vector.tensor_copy(dst[:, 1, :, :], ps[:, 2 * r:2 * r + 2, :]).then_inc(flip_ready, 1)
            forget(1, 4)
            dve.wait_ge(ats_zero, 1)
            for g in range(4):
                d, a = g // 2, g % 2
                dve.wait_ge(sc_t, g + 1)
                dve.wait_ge(sc_x, 9 * (g + 1))
                if a == 0:
                    step(nc.vector.tensor_copy(dt[:, :, :], qp[:, :, P - 1:P]))
                qt = ps[:, 0, :].rearrange("p (h t) -> p h t", h=4)
                kt = ps[:, 1, :].rearrange("p (h t) -> p h t", h=4)
                for dst, src in ((ex[:, 0, :, :], qt), (ki[:, :, :], kt), (qp[:, :, :], qt)):
                    nc.vector.tensor_tensor(dst, dst, src, ALU.mult).then_inc(sc_m, 1)
                for lev, half in enumerate((CHUNK, 2 * CHUNK, 4 * CHUNK), 1):
                    for side, src in ((1, qt), (0, kt)):
                        dst = ex[:, lev, :, :].rearrange("p h (b s u) -> p h b s u", s=2, u=half)[:, :, :, side, :]
                        part = src.rearrange("p h (b s u) -> p h b s u", s=2, u=half)[:, :, :, side, :]
                        nc.vector.tensor_tensor(dst, dst, part, ALU.mult).then_inc(sc_m, 1)
                dve.wait_ge(sc_at, g + 1)
                nc.vector.copy_predicated(ats[:, :, :], causal[:, :, :],
                                          ps[:, 7, :].rearrange("p (h t) -> p h t", h=4)).then_inc(sc_ats, 1)
                if a == 0:
                    dve.wait_ge(sc_kh, d + 1)
                    nc.vector.tensor_tensor(kh[:, :], kh[:, :], zk[:, d, 0, :], ALU.mult).then_inc(sc_kk, 1)
                    dve.wait_ge(sc_u, d + 1)
                    for h in range(GLA_HEADS):
                        c = slice(h * P, (h + 1) * P)
                        step(nc.vector.scalar_tensor_tensor(s1[:, h, :], s0[:, d, c], dt[:, h, :], ps[:, 3, c],
                                                            ALU.mult, ALU.add))
                dve.wait_ge(sc_o, g + 1)
                nc.vector.tensor_copy(o_dir[:, d, a, :], ps[:, 4, :]).then_inc(sc_end, 1)
            dve.wait_ge(sc_flip, 1)
            for t in range(NT):
                nc.vector.tensor_tensor(o_dir[:, 0, t, :], o_dir[:, 0, t, :], ps[:, 5 + t, :],
                                        ALU.add).then_inc(sc_sum, 1)
            for dst in (sgl[:, :, :], u_tok[:, :, :], vl[:, :, :], ga[:, :, 0:512], ga[:, :, 512:], gb[:, :, 0:512],
                        gb[:, :, 512:]):
                take(dst)
            o = o_dir[:, 0, :, :]
            o8 = o.rearrange("p t (h n) -> p (t h) n", h=GLA_HEADS)
            sq8 = sq[:, :, :].rearrange("p t (h n) -> p (t h) n", h=GLA_HEADS)
            step(nc.vector.tensor_tensor(sq[:, :, :], o, o, ALU.mult))
            nc.vector.reduce_sum(st8[:, :], sq8, AXX).then_inc(m_ms, 1)
            dve.wait_ge(m_rms, 1)
            step(nc.vector.reciprocal(st8b[:, :], st8b[:, :]))
            step(nc.vector.tensor_tensor(o8, o8, st8b[:, :].unsqueeze(2).to_broadcast([P, 8, P]), ALU.mult))
            dve.wait_ge(silu_g, 2)
            nc.vector.tensor_tensor(o, o, sgl[:, :, :], ALU.mult).then_inc(m_a, 1)
            dve.wait_ge(gelu_r, 2)
            dve.wait_ge(in_merge, 48)
            step(nc.vector.reduce_sum(mean[:, :], vl[:, :, :], AXX))
            step(nc.vector.tensor_scalar(mean[:, :], mean[:, :], -1.0 / CM, None, ALU.mult))
            for t in range(NT):
                step(nc.vector.tensor_scalar(vl[:, t, :], vl[:, t, :], mean[:, t:t + 1], None, ALU.add))
            step(nc.vector.tensor_tensor(sq[:, :, :], vl[:, :, :], vl[:, :, :], ALU.mult))
            nc.vector.reduce_sum(ss[:, :], sq[:, :, :], AXX).then_inc(m_ms, 1)
            dve.wait_ge(m_rms, 2)
            step(nc.vector.reciprocal(rstd[:, :], rms[:, :]))
            for t in range(NT):
                step(nc.vector.scalar_tensor_tensor(vl[:, t, :], vl[:, t, :], rstd[:, t:t + 1], ln_g[:, :], ALU.mult,
                                                    ALU.mult))
                ins = nc.vector.tensor_tensor(vl[:, t, :], vl[:, t, :], ln_b[:, :], ALU.add)
                if t == 0:
                    step(ins)
                else:
                    ins.then_inc(m_v, 1)
            gh, _ = FEAT["g_hgrn"]
            dve.wait_ge(m_ahi, 1)
            nc.vector.scalar_tensor_tensor(g_lo[:, 0:4, :], ps[:, 0:2, :].rearrange("p a (h t) -> p (a h) t", h=2),
                                           ft[:, gh:gh + 1], g_hi[:, 0:4, :].bitcast(f32), ALU.mult,
                                           ALU.subtract).then_inc(m_alo, 1)
            dve.wait_ge(m_z, 1)
            bs, _ = FEAT["b_spatial"]
            for t in range(NT):
                for g in range(GLA_HEADS):
                    c = slice(g * P, (g + 1) * P)
                    ins = nc.vector.scalar_tensor_tensor(u_tok[:, t, c], ps[:, 2 + t, c], ft[:, bs + g:bs + g + 1],
                                                         u_tok[:, t, c], ALU.add, ALU.mult)
                    if t == 1 and g == 3:
                        ins.then_inc(m_b, 1)
                    else:
                        step(ins)
            dve.wait_ge(m_bhi, 1)
            nc.vector.tensor_tensor(g_lo[:, 4:8, :], ps[:, 4:6, :].rearrange("p a (h t) -> p (a h) t", h=2),
                                    g_hi[:, 4:8, :].bitcast(f32), ALU.subtract).then_inc(m_blo, 1)
            for _ in range(4):
                pos.add("pe", 2)
                ahead()
            dve.wait_ge(gate_r, 4)
            dve.wait_ge(piece_used, pos("pe"))
            for t in range(NT):
                for src, gate in ((wide(t), ga), (ps[:, 2 * t:2 * t + 2, :].rearrange("p a b -> p (a b)"), gb)):
                    step(nc.vector.tensor_tensor(gate[:, t, :], gate[:, t, :], src, ALU.mult))
                nc.vector.tensor_tensor(xn[:, t, :], ga[:, t, :], gb[:, t, :], ALU.add).then_inc(xn_ready, 1)
            norm_lo([(x_hi, x_lo, None, None)])
            for _ in range(2):
                pos.add("pe", 4)
                ahead()

            def gated_residual(gate, ready):
                inverse()
                for t in range(NT):
                    step(nc.vector.scalar_tensor_tensor(xn[:, t, :], wide(t), rstd[:, t:t + 1], gate[:, :], ALU.mult,
                                                        ALU.mult))
                    nc.vector.tensor_tensor(x_tok[:, t, :], x_tok[:, t, :], xn[:, t, :], ALU.add).then_inc(ready, 1)

            gated_residual(gt1, x_ready)
            norm_x(x_tok)
            dve.wait_ge(in_router, 32)
            step(nc.vector.tensor_copy(wr_hi[:, :, :], wr[:, :, :]))
            nc.vector.tensor_tensor(wr_lo[:, :, :], wr[:, :, :], wr_hi[:, :, :].bitcast(f32), ALU.subtract
                                    ).then_inc(r_w, 2)
            norm_lo([(x_hi, x_lo, gains[:, 2, :], mod[:, 24:, 0])])
            dve.wait_ge(r_sig, 1)
            step(nc.vector.tensor_tensor(sel[:, :, :], sc[:, :, :], br[:, :].unsqueeze(1).to_broadcast([P, NT, EXPERTS]),
                                         ALU.add))
            for t in range(NT):
                for g in range(GROUPS):
                    step(nc.vector.max(best[:, t, g, :], sel[:, t, g * 8:(g + 1) * 8]))
            step(nc.vector.tensor_tensor(gsc[:, :, :], best[:, :, :, 0], best[:, :, :, 1], ALU.add))
            for t in range(NT):
                step(nc.vector.max(gm8[:, t, :], gsc[:, t, :]))
            step(nc.vector.memset(gm8[:, :, 4:8], BIG))
            for t in range(NT):
                step(nc.vector.match_replace(gkeep[:, t, :], gm8[:, t, :], gsc[:, t, :], BIG))
            step(nc.vector.tensor_scalar(gkeep2[:, :, :], gkeep[:, :, :], BIG, None, ALU.is_ge))
            step(nc.vector.tensor_scalar(gkeep2[:, :, :], gkeep2[:, :, :], BIG, -BIG, ALU.mult, ALU.add))
            step(nc.vector.tensor_tensor(
                sel[:, :, :].rearrange("p t (g e) -> p (t g) e", g=GROUPS),
                sel[:, :, :].rearrange("p t (g e) -> p (t g) e", g=GROUPS),
                gkeep2[:, :, :].rearrange("p t g -> p (t g)").unsqueeze(2).to_broadcast([P, NT * GROUPS, 8]), ALU.add))
            for t in range(NT):
                step(nc.vector.max(gm8[:, t, :], sel[:, t, :]))
                step(nc.vector.match_replace(t64[:, t, :], gm8[:, t, :], sel[:, t, :], BIG))
            step(nc.vector.tensor_scalar(t64[:, :, :], t64[:, :, :], BIG, None, ALU.is_ge))
            step(nc.vector.tensor_tensor(t64[:, :, :], t64[:, :, :], sc[:, :, :], ALU.mult))
            step(nc.vector.reduce_sum(wsum[:, :], t64[:, :, :], AXX))
            step(nc.vector.reciprocal(wsum[:, :], wsum[:, :]))
            for t in range(NT):
                step(nc.vector.tensor_scalar(comb[:, t, 0:EXPERTS], t64[:, t, :], wsum[:, t:t + 1], ROUTED_SCALE,
                                             ALU.mult, ALU.mult))
            step(nc.vector.memset(comb[:, :, EXPERTS:], 1.0))
            units(32, 0, routed=True)
            gated_residual(gt2, res_ready)


def kernel(**inputs):
    import concourse.bacc as _bacc
    from concourse.bass_utils import run_bass_kernel_spmd as _run

    nc, arrays, _ = assemble(_bacc, inputs)
    r = _run(nc, [arrays], core_ids=[0])
    return r.results[0]["out_dram"].reshape(1, T, D)


def stream_of(a):
    pieces = []

    def cols(w, c0, width=512):
        k = w.shape[0] // P
        part = w[:, c0:c0 + width].reshape(k // 2, 2, P, width)
        pieces.extend(part.transpose(0, 2, 1, 3).reshape(k // 2, P, 2 * width))

    def unit_gu(w, c_gate, c_up):
        part = np.stack([w[:, c_gate:c_gate + HID], w[:, c_up:c_up + HID]], 1).reshape(KD // 2, 2, P, 2 * HID)
        pieces.extend(part.transpose(0, 2, 1, 3).reshape(KD // 2, P, 4 * HID))

    def unit_down(w, r0):
        pieces.extend(w[r0:r0 + HID].reshape(2, P, D))

    def units(gus, downs):
        unit_gu(*gus[0])
        for g, d in zip(gus[1:] + [None], downs):
            if g is not None:
                unit_gu(*g)
            unit_down(*d)

    def ffn(layer):
        gu, down = a["w_gate_up"][layer], a["w_down"][layer]
        units([(gu, u * HID, D_FF + u * HID) for u in range(FFN_UNITS)], [(down, u * HID) for u in range(FFN_UNITS)])

    pw = a["pool_w"][0].reshape(2, 2, 2, P, 256)
    pieces.extend(pw.transpose(0, 3, 1, 2, 4).reshape(2, P, 1024))
    ffn(0)
    for c in range(4):
        cols(a["w_kv"], c * 512)
    for c in range(2):
        cols(a["w_q"][0], c * 512)
    for c in range(2):
        cols(a["w_o"][0], c * 512)
    ffn(1)
    for c in range(ADA_CHUNKS):
        cols(a["w_ada_2"][0], c * 512)
    w_in = a["w_in_2"][0]
    for c in (1, 2, 3):
        cols(w_in, c * 512)
    for c in (1, 2, 3, 0, 4, 5, 6, 7, 8, 9, 10):
        cols(w_in, c * 512)
    for w in (a["w_branch_a_2"][0], a["w_branch_b_2"][0], a["w_out_2"][0]):
        for c in range(2):
            cols(w, c * 512)
    egu, edn = a["w_expert_gu_2"][0], a["w_expert_down_2"][0]
    units([(egu[e], 0, HID) for e in range(EXPERTS)] + [(a["w_shared_gu_2"][0], 0, HID)],
          [(edn[e], 0) for e in range(EXPERTS)] + [(a["w_shared_down_2"][0], 0)])
    out = np.empty((len(pieces) // 2, P, 2, PIECE), np.float32)
    for n, p in enumerate(pieces):
        out[n // 2, :, n % 2, :] = p
    return out.reshape(len(pieces) // 2, P, 2 * PIECE)


def layouts(a):
    consts, pool, causal, buckets = constants()
    feat = np.zeros((P, NFEAT), np.float32)

    def vec(name, v):
        lo, hi = FEAT[name]
        feat[:, lo:hi] = v.reshape(hi - lo, P).T

    vec("norm_mixer0", a["norm_mixer"][0])
    vec("norm_mixer1", a["norm_mixer"][1])
    vec("norm_ffn0", a["norm_ffn"][0])
    vec("norm_ffn1", a["norm_ffn"][1])
    vec("kv_norm", a["kv_norm"])
    vec("g_pre_mix", a["g_pre_mix_2"][0])
    vec("g_pre_ffn", a["g_pre_ffn_2"][0])
    vec("g_hgrn", a["g_hgrn_out_2"][0])
    vec("b_ada", a["b_ada_2"][0])
    lo, hi = FEAT["b_spatial"]
    feat[:, lo:hi] = a["b_spatial_2"][0]
    lo, hi = FEAT["c"]
    feat[:, lo:hi] = np.stack([a["c_2"][0].reshape(KD, P).T, a["c_ctx_2"].reshape(KD, P).T], 2).reshape(P, 2 * KD)
    rows = np.zeros((1, NROWS), np.float32)
    for name, v in (("pool_scale", a["pool_scale"]), ("final_norm", a["final_norm"]),
                    ("gt1_b", a["b_ada_2"][0, 2 * D:3 * D]), ("gt2_b", a["b_ada_2"][0, 5 * D:]),
                    ("g_post_mix", a["g_post_mix_2"]), ("g_post_ffn", a["g_post_ffn_2"]), ("ln_g", a["cm_ln_g_2"]),
                    ("ln_b", a["cm_ln_b_2"]), ("lb", a["lb_logits_2"]), ("b_router", a["b_router_2"])):
        lo, hi = ROWS[name]
        rows[0, lo:hi] = v.reshape(-1)
    return {
        "stream": stream_of(a), "x": a["x"][0], "ctx": a["ctx_2"][0], "feat": feat, "rows": rows, "consts": consts,
        "pool_c": pool, "causal_c": causal, "buckets_c": buckets, "rel_bias": a["rel_bias"],
        "w_router": a["w_router_2"][0].reshape(KD, P, EXPERTS).transpose(1, 0, 2).reshape(P, KD * EXPERTS),
        "w_spatial": a["w_spatial_2"][0].transpose(2, 0, 1).reshape(P, GLA_HEADS * P),
    }


def assemble(bacc, inputs):
    nc = bacc.Bacc("TRN2", target_bir_lowering=False, num_devices=1)
    arrays, args = {}, {}
    for name, v in layouts({k: np.asarray(v) for k, v in inputs.items()}).items():
        v = np.ascontiguousarray(v)
        arrays[name + "_dram"] = v
        args[name] = nc.dram_tensor(name + "_dram", v.shape, mybir.dt.from_np(v.dtype), kind="ExternalInput").ap()
    args["out"] = nc.dram_tensor("out_dram", (T, D), mybir.dt.float32, kind="ExternalOutput").ap()
    program(nc, **args)
    return nc, arrays, args
```

```python
import math
from contextlib import ExitStack, contextmanager

import numpy as np

import concourse.bass as bass
from concourse import mybir

P = 128
T = 256
NT = T // P
D = 1024
KD = D // P
D_FF = 2816
HID = 256
FFN_UNITS = D_FF // HID
EXPERTS = 64
MOE_UNITS = EXPERTS + 1
GROUPS = 8
HEADS = 16
DH = 64
BUCKETS = 32
MAX_DISTANCE = 128
WINDOWS = (2, 4, 8, 16)
GLA_HEADS = 4
CHUNK = 16
CM = 512
ADA_CHUNKS = 12
EPS = 1e-6
BIG = 1e30
ROUTED_SCALE = 2.5

PIECE = 1024
RAW = 12
RING = 4

FEAT = {}
_at = 0
for _name, _n in (("norm_mixer0", 8), ("norm_mixer1", 8), ("norm_ffn0", 8), ("norm_ffn1", 8), ("kv_norm", 8),
                  ("g_pre_mix", 8), ("g_pre_ffn", 8), ("g_hgrn", 1), ("b_ada", 48), ("b_spatial", 4), ("c", 16)):
    FEAT[_name] = (_at, _at + _n)
    _at += _n
NFEAT = _at
ROWS = {}
_at = 0
for _name, _n in (("pool_scale", 1024), ("final_norm", 1024), ("gt1_b", 1024), ("gt2_b", 1024), ("g_post_mix", 1024),
                  ("g_post_ffn", 1024), ("ln_g", 512), ("ln_b", 512), ("lb", 2048), ("b_router", 64)):
    ROWS[_name] = (_at, _at + _n)
    _at += _n
NROWS = _at
CONST = {}
_at = 0
for _name, _n in (("ident", 128), ("flip", 128), ("prefix", 128), ("after", 128), ("before", 128), ("ones", 128),
                  ("levels", 512), ("sel_lat", 128)):
    CONST[_name] = (_at, _at + _n)
    _at += _n
NCONST = _at


def constants():
    u, t = np.arange(P)[:, None], np.arange(P)[None, :]
    c = np.zeros((P, NCONST), np.float32)

    def put(name, value):
        a, b = CONST[name]
        c[:value.shape[0], a:b] = value

    put("ident", (u == t).astype(np.float32))
    put("flip", (u == P - 1 - t).astype(np.float32))
    put("prefix", (u <= t).astype(np.float32))
    put("after", (u > t).astype(np.float32))
    put("before", (u < t).astype(np.float32))
    put("ones", np.ones((P, P), np.float32))
    mid = t // CHUNK * CHUNK + CHUNK // 2 - 1
    inner = ((u > mid) & (u <= t)).astype(np.float32) - ((u > t) & (u <= mid)).astype(np.float32)
    levels = [inner]
    for half in (CHUNK, 2 * CHUNK, 4 * CHUNK):
        m = t // (2 * half) * 2 * half + half
        levels.append(np.where(t < m, (u > t) & (u < m), (u >= m) & (u <= t)).astype(np.float32))
    put("levels", np.concatenate(levels, axis=1))
    r = np.arange(4)[:, None]
    put("sel_lat", np.repeat((r % 2 == 0).astype(np.float32), P, axis=1))
    s, q = np.arange(T)[:, None], np.arange(T)[None, :]
    pools = []
    for w in WINDOWS:
        cnt = np.minimum(q + 1, w)
        pools.append(((s <= q) & (s > q - w)) / cnt.astype(np.float32) - (s == q))
    pool = np.stack(pools, 1).astype(np.float32)
    pool = np.concatenate([pool[:P].reshape(P, 4 * T), pool[P:, :, P:].reshape(P, 4 * P)], axis=1)
    causal = np.repeat((u <= t).astype(np.int32)[:, None, :], GLA_HEADS, axis=1).reshape(P, GLA_HEADS * P)
    n = 255 - np.arange(384)
    exact = BUCKETS // 2
    far = np.maximum(n, exact).astype(np.float32)
    large = exact + (np.log(far / exact) / math.log(MAX_DISTANCE / exact) * (BUCKETS - exact)).astype(np.int32)
    bucket = np.where(n < exact, n, np.minimum(large, BUCKETS - 1))
    buckets = ((np.arange(BUCKETS)[:, None] == bucket[None, :]) & (n >= 0)[None, :]).astype(np.float32)
    return c, pool, causal, buckets


class Pos:

    def __init__(self):
        self.n, self.i, self.per = {}, None, {}

    def __call__(self, name, extra=0):
        v = self.n.get(name, 0) + extra
        return v if self.i is None else v + self.i * self.per.get(name, 0)

    def add(self, name, k=1):
        self.n[name] = self.n.get(name, 0) + k

    @contextmanager
    def loop(self, eng, times, per):
        start = dict(self.n)
        with eng.Fori(0, times) as i:
            self.i, self.per = i, per
            yield i
            self.i = None
        for name, v in self.n.items():
            d = v - start.get(name, 0)
            assert d == per.get(name, 0), (name, d)
            self.n[name] = v + d * (times - 1)


def program(nc, stream, x, ctx, feat, rows, consts, pool_c, causal_c, buckets_c, rel_bias, w_router, w_spatial, out):
    f32, f32r, i32 = mybir.dt.float32, mybir.dt.float32r, mybir.dt.int32
    ALU, ACT = mybir.AluOpType, mybir.ActivationFunctionType
    AXX = mybir.AxisListType.X
    es = ExitStack()
    with es:
        size = 207 * 1024
        es.enter_context(nc.sbuf_tensor("slab", [P, size // 4], f32))
        slab_at = nc.sbuf_base - size

        def place(start, *wanted):
            made = []
            for name, shape, *dt in wanted:
                n = 4 * int(np.prod(shape[1:]))
                assert start + n <= size, (name, start, n)
                made.append(nc.alloc_sbuf_tensor_at(name, shape, dt[0] if dt else f32, offset=slab_at + start))
                start += (n + 31) // 32 * 32
            return (*made, start)

        raw, w_hi, w_lo, x_tok, x_hi, x_lo, xn_at = place(
            0, ("raw", [P, RAW, PIECE]), ("w_hi", [P, RING, PIECE], f32r), ("w_lo", [P, RING, PIECE], f32r),
            ("x_tok", [P, NT, D]), ("x_hi", [P, KD, T], f32r), ("x_lo", [P, KD, T], f32r))
        (xn, cst, causal, ft, eps, zero, ss, rms, rstd, mod, gains, csil, ad, warm, phase) = place(
            xn_at, ("xn", [P, NT, D]), ("cst", [P, NCONST]), ("causal", [P, GLA_HEADS, P], i32), ("ft", [P, NFEAT]), ("eps", [P, 1]),
            ("zero", [P, P], f32r), ("ss", [P, 2]), ("rms", [P, 2]), ("rstd", [P, 2]), ("mod", [P, 48, 2]),
            ("gains", [P, 3, KD]), ("csil", [P, KD, 2]), ("ad", [P, KD, 4], f32r),
            ("warm", [P, 1]))
        a_hi, a_lo, a_tok, sg, unit_end = place(
            phase, ("a_hi", [P, NT, HID], f32r), ("a_lo", [P, NT, HID], f32r), ("a_tok", [P, NT, HID]),
            ("sg", [P, NT, HID]))
        pool_m, pool_s, oneh, rb, rv, _ = place(
            unit_end, ("pool_m", [P, 4 * T + 4 * P]), ("pool_s", [P, D]), ("oneh", [BUCKETS, 384]),
            ("rb", [BUCKETS, HEADS]), ("rv", [HEADS, 384]))
        q_even, q_odd, kT, v_tok, pt0, pt1, pr_odd, mx, rs, rr, att_end = place(
            phase, ("q_even", [P, KD, T]), ("q_odd", [P, KD, T]), ("kT", [P, KD, T]), ("v_tok", [P, NT, D]),
            ("pt0", [P, 4, T]), ("pt1", [P, 4, P]), ("pr_odd", [P, 12 * P]), ("mx", [P, 2, 8]), ("rs", [P, 2, 8]),
            ("rr", [P, 8]))
        h2_hi, h2_lo, _ = place(att_end, ("h2_hi", [P, KD, T], f32r), ("h2_lo", [P, KD, T], f32r))
        ada_out, end = place(att_end, ("ada_out", [4, 6 * D]))
        bias, _ = place(size - 4 * HEADS * T, ("bias", [P, HEADS, T]))
        assert end <= size - 4 * HEADS * T
        fin_g, _ = place(unit_end, ("fin_g", [P, D]))
        tail = (size - 4 * (2 * 512 + 2 * D + NT * MOE_UNITS) - 64) // 32 * 32
        s0, gt1, gt2, comb, _ = place(
            tail, ("s0", [P, 2, 512]), ("gt1", [P, D]), ("gt2", [P, D]), ("comb", [P, NT, MOE_UNITS]))
        lb, oml, lbend = place(phase, ("lb", [P, 2, 512]), ("oml", [P, 2, 512]))
        zk, zf, zv, zq, ex, ki_at = place(
            lbend, ("zk", [P, 2, NT, 512]), ("zf", [P, 2, NT, 512]), ("zv", [P, 2, NT, 512]),
            ("zq", [P, 2, NT, 512]), ("ex", [P, 4, GLA_HEADS, P]))
        ki, qp, ats, kh, s1, dt, o_dir_at = place(
            ki_at, ("ki", [P, GLA_HEADS, P]), ("qp", [P, GLA_HEADS, P]), ("ats", [P, GLA_HEADS, P]),
            ("kh", [P, 512]), ("s1", [P, GLA_HEADS, P]), ("dt", [P, GLA_HEADS, 1]))
        o_dir, o_dir_end = place(o_dir_at, ("o_dir", [P, 2, NT, 512]))
        zf_c, _ = place(o_dir_at, ("zf_c", [P, 2, NT, 512]))
        zv_c, _ = place(ki_at, ("zv_c", [P, NT, 512]))
        lbr, gate_rows, ctx_tok, end = place(
            unit_end + 4 * D, ("lbr", [P, 2, 2, 512]), ("gate_rows", [P, 4, D]), ("ctx_tok", [P, NT, D]))
        assert end <= tail
        sgl, u_tok, end = place(phase, ("sgl", [P, NT, 512]), ("u_tok", [P, NT, CM]))
        assert end <= lbend
        vl, ga0, _ = place(xn_at, ("vl", [P, NT, CM]), ("ga0", [P, NT, 512]))
        sq, ga1, gb0, gb1, g_hi, g_lo, end = place(
            lbend, ("sq", [P, NT, CM]), ("ga1", [P, NT, 512]), ("gb0", [P, NT, 512]), ("gb1", [P, NT, 512]),
            ("g_hi", [P, KD, T], f32r), ("g_lo", [P, KD, T], f32r))
        assert end <= o_dir_at
        squares, _ = place(o_dir_at, ("squares", [P, D]))
        ln_g, ln_b, wst, st8, st8b, mean, end = place(
            o_dir_end, ("ln_g", [P, CM]), ("ln_b", [P, CM]), ("wst", [P, GLA_HEADS, P]), ("st8", [P, 8]),
            ("st8b", [P, 8]), ("mean", [P, 2]))
        assert end <= tail
        (wr, wr2, br, sc, sel, best, gsc, gm8, gkeep, gkeep2, t64, wsum, _) = place(
            unit_end, ("wr", [P, KD, EXPERTS]), ("wr2", [P, KD, 2, EXPERTS], f32r),
            ("br", [P, EXPERTS]), ("sc", [P, NT, EXPERTS]), ("sel", [P, NT, EXPERTS]), ("best", [P, NT, 8, 8]),
            ("gsc", [P, NT, 8]), ("gm8", [P, NT, 8]), ("gkeep", [P, NT, 8]), ("gkeep2", [P, NT, 8]),
            ("t64", [P, NT, EXPERTS]), ("wsum", [P, NT]))
        ps = es.enter_context(nc.psum_tensor("ps", [P, 8, 512], f32))
        scratch = nc.dram_tensor("bias_scratch", (HEADS, P, 384), f32, kind="Internal").ap()

        def const(name, rows_=P):
            a, b = CONST[name]
            return cst[0:rows_, a:b]

        def vec(name):
            a, b = FEAT[name]
            return ft[:, a:b]

        ident = const("ident")

        def whole(k):
            return xn[:, k % 2, (k // 2) * T:(k // 2 + 1) * T]

        def probs(b):
            if b % 2:
                return (pr_odd[:, 0:512].rearrange("p (h k) -> p h k", h=4),
                        pr_odd[:, 512:1536].rearrange("p (h k) -> p h k", h=4))
            return (xn[:, 0, 0:512].rearrange("p (h k) -> p h k", h=4),
                    xn[:, 1, :].rearrange("p (h k) -> p h k", h=4))

        names = set()

        def sem(name):
            assert name not in names
            names.add(name)
            return es.enter_context(nc.semaphore(name))

        loaded = [sem(f"loaded{i}") for i in range(RAW // 2)]
        hi_ready, lo_ready, piece_used = sem("hi_ready"), sem("lo_ready"), sem("piece_used")
        g_free = sem("g_free")
        x_ready, rms_ready, xn_ready = sem("x_ready"), sem("rms_ready"), sem("xn_ready")
        t_done, h_hi, h_lo = sem("t_done"), sem("h_hi"), sem("h_lo")
        silu_ready, act_ready, act_t, act_hi = sem("silu_ready"), sem("act_ready"), sem("act_t"), sem("act_hi")
        dve_step, act_step = sem("dve_step"), sem("act_step")
        in_x, in_first, in_second, in_fin, in_gate, in_ctx, in_merge, in_router = (
            sem("in_x"), sem("in_first"), sem("in_second"), sem("in_fin"), sem("in_gate"), sem("in_ctx"), sem("in_merge"), sem("in_router"))
        bias_mm, bias_rows, bias_out, bias_in = sem("bias_mm"), sem("bias_rows"), sem("bias_out"), sem("bias_in")
        q_zero = sem("q_zero")
        s_done, p_raw, p_exp, p_ready, pt_done, pt0_ready, pt1_ready, pv_done, o_hi, o_lo = (
            sem("s_done"), sem("p_raw"), sem("p_exp"), sem("p_ready"), sem("pt_done"), sem("pt0_ready"),
            sem("pt1_ready"), sem("pv_done"), sem("o_hi"), sem("o_lo"))
        lb_diff, lb_ready, pool_step = sem("lb_diff"), sem("lb_ready"), sem("pool_step")
        c_silu, ad_ready, ada_copied, mod_mm, gate_mm, mod_ready, gate_ready = (
            sem("c_silu"), sem("ad_ready"), sem("ada_copied"), sem("mod_mm"), sem("gate_mm"), sem("mod_ready"),
            sem("gate_ready"))
        gates_done = sem("gates_done")
        sig_ready, f_ready, log_ready, k_ready = (
            sem("sig_ready"), sem("f_ready"), sem("log_ready"), sem("k_ready"))
        flip_mm, flip_ready = sem("flip_mm"), sem("flip_ready")
        cx_r, cx_exp, cx_k, cx_s, cx_ready = sem("cx_r"), sem("cx_exp"), sem("cx_k"), sem("cx_s"), sem("cx_ready")
        (sc_e, sc_t, sc_x, sc_m, sc_at, sc_ats, sc_r, sc_kh, sc_kk, sc_u, sc_o, sc_end, sc_flip, sc_sum) = (
            sem(n) for n in ("sc_e", "sc_t", "sc_x", "sc_m", "sc_at", "sc_ats", "sc_r", "sc_kh", "sc_kk", "sc_u",
                             "sc_o", "sc_end", "sc_flip", "sc_sum"))
        silu_g, gelu_r, gate_r, side_free = sem("silu_g"), sem("gelu_r"), sem("gate_r"), sem("side_free")
        (m_ms, m_rms, m_a, m_at, m_ahi, m_alo, m_v, m_z, m_b, m_bt, m_bhi, m_blo) = (
            sem(n) for n in ("m_ms", "m_rms", "m_a", "m_at", "m_ahi", "m_alo", "m_v", "m_z", "m_b", "m_bt", "m_bhi",
                             "m_blo"))
        zero_ready, ats_zero = sem("zero_ready"), sem("ats_zero")
        r_w, r_mm, r_sum, r_sig = sem("r_w"), sem("r_mm"), sem("r_sum"), sem("r_sig")
        sums_done, rstd_ready, y_squared = sem("sums_done"), sem("rstd_ready"), sem("y_squared")
        h_full = sem("h_full")
        res_ready, stored = sem("res_ready"), sem("stored")

        XR_POOL, XR_FFN0, XR_WO, XR_FFN1, XR_FIN, XR_MIX = 2, 4, 6, 8, 10, 12
        LOADS = stream.shape[0]
        N_PIECES = 2 * LOADS
        MOD_TILES = (*range(16), *range(24, 40))
        Z0 = 2 * FFN_UNITS + 6

        UNITS_PER = {"piece": 12, "pe": 12, "fill": 2, "act": 4, "t": 2}

        def kc(d, t):
            return ex[:, 2 * d + t, :, :].rearrange("p h n -> p (h n)")

        block = es.enter_context(nc.Block())

        @block.sync
        def _(sp):
            def load(l, slot, free_at):
                if free_at is not None:
                    sp.wait_ge(lo_ready, free_at)
                sp.dma_start(raw[:, 2 * slot:2 * slot + 2, :].rearrange("p a b -> p (a b)"),
                             stream[l]).then_inc(loaded[slot], 16)

            sp.dma_start(x_tok[:, :, :], x.rearrange("(t p) d -> p t d", p=P)).then_inc(in_x, 16)
            sp.dma_start(cst[:, :], consts).then_inc(in_first, 16)
            sp.dma_start(ft[:, :], feat).then_inc(in_first, 16)
            sp.dma_start(pool_m[:, :], pool_c).then_inc(in_first, 16)
            half = RAW // 2
            sp.wait_ge(in_x, 16)
            for l in range(2 * half):
                load(l, l % half, None if l < half else 2 * (l - half) + 2)
            whole = (LOADS - 2 * half) // half
            with sp.Fori(0, whole) as i:
                for j in range(half):
                    load(i * half + (2 * half + j), j, i * RAW + (RAW + 2 * j + 2))
            for l in range((2 + whole) * half, LOADS):
                load(l, l % half, 2 * (l - half) + 2)
            for t in range(NT):
                sp.wait_ge(res_ready, t + 1)
                sp.dma_start(out[t * P:(t + 1) * P, :], x_tok[:, t, :]).then_inc(stored, 16)
            sp.wait_ge(stored, 16 * NT)

        @block.gpsimd
        def _(pool):
            def row(dst, name):
                a, b = ROWS[name]
                return pool.dma_start(dst, rows[0:1, a:b].partition_broadcast(P))

            pos = Pos()

            def shifted_lo():
                for k in range(KD):
                    pool.wait_ge(h_full, pos("full", k + 1))
                    nc.gpsimd.tensor_tensor(x_lo[:, k, :], whole(k), x_hi[:, k, :].bitcast(f32), ALU.subtract
                                            ).then_inc(h_lo, 1)
                pos.add("full", KD)

            nc.gpsimd.memset(eps[:, :], EPS).then_inc(zero_ready, 1)
            nc.gpsimd.memset(zero[:, :].bitcast(f32), 0.0).then_inc(zero_ready, 1)
            pool.wait_ge(in_first, 48)
            row(pool_s[:, :], "pool_scale").then_inc(in_second, 16)
            pool.dma_start(oneh[:, :], buckets_c).then_inc(in_second, 16)
            pool.dma_start(rb[:, :], rel_bias).then_inc(in_second, 16)
            pool.dma_start(causal[:, :, :].rearrange("p h k -> p (h k)"), causal_c).then_inc(in_second, 16)
            pool.wait_ge(bias_rows, 1)
            pool.dma_start(scratch, rv[:, :].unsqueeze(1).to_broadcast([HEADS, P, 384])).then_inc(bias_out, 16)
            pool.wait_ge(bias_out, 16)
            shifted = bass.AP(tensor=scratch.tensor, offset=scratch.offset + P - 1,
                              ap=[[384 - 1, P], [P * 384, HEADS], [1, T]])
            pool.dma_start(bias[:, :, :], shifted).then_inc(bias_in, 16)
            pool.wait_ge(x_ready, XR_FFN0)
            nc.gpsimd.memset(q_even[DH:, :, :], 0.0).then_inc(q_zero, 1)
            nc.gpsimd.memset(q_odd[0:DH, :, :], 0.0).then_inc(q_zero, 1)
            pool.wait_ge(x_ready, XR_WO)
            row(fin_g[:, :], "final_norm").then_inc(in_fin, 16)
            pool.dma_start(ctx_tok[:, :, :], ctx.rearrange("(t p) d -> p t d", p=P)).then_inc(in_ctx, 16)
            for k, name in enumerate(("gt1_b", "gt2_b", "g_post_mix", "g_post_ffn")):
                row(gate_rows[:, k, :], name).then_inc(in_gate, 16)
            row(lbr[:, :, :, :].rearrange("p a b c -> p (a b c)"), "lb").then_inc(in_gate, 16)
            row(ln_g[:, :], "ln_g").then_inc(in_merge, 16)
            row(ln_b[:, :], "ln_b").then_inc(in_merge, 16)
            pool.dma_start(wst[:, :, :].rearrange("p g q -> p (g q)"), w_spatial).then_inc(in_merge, 16)
            pool.wait_ge(in_gate, 80)
            nc.gpsimd.tensor_tensor(lbr[:, :, 0, :], lbr[:, :, 0, :], lbr[:, :, 1, :], ALU.subtract).then_inc(lb_diff, 1)
            pool.wait_ge(gate_ready, 1)
            for g, dst in enumerate((gt1, gt2)):
                nc.gpsimd.tensor_tensor(dst[:, :], dst[:, :], gate_rows[:, g, :], ALU.add).then_inc(pool_step, 1)
                pool.wait_ge(pool_step, g + 1)
                nc.gpsimd.tensor_tensor(dst[:, :], dst[:, :], gate_rows[:, 2 + g, :], ALU.mult).then_inc(gates_done, 1)
            shifted_lo()
            shifted_lo()
            pool.wait_ge(cx_ready, 2)
            nc.gpsimd.memset(ats[:, :, :], 0.0).then_inc(ats_zero, 1)
            pool.wait_ge(x_ready, XR_MIX)
            pool.dma_start(wr[:, :, :].rearrange("p k e -> p (k e)"), w_router).then_inc(in_router, 16)
            row(br[:, :], "b_router").then_inc(in_router, 16)
            shifted_lo()

        @block.tensor
        def _(pe):
            pos = Pos()

            def three(o, l_hi, l_lo, r_hi, r_lo, start, stop, shared=False):
                pe.matmul(o, l_hi, r_hi, start=start, stop=False, skip_group_check=shared)
                pe.matmul(o, l_hi, r_lo, start=False, stop=False, skip_group_check=shared)
                return pe.matmul(o, l_lo, r_hi, start=False, stop=stop, skip_group_check=shared)

            def two_threes(outs, l_hi, l_lo, r_hi, r_lo, stop=False):
                halves = [(outs[h], slice(h * 512, (h + 1) * 512)) for h in range(2)]
                for o, c in halves:
                    pe.matmul(o, l_hi, r_hi[:, c], start=False, stop=False, skip_group_check=True)
                    pe.matmul(o, l_hi, r_lo[:, c], start=False, stop=False, skip_group_check=True)
                for o, c in halves:
                    last = pe.matmul(o, l_lo, r_hi[:, c], start=False, stop=stop, skip_group_check=True)
                return last

            def piece():
                pe.wait_ge(lo_ready, pos("piece", 1))
                return pos.n.get("piece", 0) % RING

            def done(last):
                last.then_inc(piece_used, 1)
                pos.add("piece")

            def wait_h(k):
                pe.wait_ge(h_lo, pos("h", k + 1))

            def tok(k, t):
                return (slice(None), k, slice(t * P, (t + 1) * P))

            def free_fill():
                if pos.i is not None or pos.n.get("fill", 0) >= 2:
                    pe.wait_ge(g_free, pos("fill", -1))

            def chunk(hi, lo, kts=tuple(range(KD)), banks=None, waits=True):
                if banks is None:
                    free_fill()
                    b = pos.n.get("fill", 0) % 2
                    banks = (2 * b, 2 * b + 1)
                    pos.add("fill")
                for j in range(len(kts) // 2):
                    slot = piece()
                    for jj in range(2):
                        k = kts[2 * j + jj]
                        if waits:
                            wait_h(k)
                        for t in range(NT):
                            c = slice(jj * 512, (jj + 1) * 512)
                            last = three(ps[:, banks[t], :], hi[tok(k, t)], lo[tok(k, t)], w_hi[:, slot, c],
                                         w_lo[:, slot, c], k == kts[0], k == kts[-1])
                    done(last)

            def chunk_t(hi, lo):
                free_fill()
                b = pos.n["fill"] % 2
                pos.add("fill")
                for j in range(KD // 2):
                    slot = piece()
                    for jj in range(2):
                        k = 2 * j + jj
                        wait_h(k)
                        for m in range(4):
                            c = slice(jj * 512 + m * P, jj * 512 + (m + 1) * P)
                            o = ps[:, 2 * b + m // 2, (m % 2) * T:(m % 2 + 1) * T]
                            start = k == 0 and m % 2 == 0
                            pe.matmul(o, w_hi[:, slot, c], hi[:, k, :], start=start, stop=False, skip_group_check=True)
                            pe.matmul(o, w_hi[:, slot, c], lo[:, k, :], start=False, stop=False, skip_group_check=True)
                            last = pe.matmul(o, w_lo[:, slot, c], hi[:, k, :], start=False, stop=k == KD - 1,
                                             skip_group_check=True)
                    done(last)

            def norm_t(parts=1, version=None):
                src = xn if version is None else x_tok
                for j in range(4):
                    for kk in range(2):
                        for t in range(NT):
                            if version is not None and j == 0 and kk == 0:
                                pe.wait_ge(x_ready, version - 1 + t)
                            elif version is None and j % (4 // parts) == 0 and kk == 0:
                                pe.wait_ge(xn_ready, pos("xn", NT * (j * parts // 4) + t + 1))
                            k = 2 * j + kk
                            last = pe.transpose(ps[:, 4 + j, kk * T + t * P:kk * T + (t + 1) * P],
                                                src[:, t, k * P:(k + 1) * P], ident)
                    last.then_inc(t_done, 1)
                if version is None:
                    pos.add("xn", NT * parts)

            def gu(j):
                if j == 0:
                    free_fill()
                b = pos.n["fill"] % 2
                slot = piece()
                for jj in range(2):
                    k = 2 * j + jj
                    for t in range(NT):
                        c = slice(jj * 512, (jj + 1) * 512)
                        last = three(ps[:, 2 * b + t, :], x_hi[tok(k, t)], x_lo[tok(k, t)], w_hi[:, slot, c],
                                     w_lo[:, slot, c], k == 0, k == KD - 1)
                done(last)
                if j == 3:
                    pos.add("fill")

            def unit_t(b):
                pe.wait_ge(act_ready, pos("act", 2))
                pos.add("act", 2)
                for j in range(2):
                    for t in range(NT):
                        last = pe.transpose(ps[:, 2 * b, j * T + t * P:j * T + (t + 1) * P],
                                            a_tok[:, t, j * P:(j + 1) * P], ident)
                last.then_inc(act_t, 1)

            def last_down():
                slots = []
                for j in range(2):
                    slots.append(piece())
                    pos.add("piece")
                pe.wait_ge(g_free, pos("fill"))
                for t in range(NT):
                    for j in range(2):
                        last = two_threes((ps[:, 4 + 2 * t, :], ps[:, 5 + 2 * t, :]), a_hi[tok(j, t)],
                                          a_lo[tok(j, t)], w_hi[:, slots[j], :], w_lo[:, slots[j], :], j == 1)
                        if t == 0 and j == 1:
                            last.then_inc(sums_done, 1)
                        if t == 1:
                            last.then_inc(piece_used, 1)

            def down(fills):
                for j in range(2):
                    slot = piece()
                    pe.wait_ge(g_free, pos("fill", -fills))
                    for t in range(NT):
                        last = two_threes((ps[:, 4 + 2 * t, :], ps[:, 5 + 2 * t, :]), a_hi[tok(j, t)],
                                          a_lo[tok(j, t)], w_hi[:, slot, :], w_lo[:, slot, :])
                    done(last)

            def unit_step():
                for j in range(3):
                    gu(j)
                unit_t((pos.n["fill"] - 1) % 2)
                gu(3)
                down(1)

            def units(before, loops, scored=False):
                for k in range(KD):
                    wait_h(k)
                for j in range(4):
                    gu(j)
                if scored:
                    pe.wait_ge(r_sig, 1)
                for b in range(4):
                    pe.matmul(ps[:, 4 + b, :], zero[:, :], x_hi[:, 0:2, :].rearrange("p k t -> p (k t)"),
                              start=True, stop=False, skip_group_check=True)
                for _ in range(before):
                    unit_step()
                with pos.loop(pe, loops, UNITS_PER | {"h": 0, "xn": 0}):
                    for _ in range(2):
                        unit_step()
                for _ in range(2):
                    unit_step()
                unit_t((pos.n["fill"] - 1) % 2)
                last_down()

            pe.wait_ge(in_first, 48)
            pe.wait_ge(zero_ready, 2)
            pm0 = pool_m[:, 0:4 * T].rearrange("p (w t) -> p w t", w=4)
            pm1 = pool_m[:, 4 * T:].rearrange("p (w t) -> p w t", w=4)
            pe.wait_ge(xn_ready, 2)
            for j in range(4):
                for kk in range(2):
                    k = 2 * j + kk
                    o = ps[:, 4 + j, kk * T:(kk + 1) * T]
                    pe.matmul(o, xn[:, 0, k * P:(k + 1) * P], pm0[:, j, :], start=True, stop=False)
                    last = pe.matmul(ps[:, 4 + j, kk * T + P:(kk + 1) * T], xn[:, 1, k * P:(k + 1) * P],
                                     pm1[:, j, :], start=False, stop=True)
                last.then_inc(t_done, 1)
            pos.add("xn", 2)
            for j in range(2):
                slot = piece()
                for g in range(2):
                    grp = 2 * j + g
                    for kk in range(2):
                        wait_h(2 * grp + kk)
                        for t in range(NT):
                            c = slice(g * 512 + kk * 256, g * 512 + (kk + 1) * 256)
                            last = three(ps[:, 2 * t + j, g * 256:(g + 1) * 256], x_hi[tok(2 * grp + kk, t)],
                                         x_lo[tok(2 * grp + kk, t)], w_hi[:, slot, c], w_lo[:, slot, c],
                                         kk == 0, kk == 1)
                done(last)
            pos.add("h", 8)
            pos.n["fill"] = 0
            pe.wait_ge(in_second, 64)
            pe.matmul(ps[0:HEADS, 4, 0:384], rb[:, :], oneh[:, :], start=True, stop=True).then_inc(bias_mm, 1)
            pe.wait_ge(bias_rows, 1)
            norm_t(version=XR_POOL)
            units(2, 3)
            pos.add("h", 8)
            norm_t()
            for _ in range(2):
                chunk_t(h2_hi, h2_lo)
            for _ in range(2):
                chunk(h2_hi, h2_lo)
            pos.add("h", 8)
            for _ in range(2):
                chunk_t(x_hi, x_lo)
            pos.add("h", 8)
            pe.wait_ge(g_free, pos("fill"))

            pe.wait_ge(q_zero, 2)

            def scores(b):
                if b >= 2:
                    pe.wait_ge(pt0_ready, b - 1)
                    pe.wait_ge(pt1_ready, b - 1)
                base = 3 * (b % 2)
                for i in range(4):
                    h = 4 * b + i
                    q = (q_even, q_odd)[h % 2]
                    pe.matmul(ps[:, base, i * P:(i + 1) * P], q[:, h // 2, 0:P], kT[:, h // 2, 0:P],
                              start=True, stop=True)
                    last = pe.matmul(ps[:, base + 1 + i // 2, (i % 2) * T:(i % 2 + 1) * T], q[:, h // 2, P:T],
                                     kT[:, h // 2, :], start=True, stop=True)
                last.then_inc(s_done, 1)

            def transpose_probs(b):
                base = 3 * (b % 2)
                p0, p1 = probs(b)
                pe.wait_ge(p_ready, b + 1)
                for i in range(4):
                    o = base + 1 + i // 2
                    c = (i % 2) * T
                    pe.transpose(ps[:, o, c:c + P], p0[:, i, :], ident)
                    pe.transpose(ps[:, o, c + P:c + T], p1[:, i, 0:P], ident)
                    last = pe.transpose(ps[:, base, i * P:(i + 1) * P], p1[:, i, P:T], ident)
                last.then_inc(pt_done, 1)

            def attend(b):
                pe.wait_ge(pt0_ready, b + 1)
                pe.wait_ge(pt1_ready, b + 1)
                if b:
                    pe.wait_ge(o_lo, b)
                for i in range(4):
                    h = 4 * b + i
                    rows_ = slice(DH * (h % 2), DH * (h % 2) + DH)
                    c = (i // 2) * T
                    pe.matmul(ps[rows_, 6, c:c + T], v_tok[:, 0, h * DH:(h + 1) * DH], pt0[:, i, :],
                              start=True, stop=False)
                    last = pe.matmul(ps[rows_, 6, c + P:c + T], v_tok[:, 1, h * DH:(h + 1) * DH],
                                     pt1[:, i, :], start=False, stop=True)
                last.then_inc(pv_done, 1)

            def modulation(c):
                if c:
                    pe.wait_ge(ada_copied, c)
                for k in range(KD):
                    if k % 2 == 0:
                        slot = piece()
                    cols = slice((k % 2) * 512, (k % 2 + 1) * 512)
                    pe.matmul(ps[0:4, 7, :], ad[:, k, :], w_hi[:, slot, cols], start=k == 0, stop=False)
                    last = pe.matmul(ps[0:4, 7, :], ad[:, k, :], w_lo[:, slot, cols], start=False, stop=k == KD - 1)
                    if k % 2:
                        done(last)

            scores(0)
            scores(1)
            pe.wait_ge(ad_ready, 1)
            for b in range(4):
                modulation(3 * b)
                transpose_probs(b)
                modulation(3 * b + 1)
                attend(b)
                modulation(3 * b + 2)
                if b < 2:
                    scores(b + 2)
            pe.wait_ge(ada_copied, ADA_CHUNKS)
            for m in MOD_TILES:
                last = pe.transpose(ps[:, 7, 4 * m:4 * m + 4], ada_out[:, m * P:(m + 1) * P], ident[0:4, 0:4])
            last.then_inc(mod_mm, 1)
            for g, first in enumerate((2 * D, 5 * D)):
                for c in range(2):
                    last = pe.matmul(ps[:, 2 * g + c, :], const("sel_lat", 4),
                                     ada_out[:, first + c * 512:first + (c + 1) * 512], start=True, stop=True)
            last.then_inc(gate_mm, 1)
            pe.wait_ge(mod_ready, 1)
            pe.wait_ge(o_lo, 4)
            for c in range(2):
                chunk(x_hi, x_lo, banks=(4 + c, 6 + c), waits=False)
            norm_t(version=XR_WO)
            pe.wait_ge(gate_ready, 1)
            units(0, 4)
            pos.add("h", 8)
            pe.wait_ge(x_ready, XR_FFN1)
            norm_t()
            for _ in range(3):
                chunk(x_hi, x_lo)
            pos.add("h", 8)
            norm_t()
            for _ in range(2):
                chunk(x_hi, x_lo)
            pe.wait_ge(log_ready, 2)
            for d, near in enumerate(("after", "before")):
                for t in range(NT):
                    o = ps[:, 4 + 2 * d + t, :]
                    outer = t == d
                    last = pe.matmul(o, const(near), zf_c[:, d, t, :], start=True, stop=not outer)
                    if outer:
                        last = pe.matmul(o, const("ones"), zf_c[:, d, 1 - t, :], start=False, stop=True)
                last.then_inc(cx_r, 1)
            chunk(x_hi, x_lo)

            def flip(bank, src):
                for t in range(NT):
                    last = pe.matmul(ps[:, bank + 1 - t, :], const("flip"), src(t), start=True, stop=True)
                last.then_inc(flip_mm, 1)

            pe.wait_ge(cx_k, 4)
            for d in range(2):
                for h in range(GLA_HEADS):
                    c = slice(h * P, (h + 1) * P)
                    for t in range(NT):
                        last = pe.matmul(ps[:, 4 + d, c], kc(d, t)[:, c], zv_c[:, t, c], start=t == 0, stop=t == 1)
                last.then_inc(cx_s, 1)
            pe.wait_ge(g_free, pos("fill", -1))
            flip(6, lambda t: xn[:, t, 0:512])
            chunk(x_hi, x_lo)
            pe.wait_ge(silu_g, 1)
            pe.wait_ge(flip_ready, 1)
            flip(6, lambda t: zq[:, 0, t, :])
            pe.wait_ge(g_free, pos("fill"))
            pe.wait_ge(cx_ready, 2)
            flip(4, lambda t: zv[:, 0, t, :])
            for g in range(4):
                d, a = g // 2, g % 2
                if g:
                    pe.wait_ge(sc_end, g)
                pe.wait_ge(log_ready, 3 + d)
                pe.wait_ge(k_ready, 3 + d)
                for h in range(GLA_HEADS):
                    if h >= 2:
                        pe.wait_ge(sc_x, 9 * g + 2 * (h - 1))
                    pe.matmul(ps[:, 2 + h % 2, :], zf[:, d, a, h * P:(h + 1) * P], const("levels"), start=True,
                              stop=True).then_inc(sc_e, 1)
                if g == 0:
                    pe.wait_ge(flip_ready, 3)
                for h in range(GLA_HEADS):
                    last = pe.matmul(ps[:, 6, h * P:(h + 1) * P], zf[:, d, a, h * P:(h + 1) * P], const("prefix"),
                                     start=True, stop=True)
                last.then_inc(sc_e, 1)
                for h in range(GLA_HEADS):
                    c = slice(h * P, (h + 1) * P)
                    pe.transpose(ps[:, 0, c], zq[:, d, a, c], ident)
                    last = pe.transpose(ps[:, 1, c], zk[:, d, a, c], ident)
                last.then_inc(sc_t, 1)
                if g:
                    pe.wait_ge(side_free, g)
                chunk(x_hi, x_lo, banks=(4, 5))
                if a == 0:
                    pe.wait_ge(sc_x, 9 * (g + 1))
                    pe.matmul(ps[:, 2, :], const("after"), zf[:, d, 0, :], start=True, stop=True).then_inc(sc_r, 1)
                pe.wait_ge(sc_m, 9 * (g + 1))
                for h in range(GLA_HEADS):
                    c0 = h * P
                    last = pe.matmul(ps[:, 7, c0:c0 + P], ki[:, h, :], ex[:, 0, h, :], start=True, stop=True,
                                     skip_group_check=True)
                    for lev, half in enumerate((CHUNK, 2 * CHUNK, 4 * CHUNK), 1):
                        for s in range(0, P, 2 * half):
                            last = pe.matmul(ps[s:s + half, 7, c0 + s + half:c0 + s + 2 * half],
                                             ex[:, lev, h, s:s + half], ex[:, lev, h, s + half:s + 2 * half],
                                             start=True, stop=True, skip_group_check=True)
                last.then_inc(sc_at, 1)
                if a == 0:
                    pe.wait_ge(sc_kk, d + 1)
                    for h in range(GLA_HEADS):
                        c = slice(h * P, (h + 1) * P)
                        last = pe.matmul(ps[:, 3, c], kh[:, c], zv[:, d, 0, c], start=True, stop=True)
                    last.then_inc(sc_u, 1)
                pe.wait_ge(sc_ats, g + 1)
                for h in range(GLA_HEADS):
                    c = slice(h * P, (h + 1) * P)
                    pe.matmul(ps[:, 0, c], ats[:, h, :], zv[:, d, a, c], start=True, stop=False)
                    state = s0[:, d, c] if a == 0 else s1[:, h, :]
                    last = pe.matmul(ps[:, 0, c], qp[:, h, :], state, start=False, stop=True)
                last.then_inc(sc_o, 1)
            pe.wait_ge(sc_end, 4)
            for t in range(NT):
                last = pe.matmul(ps[:, 2 + 1 - t, :], const("flip"), o_dir[:, 1, t, :], start=True, stop=True)
            last.then_inc(sc_flip, 1)
            pe.wait_ge(sc_sum, 2)
            chunk(x_hi, x_lo)
            pe.wait_ge(in_merge, 48)
            pe.wait_ge(m_v, 1)
            for t in range(NT):
                for g in range(GLA_HEADS):
                    c = slice(g * P, (g + 1) * P)
                    last = pe.matmul(ps[:, 6 + t, c], wst[:, g, :], vl[:, t, c], start=True, stop=True)
            last.then_inc(m_z, 1)
            pe.wait_ge(m_a, 1)
            pe.wait_ge(side_free, 4)
            for t in range(NT):
                for h in range(GLA_HEADS):
                    last = pe.transpose(ps[:, 4 + h // 2, (h % 2) * T + t * P:(h % 2) * T + (t + 1) * P],
                                        o_dir[:, 0, t, h * P:(h + 1) * P], ident)
            last.then_inc(m_at, 1)
            chunk(x_hi, x_lo)
            pe.wait_ge(m_b, 1)
            pe.wait_ge(m_alo, 1)
            for t in range(NT):
                for h in range(GLA_HEADS):
                    last = pe.transpose(ps[:, 4 + h // 2, (h % 2) * T + t * P:(h % 2) * T + (t + 1) * P],
                                        u_tok[:, t, h * P:(h + 1) * P], ident)
            last.then_inc(m_bt, 1)
            chunk(x_hi, x_lo)
            pos.add("h", 8)
            pe.wait_ge(m_blo, 1)
            for c in range(2):
                chunk(g_hi, g_lo, (0, 1, 2, 3), (4 + 2 * c, 5 + 2 * c), waits=False)
                if c == 0:
                    pe.wait_ge(g_free, pos("fill"))
                chunk(g_hi, g_lo, (4, 5, 6, 7), (c, 2 + c), waits=False)
            norm_t(2)
            for k in range(KD):
                wait_h(k)
            for c in range(2):
                chunk(x_hi, x_lo, banks=(4 + c, 6 + c), waits=False)
            pos.add("h", 8)
            norm_t()
            pe.wait_ge(r_w, 1)
            for k in range(KD):
                wait_h(k)
            for t in range(NT):
                for k in range(KD):
                    pe.matmul(ps[:, 6 + t, 0:2 * EXPERTS], x_hi[tok(k, t)],
                              wr2[:, k, :, :].rearrange("p a e -> p (a e)"), start=k == 0, stop=False,
                              skip_group_check=True)
                    last = pe.matmul(ps[:, 6 + t, 0:EXPERTS], x_lo[tok(k, t)], wr2[:, k, 0, :], start=False,
                                     stop=k == KD - 1, skip_group_check=True)
            last.then_inc(r_mm, 1)
            units(0, EXPERTS // 2 - 1, scored=True)

        @block.scalar
        def _(act):
            pos = Pos()

            def step(ins):
                ins.then_inc(act_step, 1)
                pos.add("step")
                act.wait_ge(act_step, pos("step"))

            def prep(k):
                for _ in range(k):
                    n = pos.n.get("piece", 0)
                    if n % 2 == 0:
                        at = n // 2 % (RAW // 2)
                        times = n // RAW
                        full = 16 * (times + 1)
                        if pos.i is not None:
                            full = full + pos.i * 16
                        act.wait_ge(loaded[at], full)
                    if pos.i is not None or n >= RING:
                        act.wait_ge(piece_used, pos("piece", 1 - RING))
                    nc.scalar.activation(w_hi[:, n % RING, :], raw[:, n % RAW, :], ACT.Copy).then_inc(hi_ready, 1)
                    pos.add("piece")

            def ahead(hold=0):
                prep(min(pos.n.get("pe", 0) + RING, N_PIECES) - hold - pos.n.get("piece", 0))

            def load_sqrt():
                step(nc.scalar.activation(warm[:, :], eps[:, :], ACT.Sqrt))

            def root(parts, version=None):
                load_sqrt()
                for t in range(NT):
                    if version is not None:
                        act.wait_ge(x_ready, version - 1 + t)
                    step(nc.scalar.activation(xn[:, t, :], parts[t], ACT.Square, accum_out=ss[:, t:t + 1]))
                nc.scalar.activation(rms[:, :], ss[:, :], ACT.Sqrt, scale=1.0 / D, bias=eps[:, :]).then_inc(
                    rms_ready, 1)

            def root_sums(sums=None):
                load_sqrt()
                for t in range(NT):
                    if t == 0 and sums is not None:
                        act.wait_ge(sums_done, sums)
                    else:
                        act.wait_ge(piece_used, pos("pe"))
                    nc.scalar.activation(squares[:, :], ps[:, 4 + 2 * t:6 + 2 * t, :].rearrange("p a b -> p (a b)"),
                                         ACT.Square, accum_out=ss[:, t:t + 1]).then_inc(y_squared, 1)
                    pos.add("y")
                    act.wait_ge(y_squared, pos("y"))
                nc.scalar.activation(rms[:, :], ss[:, :], ACT.Sqrt, scale=1.0 / D, bias=eps[:, :]).then_inc(
                    rms_ready, 1)

            def norm_hi(targets):
                for n, (dst, gain, shift) in enumerate(targets):
                    for j in range(4):
                        if n == 0:
                            act.wait_ge(t_done, pos("t_done", j + 1))
                        else:
                            act.wait_ge(h_lo, pos("h", -8 + 2 * j + 2))
                        for k in (2 * j, 2 * j + 1):
                            src = ps[:, 4 + j, (k % 2) * T:(k % 2 + 1) * T]
                            if gain is None:
                                ins = nc.scalar.activation(dst[:, k, :], src, ACT.Copy)
                            elif shift is None:
                                ins = nc.scalar.activation(dst[:, k, :], src, ACT.Copy, scale=gain[:, k:k + 1])
                            else:
                                ins = nc.scalar.activation(dst[:, k, :], src, ACT.Identity, scale=gain[:, k:k + 1],
                                                           bias=shift[:, k:k + 1])
                            ins.then_inc(h_hi, 1)
                    pos.add("h", 8)
                pos.add("t_done", 4)

            def unit_silu(b, routed, early=0):
                act.wait_ge(piece_used, pos("pe", -early))
                if pos.i is not None or pos.n.get("act", 0) > 0:
                    act.wait_ge(act_ready, pos("act"))
                for t in range(NT):
                    if routed:
                        ins = nc.scalar.activation(sg[:, t, :], ps[:, 2 * b + t, 0:HID], ACT.Silu)
                    else:
                        ins = nc.scalar.activation(sg[:, t, :], ps[:, 2 * b + t, 0:HID], ACT.Silu,
                                                   scale=rstd[:, t:t + 1])
                    ins.then_inc(silu_ready, 1)
                pos.add("act", 2)

            def unit_hi(b):
                act.wait_ge(act_t, pos("t", 1))
                pos.add("t")
                nc.scalar.activation(a_hi[:, :, :], ps[:, 2 * b, :].rearrange("p (j t) -> p j t", j=2),
                                     ACT.Copy).then_inc(act_hi, 1)

            def unit_step(routed, last=False):
                b = pos.n.get("fill", 0) % 2
                prep(2)
                unit_silu(b, routed)
                prep(3)
                unit_hi(b)
                pos.add("fill")
                pos.add("pe", 6)
                if last:
                    unit_silu(1 - b, routed, 2)
                prep(1)

            def units(before, loops, routed=False):
                if not routed:
                    act.wait_ge(rstd_ready, pos("rstd", 1))
                    pos.add("rstd")
                pos.add("pe", 4)
                for _ in range(before):
                    unit_step(routed)
                with pos.loop(act, loops, UNITS_PER):
                    for _ in range(2):
                        unit_step(routed)
                unit_step(routed)
                unit_step(routed, True)
                prep(2)
                unit_hi(pos.n["fill"] % 2)
                pos.add("fill")
                pos.add("pe", 2)

            def gates(zf, d, z):
                act.wait_ge(g_free, Z0 + z)
                step(nc.scalar.activation(zk[:, d, :, :], zf[:, d, :, :], ACT.Sigmoid, scale=-1.0))
                nc.scalar.activation(zf[:, d, :, :], zf[:, d, :, :], ACT.Sigmoid).then_inc(sig_ready, 1)

            def log(zf, d, n):
                act.wait_ge(f_ready, n)
                nc.scalar.activation(zf[:, d, :, :], zf[:, d, :, :], ACT.Ln).then_inc(log_ready, 1)

            act.wait_ge(in_x, 16)
            act.wait_ge(zero_ready, 2)
            root([x_tok[:, t, :] for t in range(NT)])
            ahead()
            act.wait_ge(in_first, 48)
            norm_hi([(x_hi, vec("norm_mixer0"), None)])
            pos.add("pe", 2)
            ahead()
            norm_hi([(x_hi, vec("norm_ffn0"), None)])
            root([x_tok[:, t, :] for t in range(NT)], XR_POOL)
            nc.scalar.activation(csil[:, :, :].rearrange("p k c -> p (k c)"), vec("c"), ACT.Silu).then_inc(c_silu, 1)
            units(2, 3)
            root([x_tok[:, t, :] for t in range(NT)], XR_FFN0)
            ahead()
            norm_hi([(h2_hi, vec("kv_norm"), None), (x_hi, vec("norm_mixer1"), None)])

            def after_chunks(k):
                for _ in range(k):
                    pos.add("pe", 4)
                    ahead()

            after_chunks(6)

            def exps(b):
                p0, p1 = probs(b)
                act.wait_ge(p_raw, 2 * b + 2)
                for n, pr in enumerate((p0, p1)):
                    for i in range(4):
                        c = 4 * n + i
                        nc.scalar.activation(pr[:, i, :], pr[:, i, :], ACT.Exp, bias=mx[:, b % 2, c:c + 1],
                                             accum_out=rs[:, b % 2, c:c + 1]).then_inc(p_exp, 1)

            exps(0)
            for b in range(4):
                after_chunks(1)
                act.wait_ge(pt_done, b + 1)
                if b:
                    act.wait_ge(pv_done, b)
                base = 3 * (b % 2)
                nc.scalar.activation(pt0[:, :, :], ps[:, base + 1:base + 3, :].rearrange("p a (h q) -> p (a h) q", h=2),
                                     ACT.Copy).then_inc(pt0_ready, 1)
                after_chunks(1)
                if b < 3:
                    exps(b + 1)
                act.wait_ge(pv_done, b + 1)
                nc.scalar.activation(x_hi[:, 2 * b:2 * b + 2, :],
                                     ps[:, 6, :].rearrange("p (k t) -> p k t", k=2), ACT.Copy).then_inc(o_hi, 1)
                after_chunks(1)
            after_chunks(2)
            norm_hi([(x_hi, vec("norm_ffn1"), None)])
            root([x_tok[:, t, :] for t in range(NT)], XR_WO)
            units(0, 4)
            act.wait_ge(in_ctx, 16)
            root([ctx_tok[:, t, :] for t in range(NT)])
            ahead()
            norm_hi([(x_hi, gains[:, 1, :], mod[:, :, 1])])
            act.wait_ge(h_lo, pos("h"))
            root([x_tok[:, t, :] for t in range(NT)], XR_FFN1)
            act.wait_ge(lb_diff, 1)
            nc.scalar.activation(lb[:, :, :], lbr[:, :, 0, :], ACT.Sigmoid).then_inc(lb_ready, 1)
            after_chunks(1)
            root([x_tok[:, t, :] for t in range(NT)], XR_FIN)
            after_chunks(2)
            norm_hi([(x_hi, gains[:, 0, :], mod[:, :, 0])])
            gates(zf_c, 0, 2)
            gates(zf_c, 1, 2)
            after_chunks(1)
            log(zf_c, 0, 1)
            log(zf_c, 1, 2)
            act.wait_ge(g_free, Z0 + 4)
            nc.scalar.activation(zq[:, 0, :, :], zq[:, 0, :, :], ACT.Silu).then_inc(silu_g, 1)
            after_chunks(1)
            for d in range(2):
                act.wait_ge(cx_r, d + 1)
                for t in range(NT):
                    nc.scalar.activation(kc(d, t), ps[:, 4 + 2 * d + t, :], ACT.Exp).then_inc(cx_exp, 1)
            after_chunks(1)
            gates(zf, 0, 6)
            act.wait_ge(flip_ready, 1)
            step(nc.scalar.activation(zk[:, 1, :, :], zf[:, 1, :, :], ACT.Sigmoid, scale=-1.0))
            nc.scalar.activation(zf[:, 1, :, :], zf[:, 1, :, :], ACT.Sigmoid).then_inc(sig_ready, 1)
            log(zf, 0, 3)
            log(zf, 1, 4)
            after_chunks(1)
            for g in range(4):
                d, a = g // 2, g % 2
                if g:
                    act.wait_ge(sc_end, g)
                for h in range(GLA_HEADS):
                    act.wait_ge(sc_e, 5 * g + h + 1)
                    nc.scalar.activation(ex[:, :, h, :], ps[:, 2 + h % 2, :].rearrange("p (l t) -> p l t", l=4),
                                         ACT.Exp).then_inc(sc_x, 1)
                    nc.scalar.activation(ki[:, h, :], ps[:, 2 + h % 2, 0:P], ACT.Exp, scale=-1.0).then_inc(sc_x, 1)
                act.wait_ge(sc_e, 5 * g + 5)
                nc.scalar.activation(qp[:, :, :], ps[:, 6, :].rearrange("p (h t) -> p h t", h=4),
                                     ACT.Exp).then_inc(sc_x, 1)
                after_chunks(1)
                if a == 0:
                    act.wait_ge(sc_r, d + 1)
                    nc.scalar.activation(kh[:, :], ps[:, 2, :], ACT.Exp).then_inc(sc_kh, 1)
                dst, fn, ready = ((vl, ACT.Gelu_apprx_tanh, gelu_r), (u_tok, ACT.Gelu_apprx_tanh, gelu_r),
                                  (sgl, ACT.Silu, silu_g), (ga0, ACT.Sigmoid, gate_r))[g]
                act.wait_ge(side_free, g + 1)
                nc.scalar.activation(dst[:, :, :], dst[:, :, :], fn).then_inc(ready, 1)
                if g == 2:
                    act.wait_ge(m_ms, 1)
                    nc.scalar.activation(rms[:, :], ss[:, :], ACT.Sqrt, scale=1.0 / CM, bias=eps[:, :]
                                         ).then_inc(m_rms, 1)
            def function(c, dst):
                act.wait_ge(g_free, Z0 + 8 + c)
                nc.scalar.activation(dst[:, :, :], dst[:, :, :], ACT.Sigmoid).then_inc(gate_r, 1)

            act.wait_ge(m_ms, 2)
            nc.scalar.activation(st8b[:, :], st8[:, :], ACT.Sqrt, scale=1.0 / P, bias=eps[:, :]).then_inc(m_rms, 1)
            after_chunks(1)
            function(0, ga1)
            act.wait_ge(m_at, 1)
            ga_, _ = FEAT["g_hgrn"]
            nc.scalar.activation(g_hi[:, 0:4, :], ps[:, 4:6, :].rearrange("p a (h t) -> p (a h) t", h=2), ACT.Copy,
                                 scale=ft[:, ga_:ga_ + 1]).then_inc(m_ahi, 1)
            after_chunks(1)
            function(1, gb0)
            act.wait_ge(m_bt, 1)
            nc.scalar.activation(g_hi[:, 4:8, :], ps[:, 4:6, :].rearrange("p a (h t) -> p (a h) t", h=2),
                                 ACT.Copy).then_inc(m_bhi, 1)
            after_chunks(1)
            function(2, gb1)
            for _ in range(4):
                pos.add("pe", 2)
                ahead()
            norm_hi([(x_hi, None, None)])
            after_chunks(1)
            pos.add("pe", 4)
            ahead(1)
            root_sums()
            root([x_tok[:, t, :] for t in range(NT)], XR_MIX)
            ahead()
            norm_hi([(x_hi, gains[:, 2, :], mod[:, 24:, 0])])
            act.wait_ge(r_sum, 1)
            nc.scalar.activation(sc[:, :, :], sc[:, :, :], ACT.Sigmoid).then_inc(r_sig, 1)
            units(0, EXPERTS // 2 - 1, routed=True)
            root_sums(3)

        @block.vector
        def _(dve):
            pos = Pos()

            def step(ins):
                ins.then_inc(dve_step, 1)
                pos.add("step")
                dve.wait_ge(dve_step, pos("step"))

            def prep(k):
                for _ in range(k):
                    n = pos.n.get("piece", 0)
                    dve.wait_ge(hi_ready, pos("piece", 1))
                    nc.vector.tensor_tensor(w_lo[:, n % RING, :], raw[:, n % RAW, :],
                                            w_hi[:, n % RING, :].bitcast(f32), ALU.subtract).then_inc(lo_ready, 1)
                    pos.add("piece")

            def ahead(hold=0):
                prep(min(pos.n.get("pe", 0) + RING, N_PIECES) - hold - pos.n.get("piece", 0))

            def inverse():
                dve.wait_ge(rms_ready, pos("rms", 1))
                pos.add("rms")
                step(nc.vector.reciprocal(rstd[:, :], rms[:, :]))

            def inverse_shared():
                dve.wait_ge(rms_ready, pos("rms", 1))
                pos.add("rms")
                nc.vector.reciprocal(rstd[:, :], rms[:, :]).then_inc(rstd_ready, 1)
                pos.add("rstd")
                dve.wait_ge(rstd_ready, pos("rstd"))

            def norm_x(src):
                inverse()
                for t in range(NT):
                    nc.vector.tensor_scalar(xn[:, t, :], src[:, t, :], rstd[:, t:t + 1], None,
                                            ALU.mult).then_inc(xn_ready, 1)

            def norm_lo(targets):
                for dst_hi, dst, gain, shift in targets:
                    for k in range(KD):
                        dve.wait_ge(h_hi, pos("h", 2 * (k // 2) + 2))
                        src = ps[:, 4 + k // 2, (k % 2) * T:(k % 2 + 1) * T]
                        high = dst_hi[:, k, :].bitcast(f32)
                        if gain is None:
                            ins = nc.vector.tensor_tensor(dst[:, k, :], src, high, ALU.subtract)
                        elif shift is None:
                            ins = nc.vector.scalar_tensor_tensor(dst[:, k, :], src, gain[:, k:k + 1], high, ALU.mult,
                                                                 ALU.subtract)
                        else:
                            nc.vector.tensor_scalar(whole(k), src, gain[:, k:k + 1],
                                                    shift[:, k:k + 1], ALU.mult, ALU.add).then_inc(h_full, 1)
                            continue
                        ins.then_inc(h_lo, 1)
                    pos.add("h", 8)

            def wide(t):
                return ps[:, 4 + 2 * t:6 + 2 * t, :].rearrange("p a b -> p (a b)")

            def add_residual(sums=None):
                for t in range(NT):
                    if t == 0 and sums is not None:
                        dve.wait_ge(sums_done, sums)
                    else:
                        dve.wait_ge(piece_used, pos("pe"))
                    nc.vector.tensor_tensor(x_tok[:, t, :], x_tok[:, t, :], wide(t), ALU.add).then_inc(x_ready, 1)

            def unit_act(b, weight):
                for t in range(NT):
                    dve.wait_ge(silu_ready, pos("act", t + 1))
                    up = ps[:, 2 * b + t, HID:2 * HID]
                    factor = rstd[:, t:t + 1] if weight is None else comb[:, t, weight]
                    nc.vector.scalar_tensor_tensor(a_tok[:, t, :], sg[:, t, :], factor, up, ALU.mult,
                                                   ALU.mult).then_inc(act_ready, 1)
                pos.add("act", 2)

            def unit_lo(b):
                dve.wait_ge(act_hi, pos("t", 1))
                pos.add("t")
                nc.vector.tensor_tensor(a_lo[:, :, :], ps[:, 2 * b, :].rearrange("p (j t) -> p j t", j=2),
                                        a_hi[:, :, :].bitcast(f32), ALU.subtract).then_inc(g_free, 1)

            def unit_step(weight, last=None):
                b = pos.n.get("fill", 0) % 2
                prep(2)
                unit_act(b, weight)
                prep(3)
                unit_lo(b)
                pos.add("fill")
                pos.add("pe", 6)
                if last is not None:
                    unit_act(1 - b, *last)
                prep(1)

            def units(before, loops, routed=False):
                def weight(e):
                    return slice(e, e + 1) if routed else None

                pos.add("pe", 4)
                for _ in range(before):
                    unit_step(None)
                with pos.loop(dve, loops, UNITS_PER) as i:
                    for e in range(2):
                        unit_step(bass.ds(i * 2 + e, 1) if routed else None)
                unit_step(weight(2 * loops))
                unit_step(weight(2 * loops + 1), (weight(2 * loops + 2),))
                prep(2)
                unit_lo(pos.n["fill"] % 2)
                pos.add("fill")
                pos.add("pe", 2)

            def copy_queries(c):
                b = pos.n["fill"] % 2
                pos.add("fill")
                dve.wait_ge(piece_used, pos("pe"))
                k = slice(4 * c, 4 * c + 4)
                for r, dst in ((slice(0, DH), q_even), (slice(DH, P), q_odd)):
                    ins = nc.vector.tensor_copy(dst[r, k, :], ps[r, 2 * b:2 * b + 2, :].rearrange(
                        "p a (k t) -> p (a k) t", k=2))
                    if r.start:
                        ins.then_inc(g_free, 1)
                    else:
                        step(ins)

            def copy_fill(dst, transposed=False):
                b = pos.n["fill"] % 2
                pos.add("fill")
                dve.wait_ge(piece_used, pos("pe"))
                src = ps[:, 2 * b:2 * b + 2, :]
                if transposed:
                    src = src.rearrange("p a (k t) -> p (a k) t", k=2)
                nc.vector.tensor_copy(dst, src).then_inc(g_free, 1)

            dve.wait_ge(in_x, 16)
            norm_x(x_tok)
            ahead()
            dve.wait_ge(in_first, 48)
            norm_lo([(x_hi, x_lo, vec("norm_mixer0"), None)])
            pos.add("pe", 2)
            ahead()
            dve.wait_ge(in_second, 64)
            dve.wait_ge(piece_used, pos("pe"))
            for t in range(NT):
                step(nc.vector.tensor_tensor(xn[:, t, :], ps[:, 2 * t:2 * t + 2, :].rearrange("p a b -> p (a b)"),
                                             pool_s[:, :], ALU.mult))
                nc.vector.tensor_tensor(x_tok[:, t, :], x_tok[:, t, :], xn[:, t, :], ALU.add).then_inc(x_ready, 1)
            dve.wait_ge(bias_mm, 1)
            step(nc.vector.tensor_copy(rv[:, :], ps[0:HEADS, 4, 0:384]))
            nc.vector.memset(rv[:, 256:384], -BIG).then_inc(bias_rows, 1)
            norm_lo([(x_hi, x_lo, vec("norm_ffn0"), None)])
            inverse_shared()
            dve.wait_ge(c_silu, 1)
            step(nc.vector.tensor_copy(ad[:, :, 0:2], csil[:, :, :]))
            nc.vector.tensor_tensor(ad[:, :, 2:4], csil[:, :, :], ad[:, :, 0:2].bitcast(f32),
                                    ALU.subtract).then_inc(ad_ready, 1)
            units(2, 3)
            add_residual(1)
            norm_x(x_tok)
            ahead()
            norm_lo([(h2_hi, h2_lo, vec("kv_norm"), None), (x_hi, x_lo, vec("norm_mixer1"), None)])
            dve.wait_ge(bias_in, 16)
            for dst, transposed in ((kT[:, 0:4, :], True), (kT[:, 4:8, :], True), (v_tok[:, :, 0:512], False),
                                    (v_tok[:, :, 512:], False)):
                pos.add("pe", 4)
                ahead(1)
                copy_fill(dst, transposed=transposed)
                ahead()
            for c in range(2):
                pos.add("pe", 4)
                ahead(1)
                copy_queries(c)
                ahead()

            def raw_scores(b):
                p0, p1 = probs(b)
                base = 3 * (b % 2)
                dve.wait_ge(s_done, b + 1)
                if b >= 2:
                    dve.wait_ge(pt_done, b - 1)
                for n, (pr, src, rel) in enumerate((
                        (p0, ps[:, base, :].rearrange("p (h k) -> p h k", h=4), bias[:, 4 * b:4 * b + 4, P:T]),
                        (p1, ps[:, base + 1:base + 3, :].rearrange("p a (h k) -> p (a h) k", h=2),
                         bias[:, 4 * b:4 * b + 4, :]))):
                    step(nc.vector.scalar_tensor_tensor(pr, src, DH ** -0.5, rel, ALU.mult, ALU.add))
                    nc.vector.reduce_max(mx[:, b % 2, 4 * n:4 * n + 4], pr, AXX, negate=True).then_inc(p_raw, 1)

            def copy_modulation(c):
                pos.add("pe", 4)
                ahead(1)
                dve.wait_ge(piece_used, pos("pe"))
                nc.vector.tensor_copy(ada_out[:, c * 512:(c + 1) * 512], ps[0:4, 7, :]).then_inc(ada_copied, 1)
                ahead()

            raw_scores(0)
            for b in range(4):
                p0, p1 = probs(b)
                dve.wait_ge(p_exp, 8 * (b + 1))
                step(nc.vector.reciprocal(rr[:, :], rs[:, b % 2, :]))
                step(nc.vector.tensor_tensor(p0, p0, rr[:, 0:4].unsqueeze(2).to_broadcast([P, 4, P]), ALU.mult))
                nc.vector.tensor_tensor(p1, p1, rr[:, 4:8].unsqueeze(2).to_broadcast([P, 4, T]),
                                        ALU.mult).then_inc(p_ready, 1)
                copy_modulation(3 * b)
                dve.wait_ge(pt_done, b + 1)
                if b:
                    dve.wait_ge(pv_done, b)
                nc.vector.tensor_copy(pt1[:, :, :], ps[:, 3 * (b % 2), :].rearrange("p (h q) -> p h q", h=4)
                                      ).then_inc(pt1_ready, 1)
                if b < 3:
                    raw_scores(b + 1)
                copy_modulation(3 * b + 1)
                dve.wait_ge(o_hi, b + 1)
                nc.vector.tensor_tensor(x_lo[:, 2 * b:2 * b + 2, :],
                                        ps[:, 6, :].rearrange("p (k t) -> p k t", k=2),
                                        x_hi[:, 2 * b:2 * b + 2, :].bitcast(f32), ALU.subtract).then_inc(o_lo, 1)
                copy_modulation(3 * b + 2)
            dve.wait_ge(mod_mm, 1)
            a, b_ = FEAT["b_ada"]
            for m in (slice(0, 16), slice(24, 40)):
                parts = ps[:, 7, 4 * m.start:4 * m.stop].rearrange("p (m c) -> p m c", c=4)
                shape = [P, m.stop - m.start, 2]
                step(nc.vector.tensor_tensor(mod[:, m, :], parts[:, :, 0:2],
                                             ft[:, a + m.start:a + m.stop].unsqueeze(2).to_broadcast(shape), ALU.add))
                step(nc.vector.tensor_tensor(mod[:, m, :], mod[:, m, :], parts[:, :, 2:4], ALU.add))
            for n, (g, m, c) in enumerate((("g_pre_mix", 8, 0), ("g_pre_mix", 8, 1), ("g_pre_ffn", 32, 0))):
                ins = nc.vector.scalar_tensor_tensor(gains[:, n, :], mod[:, m:m + 8, c], 1.0, vec(g), ALU.add, ALU.mult)
                if n < 2:
                    step(ins)
                else:
                    ins.then_inc(mod_ready, 1)
            pos.add("pe", 4)
            ahead()
            dve.wait_ge(gate_mm, 1)
            step(nc.vector.tensor_copy(gt1[:, :], ps[:, 0:2, :].rearrange("p a b -> p (a b)")))
            nc.vector.tensor_copy(gt2[:, :], ps[:, 2:4, :].rearrange("p a b -> p (a b)")).then_inc(gate_ready, 1)
            pos.add("pe", 4)
            ahead(1)
            add_residual()
            ahead()
            norm_lo([(x_hi, x_lo, vec("norm_ffn1"), None)])
            inverse_shared()
            units(0, 4)
            norm_x(ctx_tok)
            ahead()
            add_residual(2)
            norm_lo([(x_hi, x_lo, gains[:, 1, :], mod[:, :, 1])])
            inverse()
            dve.wait_ge(in_fin, 16)
            for t in range(NT):
                nc.vector.scalar_tensor_tensor(x_tok[:, t, :], x_tok[:, t, :], rstd[:, t:t + 1], fin_g[:, :],
                                               ALU.mult, ALU.mult).then_inc(x_ready, 1)

            def take(dst):
                pos.add("pe", 4)
                ahead(1)
                b = pos.n["fill"] % 2
                pos.add("fill")
                dve.wait_ge(piece_used, pos("pe"))
                nc.vector.tensor_copy(dst, ps[:, 2 * b:2 * b + 2, :]).then_inc(g_free, 1)
                ahead()

            def forget(zf, d, n):
                dve.wait_ge(sig_ready, n)
                for t in range(NT):
                    nc_ = nc.vector.tensor_tensor(zk[:, d, t, :], zk[:, d, t, :], oml[:, d, :], ALU.mult)
                    if t == 0:
                        step(nc_)
                    else:
                        nc_.then_inc(k_ready, 1)
                    step(nc.vector.tensor_tensor(zf[:, d, t, :], zf[:, d, t, :], oml[:, d, :], ALU.mult))
                    f = nc.vector.tensor_tensor(zf[:, d, t, :], zf[:, d, t, :], lb[:, d, :], ALU.add)
                    if t == 0:
                        step(f)
                    else:
                        f.then_inc(f_ready, 1)

            take(zf_c[:, 0, :, :])
            norm_x(x_tok)
            take(zf_c[:, 1, :, :])
            dve.wait_ge(lb_ready, 1)
            step(nc.vector.tensor_scalar(oml[:, :, :], lb[:, :, :], -1.0, 1.0, ALU.mult, ALU.add))
            take(zv_c[:, :, :])
            norm_lo([(x_hi, x_lo, gains[:, 0, :], mod[:, :, 0])])
            forget(zf_c, 0, 1)
            dve.wait_ge(gates_done, 2)
            take(zq[:, 0, :, :])
            forget(zf_c, 1, 2)
            take(xn[:, :, 0:512])
            for d in range(2):
                for t in range(NT):
                    dve.wait_ge(cx_exp, 2 * d + t + 1)
                    nc.vector.tensor_tensor(kc(d, t), kc(d, t), zk[:, d, t, :], ALU.mult).then_inc(cx_k, 1)
            take(zf[:, 0, :, :])
            for d in range(2):
                dve.wait_ge(cx_s, d + 1)
                nc.vector.tensor_copy(s0[:, d, :], ps[:, 4 + d, :]).then_inc(cx_ready, 1)

            def take_flipped(r, dst, bank):
                dve.wait_ge(flip_mm, r + 1)
                nc.vector.tensor_copy(dst[:, 1, :, :], ps[:, bank:bank + 2, :]).then_inc(flip_ready, 1)

            take_flipped(0, zf, 6)
            forget(zf, 0, 3)
            forget(zf, 1, 4)
            take(zv[:, 0, :, :])
            take_flipped(1, zq, 6)
            take_flipped(2, zv, 4)
            dve.wait_ge(ats_zero, 1)
            for g in range(4):
                d, a = g // 2, g % 2
                dve.wait_ge(sc_t, g + 1)
                dve.wait_ge(sc_x, 9 * (g + 1))
                if a == 0:
                    step(nc.vector.tensor_copy(dt[:, :, :], qp[:, :, P - 1:P]))
                qt = ps[:, 0, :].rearrange("p (h t) -> p h t", h=4)
                kt = ps[:, 1, :].rearrange("p (h t) -> p h t", h=4)
                for dst, src in ((ex[:, 0, :, :], qt), (ki[:, :, :], kt), (qp[:, :, :], qt)):
                    nc.vector.tensor_tensor(dst, dst, src, ALU.mult).then_inc(sc_m, 1)
                for lev, half in enumerate((CHUNK, 2 * CHUNK, 4 * CHUNK), 1):
                    for side, src in ((1, qt), (0, kt)):
                        dst = ex[:, lev, :, :].rearrange("p h (b s u) -> p h b s u", s=2, u=half)[:, :, :, side, :]
                        part = src.rearrange("p h (b s u) -> p h b s u", s=2, u=half)[:, :, :, side, :]
                        nc.vector.tensor_tensor(dst, dst, part, ALU.mult).then_inc(sc_m, 1)
                pos.add("pe", 4)
                ahead(1)
                dve.wait_ge(piece_used, pos("pe"))
                nc.vector.tensor_copy((vl, u_tok, sgl, ga0)[g][:, :, :], ps[:, 4:6, :]).then_inc(side_free, 1)
                ahead()
                dve.wait_ge(sc_at, g + 1)
                nc.vector.copy_predicated(ats[:, :, :], causal[:, :, :],
                                          ps[:, 7, :].rearrange("p (h t) -> p h t", h=4)).then_inc(sc_ats, 1)
                if a == 0:
                    dve.wait_ge(sc_kh, d + 1)
                    nc.vector.tensor_tensor(kh[:, :], kh[:, :], zk[:, d, 0, :], ALU.mult).then_inc(sc_kk, 1)
                    dve.wait_ge(sc_u, d + 1)
                    for h in range(GLA_HEADS):
                        c = slice(h * P, (h + 1) * P)
                        step(nc.vector.scalar_tensor_tensor(s1[:, h, :], s0[:, d, c], dt[:, h, :], ps[:, 3, c],
                                                            ALU.mult, ALU.add))
                dve.wait_ge(sc_o, g + 1)
                nc.vector.tensor_copy(o_dir[:, d, a, :], ps[:, 0, :]).then_inc(sc_end, 1)
                if g == 1:
                    dve.wait_ge(gelu_r, 1)
                    step(nc.vector.reduce_sum(mean[:, :], vl[:, :, :], AXX))
                    step(nc.vector.tensor_scalar(mean[:, :], mean[:, :], -1.0 / CM, None, ALU.mult))
                    for t in range(NT):
                        step(nc.vector.tensor_scalar(vl[:, t, :], vl[:, t, :], mean[:, t:t + 1], None, ALU.add))
                    step(nc.vector.tensor_tensor(sq[:, :, :], vl[:, :, :], vl[:, :, :], ALU.mult))
                    nc.vector.reduce_sum(ss[:, :], sq[:, :, :], AXX).then_inc(m_ms, 1)
                if g == 2:
                    dve.wait_ge(in_merge, 48)
                    dve.wait_ge(m_rms, 1)
                    step(nc.vector.reciprocal(rstd[:, :], rms[:, :]))
                    for t in range(NT):
                        step(nc.vector.scalar_tensor_tensor(vl[:, t, :], vl[:, t, :], rstd[:, t:t + 1], ln_g[:, :],
                                                            ALU.mult, ALU.mult))
                        ins = nc.vector.tensor_tensor(vl[:, t, :], vl[:, t, :], ln_b[:, :], ALU.add)
                        if t == 0:
                            step(ins)
                        else:
                            ins.then_inc(m_v, 1)
            dve.wait_ge(sc_flip, 1)
            for t in range(NT):
                nc.vector.tensor_tensor(o_dir[:, 0, t, :], o_dir[:, 0, t, :], ps[:, 2 + t, :],
                                        ALU.add).then_inc(sc_sum, 1)
            o = o_dir[:, 0, :, :]
            o8 = o.rearrange("p t (h n) -> p (t h) n", h=GLA_HEADS)
            sq8 = sq[:, :, :].rearrange("p t (h n) -> p (t h) n", h=GLA_HEADS)
            dve.wait_ge(sc_sum, 2)
            step(nc.vector.tensor_tensor(sq[:, :, :], o, o, ALU.mult))
            nc.vector.reduce_sum(st8[:, :], sq8, AXX).then_inc(m_ms, 1)
            dve.wait_ge(m_rms, 2)
            step(nc.vector.reciprocal(st8b[:, :], st8b[:, :]))
            step(nc.vector.tensor_tensor(o8, o8, st8b[:, :].unsqueeze(2).to_broadcast([P, 8, P]), ALU.mult))
            dve.wait_ge(silu_g, 2)
            nc.vector.tensor_tensor(o, o, sgl[:, :, :], ALU.mult).then_inc(m_a, 1)
            take(ga1[:, :, :])
            gh, _ = FEAT["g_hgrn"]
            dve.wait_ge(m_ahi, 1)
            nc.vector.scalar_tensor_tensor(g_lo[:, 0:4, :], ps[:, 4:6, :].rearrange("p a (h t) -> p (a h) t", h=2),
                                           ft[:, gh:gh + 1], g_hi[:, 0:4, :].bitcast(f32), ALU.mult,
                                           ALU.subtract).then_inc(m_alo, 1)
            dve.wait_ge(m_z, 1)
            dve.wait_ge(gelu_r, 2)
            bs, _ = FEAT["b_spatial"]
            for t in range(NT):
                for g in range(GLA_HEADS):
                    c = slice(g * P, (g + 1) * P)
                    ins = nc.vector.scalar_tensor_tensor(u_tok[:, t, c], ps[:, 6 + t, c], ft[:, bs + g:bs + g + 1],
                                                         u_tok[:, t, c], ALU.add, ALU.mult)
                    if t == 1 and g == 3:
                        ins.then_inc(m_b, 1)
                    else:
                        step(ins)
            take(gb0[:, :, :])
            dve.wait_ge(m_bhi, 1)
            nc.vector.tensor_tensor(g_lo[:, 4:8, :], ps[:, 4:6, :].rearrange("p a (h t) -> p (a h) t", h=2),
                                    g_hi[:, 4:8, :].bitcast(f32), ALU.subtract).then_inc(m_blo, 1)
            take(gb1[:, :, :])
            for c in range(2):
                for _ in range(2):
                    pos.add("pe", 2)
                    ahead()
                dve.wait_ge(gate_r, 3 + c)
                dve.wait_ge(piece_used, pos("pe"))
                cols = slice(c * 512, (c + 1) * 512)
                ga, gb = ((ga0, gb0), (ga1, gb1))[c]
                for t in range(NT):
                    for bank, gate in ((4 + 2 * c + t, ga), (c + 2 * t, gb)):
                        step(nc.vector.tensor_tensor(gate[:, t, :], gate[:, t, :], ps[:, bank, :], ALU.mult))
                    nc.vector.tensor_tensor(xn[:, t, cols], ga[:, t, :], gb[:, t, :], ALU.add).then_inc(xn_ready, 1)
            norm_lo([(x_hi, x_lo, None, None)])
            pos.add("pe", 4)
            ahead()
            pos.add("pe", 4)
            ahead(1)

            def gated_residual(gate, ready):
                for t in range(NT):
                    dve.wait_ge(y_squared, pos("y", 1))
                    pos.add("y")
                    ins = nc.vector.tensor_tensor(xn[:, t, :], wide(t), gate[:, :], ALU.mult)
                    if t == 0:
                        step(ins)
                    else:
                        ins.then_inc(dve_step, 1)
                        pos.add("step")
                inverse()
                for t in range(NT):
                    nc.vector.scalar_tensor_tensor(x_tok[:, t, :], xn[:, t, :], rstd[:, t:t + 1], x_tok[:, t, :],
                                                   ALU.mult, ALU.add).then_inc(ready, 1)

            gated_residual(gt1, x_ready)
            norm_x(x_tok)
            ahead()
            dve.wait_ge(in_router, 32)
            step(nc.vector.tensor_copy(wr2[:, :, 0, :], wr[:, :, :]))
            nc.vector.tensor_tensor(wr2[:, :, 1, :], wr[:, :, :], wr2[:, :, 0, :].bitcast(f32), ALU.subtract
                                    ).then_inc(r_w, 1)
            norm_lo([(x_hi, x_lo, gains[:, 2, :], mod[:, 24:, 0])])
            dve.wait_ge(r_mm, 1)
            step(nc.vector.tensor_copy(t64[:, :, :], ps[:, 6:8, EXPERTS:2 * EXPERTS]))
            nc.vector.tensor_tensor(sc[:, :, :], t64[:, :, :], ps[:, 6:8, 0:EXPERTS], ALU.add).then_inc(r_sum, 1)
            dve.wait_ge(r_sig, 1)
            step(nc.vector.tensor_tensor(sel[:, :, :], sc[:, :, :], br[:, :].unsqueeze(1).to_broadcast([P, NT, EXPERTS]),
                                         ALU.add))
            for t in range(NT):
                for g in range(GROUPS):
                    step(nc.vector.max(best[:, t, g, :], sel[:, t, g * 8:(g + 1) * 8]))
            step(nc.vector.tensor_tensor(gsc[:, :, :], best[:, :, :, 0], best[:, :, :, 1], ALU.add))
            for t in range(NT):
                step(nc.vector.max(gm8[:, t, :], gsc[:, t, :]))
            step(nc.vector.memset(gm8[:, :, 4:8], BIG))
            for t in range(NT):
                step(nc.vector.match_replace(gkeep[:, t, :], gm8[:, t, :], gsc[:, t, :], BIG))
            step(nc.vector.tensor_scalar(gkeep2[:, :, :], gkeep[:, :, :], BIG, None, ALU.is_ge))
            step(nc.vector.tensor_scalar(gkeep2[:, :, :], gkeep2[:, :, :], BIG, -BIG, ALU.mult, ALU.add))
            step(nc.vector.tensor_tensor(
                sel[:, :, :].rearrange("p t (g e) -> p (t g) e", g=GROUPS),
                sel[:, :, :].rearrange("p t (g e) -> p (t g) e", g=GROUPS),
                gkeep2[:, :, :].rearrange("p t g -> p (t g)").unsqueeze(2).to_broadcast([P, NT * GROUPS, 8]), ALU.add))
            for t in range(NT):
                step(nc.vector.max(gm8[:, t, :], sel[:, t, :]))
                step(nc.vector.match_replace(t64[:, t, :], gm8[:, t, :], sel[:, t, :], BIG))
            step(nc.vector.tensor_scalar(t64[:, :, :], t64[:, :, :], BIG, None, ALU.is_ge))
            step(nc.vector.tensor_tensor(t64[:, :, :], t64[:, :, :], sc[:, :, :], ALU.mult))
            step(nc.vector.reduce_sum(wsum[:, :], t64[:, :, :], AXX))
            step(nc.vector.reciprocal(wsum[:, :], wsum[:, :]))
            for t in range(NT):
                step(nc.vector.tensor_scalar(comb[:, t, 0:EXPERTS], t64[:, t, :], wsum[:, t:t + 1], ROUTED_SCALE,
                                             ALU.mult, ALU.mult))
            step(nc.vector.memset(comb[:, :, EXPERTS:], 1.0))
            units(0, EXPERTS // 2 - 1, routed=True)
            gated_residual(gt2, res_ready)


def kernel(**inputs):
    import concourse.bacc as _bacc
    from concourse.bass_utils import run_bass_kernel_spmd as _run

    nc, arrays, _ = assemble(_bacc, inputs)
    r = _run(nc, [arrays], core_ids=[0])
    return r.results[0]["out_dram"].reshape(1, T, D)


def stream_of(a):
    pieces = []

    def cols(w, c0, width=512):
        k = w.shape[0] // P
        part = w[:, c0:c0 + width].reshape(k // 2, 2, P, width)
        pieces.extend(part.transpose(0, 2, 1, 3).reshape(k // 2, P, 2 * width))

    def unit_gu(w, c_gate, c_up):
        part = np.stack([w[:, c_gate:c_gate + HID], w[:, c_up:c_up + HID]], 1).reshape(KD // 2, 2, P, 2 * HID)
        pieces.extend(part.transpose(0, 2, 1, 3).reshape(KD // 2, P, 4 * HID))

    def unit_down(w, r0):
        pieces.extend(w[r0:r0 + HID].reshape(2, P, D))

    def units(gus, downs):
        unit_gu(*gus[0])
        for g, d in zip(gus[1:] + [None], downs):
            if g is not None:
                unit_gu(*g)
            unit_down(*d)

    def ffn(layer):
        gu, down = a["w_gate_up"][layer], a["w_down"][layer]
        units([(gu, u * HID, D_FF + u * HID) for u in range(FFN_UNITS)], [(down, u * HID) for u in range(FFN_UNITS)])

    pw = a["pool_w"][0].reshape(2, 2, 2, P, 256)
    pieces.extend(pw.transpose(0, 3, 1, 2, 4).reshape(2, P, 1024))
    ffn(0)
    for c in range(4):
        cols(a["w_kv"], c * 512)
    for c in range(2):
        cols(a["w_q"][0], c * 512)
    for c in range(ADA_CHUNKS):
        cols(a["w_ada_2"][0], c * 512)
    for c in range(2):
        cols(a["w_o"][0], c * 512)
    ffn(1)
    w_in = a["w_in_2"][0]
    for c in (1, 2, 3):
        cols(w_in, c * 512)
    for c in (0, 2, 1, 3, 6, 5, 4, 7, 8, 9, 10):
        cols(w_in, c * 512)
    for c in range(2):
        cols(a["w_branch_a_2"][0], c * 512)
        cols(a["w_branch_b_2"][0], c * 512)
    for c in range(2):
        cols(a["w_out_2"][0], c * 512)
    egu, edn = a["w_expert_gu_2"][0], a["w_expert_down_2"][0]
    units([(egu[e], 0, HID) for e in range(EXPERTS)] + [(a["w_shared_gu_2"][0], 0, HID)],
          [(edn[e], 0) for e in range(EXPERTS)] + [(a["w_shared_down_2"][0], 0)])
    out = np.empty((len(pieces) // 2, P, 2, PIECE), np.float32)
    for n, p in enumerate(pieces):
        out[n // 2, :, n % 2, :] = p
    return out.reshape(len(pieces) // 2, P, 2 * PIECE)


def layouts(a):
    consts, pool, causal, buckets = constants()
    feat = np.zeros((P, NFEAT), np.float32)

    def vec(name, v):
        lo, hi = FEAT[name]
        feat[:, lo:hi] = v.reshape(hi - lo, P).T

    vec("norm_mixer0", a["norm_mixer"][0])
    vec("norm_mixer1", a["norm_mixer"][1])
    vec("norm_ffn0", a["norm_ffn"][0])
    vec("norm_ffn1", a["norm_ffn"][1])
    vec("kv_norm", a["kv_norm"])
    vec("g_pre_mix", a["g_pre_mix_2"][0])
    vec("g_pre_ffn", a["g_pre_ffn_2"][0])
    vec("g_hgrn", a["g_hgrn_out_2"][0])
    vec("b_ada", a["b_ada_2"][0])
    lo, hi = FEAT["b_spatial"]
    feat[:, lo:hi] = a["b_spatial_2"][0]
    lo, hi = FEAT["c"]
    feat[:, lo:hi] = np.stack([a["c_2"][0].reshape(KD, P).T, a["c_ctx_2"].reshape(KD, P).T], 2).reshape(P, 2 * KD)
    rows = np.zeros((1, NROWS), np.float32)
    for name, v in (("pool_scale", a["pool_scale"]), ("final_norm", a["final_norm"]),
                    ("gt1_b", a["b_ada_2"][0, 2 * D:3 * D]), ("gt2_b", a["b_ada_2"][0, 5 * D:]),
                    ("g_post_mix", a["g_post_mix_2"]), ("g_post_ffn", a["g_post_ffn_2"]), ("ln_g", a["cm_ln_g_2"]),
                    ("ln_b", a["cm_ln_b_2"]), ("lb", a["lb_logits_2"]), ("b_router", a["b_router_2"])):
        lo, hi = ROWS[name]
        rows[0, lo:hi] = v.reshape(-1)
    return {
        "stream": stream_of(a), "x": a["x"][0], "ctx": a["ctx_2"][0], "feat": feat, "rows": rows, "consts": consts,
        "pool_c": pool, "causal_c": causal, "buckets_c": buckets, "rel_bias": a["rel_bias"],
        "w_router": a["w_router_2"][0].reshape(KD, P, EXPERTS).transpose(1, 0, 2).reshape(P, KD * EXPERTS),
        "w_spatial": a["w_spatial_2"][0].transpose(2, 0, 1).reshape(P, GLA_HEADS * P),
    }


def assemble(bacc, inputs):
    nc = bacc.Bacc("TRN2", target_bir_lowering=False, num_devices=1)
    arrays, args = {}, {}
    for name, v in layouts({k: np.asarray(v) for k, v in inputs.items()}).items():
        v = np.ascontiguousarray(v)
        arrays[name + "_dram"] = v
        args[name] = nc.dram_tensor(name + "_dram", v.shape, mybir.dt.from_np(v.dtype), kind="ExternalInput").ap()
    args["out"] = nc.dram_tensor("out_dram", (T, D), mybir.dt.float32, kind="ExternalOutput").ap()
    program(nc, **args)
    return nc, arrays, args
```

```python
import math
from contextlib import ExitStack, contextmanager

import numpy as np

import concourse.bass as bass
from concourse import mybir

P = 128
T = 256
NT = T // P
D = 1024
KD = D // P
D_FF = 2816
HID = 256
FFN_UNITS = D_FF // HID
EXPERTS = 64
MOE_UNITS = EXPERTS + 1
GROUPS = 8
HEADS = 16
DH = 64
BUCKETS = 32
MAX_DISTANCE = 128
SPAN = T + P
WINDOWS = (2, 4, 8, 16)
GLA_HEADS = 4
CHUNK = 16
CM = 512
ADA_CHUNKS = 12
EPS = 1e-6
BIG = 1e30
ROUTED_SCALE = 2.5

PIECE = 1024
RAW = 12
RING = 4

FEAT = {}
_at = 0
for _name, _n in (("norm_mixer0", 8), ("norm_mixer1", 8), ("norm_ffn0", 8), ("norm_ffn1", 8), ("kv_norm", 8),
                  ("g_pre_mix", 8), ("g_pre_ffn", 8), ("g_hgrn", 1), ("b_ada", 48), ("b_spatial", 4), ("c", 16)):
    FEAT[_name] = (_at, _at + _n)
    _at += _n
NFEAT = _at
ROWS = {}
_at = 0
for _name, _n in (("pool_scale", 1024), ("final_norm", 1024), ("gt1_b", 1024), ("gt2_b", 1024), ("g_post_mix", 1024),
                  ("g_post_ffn", 1024), ("ln_g", 512), ("ln_b", 512), ("lb", 2048), ("b_router", 64)):
    ROWS[_name] = (_at, _at + _n)
    _at += _n
NROWS = _at
CONST = {}
_at = 0
for _name, _n in (("ident", 128), ("flip", 128), ("prefix", 128), ("after", 128), ("before", 128), ("ones", 128),
                  ("levels", 512), ("sel_lat", 128)):
    CONST[_name] = (_at, _at + _n)
    _at += _n
NCONST = _at


def constants():
    u, t = np.arange(P)[:, None], np.arange(P)[None, :]
    c = np.zeros((P, NCONST), np.float32)

    def put(name, value):
        a, b = CONST[name]
        c[:value.shape[0], a:b] = value

    put("ident", (u == t).astype(np.float32))
    put("flip", (u == P - 1 - t).astype(np.float32))
    put("prefix", (u <= t).astype(np.float32))
    put("after", (u > t).astype(np.float32))
    put("before", (u < t).astype(np.float32))
    put("ones", np.ones((P, P), np.float32))
    mid = t // CHUNK * CHUNK + CHUNK // 2 - 1
    inner = ((u > mid) & (u <= t)).astype(np.float32) - ((u > t) & (u <= mid)).astype(np.float32)
    levels = [inner]
    for half in (CHUNK, 2 * CHUNK, 4 * CHUNK):
        m = t // (2 * half) * 2 * half + half
        levels.append(np.where(t < m, (u > t) & (u < m), (u >= m) & (u <= t)).astype(np.float32))
    put("levels", np.concatenate(levels, axis=1))
    r = np.arange(4)[:, None]
    put("sel_lat", np.repeat((r % 2 == 0).astype(np.float32), P, axis=1))
    s, q = np.arange(T)[:, None], np.arange(T)[None, :]
    pools = []
    for w in WINDOWS:
        cnt = np.minimum(q + 1, w)
        pools.append(((s <= q) & (s > q - w)) / cnt.astype(np.float32) - (s == q))
    pool = np.stack(pools, 1).astype(np.float32)
    pool = np.concatenate([pool[:P].reshape(P, 4 * T), pool[P:, :, P:].reshape(P, 4 * P)], axis=1)
    causal = np.repeat((u <= t).astype(np.int32)[:, None, :], GLA_HEADS, axis=1).reshape(P, GLA_HEADS * P)
    n = T - 1 - np.arange(SPAN)
    exact = BUCKETS // 2
    far = np.maximum(n, exact).astype(np.float32)
    large = exact + (np.log(far / exact) / math.log(MAX_DISTANCE / exact) * (BUCKETS - exact)).astype(np.int32)
    bucket = np.where(n < exact, n, np.minimum(large, BUCKETS - 1))
    buckets = ((np.arange(BUCKETS)[:, None] == bucket[None, :]) & (n >= 0)[None, :]).astype(np.float32)
    return c, pool, causal, buckets


class Pos:

    def __init__(self):
        self.n, self.i, self.per = {}, None, {}

    def __call__(self, name, extra=0):
        v = self.n.get(name, 0) + extra
        return v if self.i is None else v + self.i * self.per.get(name, 0)

    def add(self, name, k=1):
        self.n[name] = self.n.get(name, 0) + k

    @contextmanager
    def loop(self, eng, times, per):
        start = dict(self.n)
        with eng.Fori(0, times) as i:
            self.i, self.per = i, per
            yield i
            self.i = None
        for name, v in self.n.items():
            d = v - start.get(name, 0)
            assert d == per.get(name, 0), (name, d)
            self.n[name] = v + d * (times - 1)


def program(nc, stream, x, ctx, feat, rows, consts, pool_c, causal_c, buckets_c, rel_bias, w_router, w_spatial, out):
    f32, f32r, i32 = mybir.dt.float32, mybir.dt.float32r, mybir.dt.int32
    ALU, ACT = mybir.AluOpType, mybir.ActivationFunctionType
    AXX = mybir.AxisListType.X
    es = ExitStack()
    with es:
        size = 207 * 1024
        es.enter_context(nc.sbuf_tensor("slab", [P, size // 4], f32))
        slab_at = nc.sbuf_base - size

        def place(start, *wanted):
            made = []
            for name, shape, *dt in wanted:
                n = 4 * int(np.prod(shape[1:]))
                assert start + n <= size, (name, start, n)
                made.append(nc.alloc_sbuf_tensor_at(name, shape, dt[0] if dt else f32, offset=slab_at + start))
                start += (n + 31) // 32 * 32
            return (*made, start)

        raw, w_hi, w_lo, x_tok, x_hi, x_lo, xn_at = place(
            0, ("raw", [P, RAW, PIECE]), ("w_hi", [P, RING, PIECE], f32r), ("w_lo", [P, RING, PIECE], f32r),
            ("x_tok", [P, NT, D]), ("x_hi", [P, KD, T], f32r), ("x_lo", [P, KD, T], f32r))
        (xn, cst, causal, ft, eps, zero, ss, rms, rstd, mod, gains, csil, ad, warm, phase) = place(
            xn_at, ("xn", [P, NT, D]), ("cst", [P, NCONST]), ("causal", [P, GLA_HEADS, P], i32), ("ft", [P, NFEAT]), ("eps", [P, 1]),
            ("zero", [P, P], f32r), ("ss", [P, 2]), ("rms", [P, 2]), ("rstd", [P, 2]), ("mod", [P, 48, 2]),
            ("gains", [P, 3, KD]), ("csil", [P, KD, 2]), ("ad", [P, KD, 4], f32r),
            ("warm", [P, 1]))
        a_hi, a_lo, a_tok, sg, unit_end = place(
            phase, ("a_hi", [P, NT, HID], f32r), ("a_lo", [P, NT, HID], f32r), ("a_tok", [P, NT, HID]),
            ("sg", [P, NT, HID]))
        pool_m, pool_s, oneh, rb, rv, _ = place(
            unit_end, ("pool_m", [P, 4 * T + 4 * P]), ("pool_s", [P, D]), ("oneh", [BUCKETS, SPAN]),
            ("rb", [BUCKETS, HEADS]), ("rv", [HEADS, SPAN]))
        q_even, q_odd, kT, v_tok, pt0, pt1, pr_odd, mx, rs, rr, att_end = place(
            phase, ("q_even", [P, KD, T]), ("q_odd", [P, KD, T]), ("kT", [P, KD, T]), ("v_tok", [P, NT, D]),
            ("pt0", [P, 4, T]), ("pt1", [P, 4, P]), ("pr_odd", [P, 12 * P]), ("mx", [P, 2, 8]), ("rs", [P, 2, 8]),
            ("rr", [P, 8]))
        h2_hi, h2_lo, _ = place(att_end, ("h2_hi", [P, KD, T], f32r), ("h2_lo", [P, KD, T], f32r))
        ada_out, end = place(att_end, ("ada_out", [4, 6 * D]))
        bias, _ = place(size - 4 * HEADS * T, ("bias", [P, HEADS, T]))
        assert end <= size - 4 * HEADS * T
        fin_g, _ = place(unit_end, ("fin_g", [P, D]))
        tail = (size - 4 * (2 * 512 + 2 * D + NT * MOE_UNITS) - 64) // 32 * 32
        s0, gt1, gt2, comb, _ = place(
            tail, ("s0", [P, 2, 512]), ("gt1", [P, D]), ("gt2", [P, D]), ("comb", [P, NT, MOE_UNITS]))
        lb, oml, lbend = place(phase, ("lb", [P, 2, 512]), ("oml", [P, 2, 512]))
        zk, zf, zv, zq, ex, ki_at = place(
            lbend, ("zk", [P, 2, NT, 512]), ("zf", [P, 2, NT, 512]), ("zv", [P, 2, NT, 512]),
            ("zq", [P, 2, NT, 512]), ("ex", [P, 4, GLA_HEADS, P]))
        ki, qp, ats, kh, s1, dt, o_dir_at = place(
            ki_at, ("ki", [P, GLA_HEADS, P]), ("qp", [P, GLA_HEADS, P]), ("ats", [P, GLA_HEADS, P]),
            ("kh", [P, 512]), ("s1", [P, GLA_HEADS, P]), ("dt", [P, GLA_HEADS, 1]))
        o_dir, o_dir_end = place(o_dir_at, ("o_dir", [P, 2, NT, 512]))
        zf_c, _ = place(o_dir_at, ("zf_c", [P, 2, NT, 512]))
        zv_c, _ = place(ki_at, ("zv_c", [P, NT, 512]))
        lbr, gate_rows, ctx_tok, end = place(
            unit_end + 4 * D, ("lbr", [P, 2, 2, 512]), ("gate_rows", [P, 4, D]), ("ctx_tok", [P, NT, D]))
        assert end <= tail
        sgl, u_tok, end = place(phase, ("sgl", [P, NT, 512]), ("u_tok", [P, NT, CM]))
        assert end <= lbend
        vl, ga0, _ = place(xn_at, ("vl", [P, NT, CM]), ("ga0", [P, NT, 512]))
        sq, ga1, gb0, gb1, g_hi, g_lo, end = place(
            lbend, ("sq", [P, NT, CM]), ("ga1", [P, NT, 512]), ("gb0", [P, NT, 512]), ("gb1", [P, NT, 512]),
            ("g_hi", [P, KD, T], f32r), ("g_lo", [P, KD, T], f32r))
        assert end <= o_dir_at
        squares, _ = place(o_dir_at, ("squares", [P, D]))
        ln_g, ln_b, wst, st8, st8b, mean, end = place(
            o_dir_end, ("ln_g", [P, CM]), ("ln_b", [P, CM]), ("wst", [P, GLA_HEADS, P]), ("st8", [P, 8]),
            ("st8b", [P, 8]), ("mean", [P, 2]))
        assert end <= tail
        (wr, wr2, br, sc, sel, best, gsc, gm8, gkeep, gkeep2, t64, wsum, _) = place(
            unit_end, ("wr", [P, KD, EXPERTS]), ("wr2", [P, KD, 2, EXPERTS], f32r),
            ("br", [P, EXPERTS]), ("sc", [P, NT, EXPERTS]), ("sel", [P, NT, EXPERTS]), ("best", [P, NT, 8, 8]),
            ("gsc", [P, NT, 8]), ("gm8", [P, NT, 8]), ("gkeep", [P, NT, 8]), ("gkeep2", [P, NT, 8]),
            ("t64", [P, NT, EXPERTS]), ("wsum", [P, NT]))
        ps = es.enter_context(nc.psum_tensor("ps", [P, 8, 512], f32))
        scratch = nc.dram_tensor("bias_scratch", (HEADS, P, SPAN), f32, kind="Internal").ap()

        def const(name, rows_=P):
            a, b = CONST[name]
            return cst[0:rows_, a:b]

        def vec(name):
            a, b = FEAT[name]
            return ft[:, a:b]

        ident = const("ident")

        def whole(k):
            return xn[:, k % 2, (k // 2) * T:(k // 2 + 1) * T]

        def probs(b):
            if b % 2:
                return (pr_odd[:, 0:512].rearrange("p (h k) -> p h k", h=4),
                        pr_odd[:, 512:1536].rearrange("p (h k) -> p h k", h=4))
            return (xn[:, 0, 0:512].rearrange("p (h k) -> p h k", h=4),
                    xn[:, 1, :].rearrange("p (h k) -> p h k", h=4))

        names = set()

        def sem(name):
            assert name not in names
            names.add(name)
            return es.enter_context(nc.semaphore(name))

        loaded = [sem(f"loaded{i}") for i in range(RAW // 2)]
        hi_ready, lo_ready, piece_used = sem("hi_ready"), sem("lo_ready"), sem("piece_used")
        g_free = sem("g_free")
        x_ready, rms_ready, xn_ready = sem("x_ready"), sem("rms_ready"), sem("xn_ready")
        t_done, h_hi, h_lo = sem("t_done"), sem("h_hi"), sem("h_lo")
        silu_ready, act_ready, act_t, act_hi = sem("silu_ready"), sem("act_ready"), sem("act_t"), sem("act_hi")
        dve_step, act_step, pool_step = sem("dve_step"), sem("act_step"), sem("pool_step")
        in_x, in_first, in_second, in_fin, in_gate, in_ctx, in_merge, in_router = (
            sem(f"in_{n}") for n in ("x", "first", "second", "fin", "gate", "ctx", "merge", "router"))
        zero_ready = sem("zero_ready")
        bias_mm, bias_rows, bias_out, bias_in = (sem(f"bias_{n}") for n in ("mm", "rows", "out", "in"))
        q_zero, s_done, p_raw, p_exp, p_ready, pt_done, pt0_ready, pt1_ready, pv_done, o_hi, o_lo = (
            sem(n) for n in ("q_zero", "s_done", "p_raw", "p_exp", "p_ready", "pt_done", "pt0_ready", "pt1_ready",
                             "pv_done", "o_hi", "o_lo"))
        c_silu, ad_ready, ada_copied, mod_mm, mod_ready, gate_mm, gate_ready, gates_done = (
            sem(n) for n in ("c_silu", "ad_ready", "ada_copied", "mod_mm", "mod_ready", "gate_mm", "gate_ready",
                             "gates_done"))
        lb_diff, lb_ready = sem("lb_diff"), sem("lb_ready")
        sig_ready, f_ready, log_ready, k_ready = (
            sem(n) for n in ("sig_ready", "f_ready", "log_ready", "k_ready"))
        flip_mm, flip_ready = sem("flip_mm"), sem("flip_ready")
        ctx_sums, ctx_decays, ctx_keys_ready, ctx_state_mm, ctx_state_ready = (
            sem(f"ctx_{n}") for n in ("sums", "decays", "keys_ready", "state_mm", "state_ready"))
        (decay_sums, scan_transposed, decays_ready, decayed_ready, scan_weights_mm, scan_weights_ready, ats_zero,
         rest_sums, rest_decays, rest_keys_ready, state_mm, scan_out_mm, scan_tile_done, back_mm, scan_sum_ready) = (
            sem(n) for n in ("decay_sums", "scan_transposed", "decays_ready", "decayed_ready", "scan_weights_mm",
                             "scan_weights_ready", "ats_zero", "rest_sums", "rest_decays", "rest_keys_ready",
                             "state_mm", "scan_out_mm", "scan_tile_done", "back_mm", "scan_sum_ready"))
        side_free = sem("side_free")
        silu_g, gelu_r, gate_r = sem("silu_g"), sem("gelu_r"), sem("gate_r")
        (merge_squares, merge_rms, branch_a_ready, branch_a_t, branch_a_hi, branch_a_lo, layer_norm_ready, spatial_mm,
         branch_b_ready, branch_b_t, branch_b_hi, branch_b_lo) = (
            sem(n) for n in ("merge_squares", "merge_rms", "branch_a_ready", "branch_a_t", "branch_a_hi",
                             "branch_a_lo", "layer_norm_ready", "spatial_mm", "branch_b_ready", "branch_b_t",
                             "branch_b_hi", "branch_b_lo"))
        router_split, router_mm, logits_ready, scores_ready = (
            sem(n) for n in ("router_split", "router_mm", "logits_ready", "scores_ready"))
        sums_done = sem("sums_done")
        rstd_ready = sem("rstd_ready")
        y_squared = sem("y_squared")
        h_full = sem("h_full")
        res_ready, stored = sem("res_ready"), sem("stored")

        XR_POOL, XR_FFN0, XR_WO, XR_FFN1, XR_FIN, XR_MIX = 2, 4, 6, 8, 10, 12
        LOADS = stream.shape[0]
        N_PIECES = 2 * LOADS
        MOD_TILES = (*range(16), *range(24, 40))
        Z0 = 2 * FFN_UNITS + 6

        UNITS_PER = {"piece": 12, "pe": 12, "fill": 2, "act": 4, "t": 2}

        def kc(d, t):
            return ex[:, 2 * d + t, :, :].rearrange("p h n -> p (h n)")

        block = es.enter_context(nc.Block())

        @block.sync
        def _(sp):
            def load(l, slot, free_at):
                if free_at is not None:
                    sp.wait_ge(lo_ready, free_at)
                sp.dma_start(raw[:, 2 * slot:2 * slot + 2, :].rearrange("p a b -> p (a b)"),
                             stream[l]).then_inc(loaded[slot], 16)

            sp.dma_start(x_tok[:, :, :], x.rearrange("(t p) d -> p t d", p=P)).then_inc(in_x, 16)
            sp.dma_start(cst[:, :], consts).then_inc(in_first, 16)
            sp.dma_start(ft[:, :], feat).then_inc(in_first, 16)
            sp.dma_start(pool_m[:, :], pool_c).then_inc(in_first, 16)
            half = RAW // 2
            sp.wait_ge(in_x, 16)
            for l in range(2 * half):
                load(l, l % half, None if l < half else 2 * (l - half) + 2)
            whole = (LOADS - 2 * half) // half
            with sp.Fori(0, whole) as i:
                for j in range(half):
                    load(i * half + (2 * half + j), j, i * RAW + (RAW + 2 * j + 2))
            for l in range((2 + whole) * half, LOADS):
                load(l, l % half, 2 * (l - half) + 2)
            for t in range(NT):
                sp.wait_ge(res_ready, t + 1)
                sp.dma_start(out[t * P:(t + 1) * P, :], x_tok[:, t, :]).then_inc(stored, 16)
            sp.wait_ge(stored, 16 * NT)

        @block.gpsimd
        def _(pool):
            def row(dst, name):
                a, b = ROWS[name]
                return pool.dma_start(dst, rows[0:1, a:b].partition_broadcast(P))

            pos = Pos()

            def shifted_lo():
                for k in range(KD):
                    pool.wait_ge(h_full, pos("full", k + 1))
                    nc.gpsimd.tensor_tensor(x_lo[:, k, :], whole(k), x_hi[:, k, :].bitcast(f32), ALU.subtract
                                            ).then_inc(h_lo, 1)
                pos.add("full", KD)

            nc.gpsimd.memset(eps[:, :], EPS).then_inc(zero_ready, 1)
            nc.gpsimd.memset(zero[:, :].bitcast(f32), 0.0).then_inc(zero_ready, 1)
            pool.wait_ge(in_first, 48)
            row(pool_s[:, :], "pool_scale").then_inc(in_second, 16)
            pool.dma_start(oneh[:, :], buckets_c).then_inc(in_second, 16)
            pool.dma_start(rb[:, :], rel_bias).then_inc(in_second, 16)
            pool.dma_start(causal[:, :, :].rearrange("p h k -> p (h k)"), causal_c).then_inc(in_second, 16)
            pool.wait_ge(bias_rows, 1)
            pool.dma_start(scratch, rv[:, :].unsqueeze(1).to_broadcast([HEADS, P, SPAN])).then_inc(bias_out, 16)
            pool.wait_ge(bias_out, 16)
            shifted = bass.AP(tensor=scratch.tensor, offset=scratch.offset + P - 1,
                              ap=[[SPAN - 1, P], [P * SPAN, HEADS], [1, T]])
            pool.dma_start(bias[:, :, :], shifted).then_inc(bias_in, 16)
            pool.wait_ge(x_ready, XR_FFN0)
            nc.gpsimd.memset(q_even[DH:, :, :], 0.0).then_inc(q_zero, 1)
            nc.gpsimd.memset(q_odd[0:DH, :, :], 0.0).then_inc(q_zero, 1)
            pool.wait_ge(x_ready, XR_WO)
            row(fin_g[:, :], "final_norm").then_inc(in_fin, 16)
            pool.dma_start(ctx_tok[:, :, :], ctx.rearrange("(t p) d -> p t d", p=P)).then_inc(in_ctx, 16)
            for k, name in enumerate(("gt1_b", "gt2_b", "g_post_mix", "g_post_ffn")):
                row(gate_rows[:, k, :], name).then_inc(in_gate, 16)
            row(lbr[:, :, :, :].rearrange("p a b c -> p (a b c)"), "lb").then_inc(in_gate, 16)
            row(ln_g[:, :], "ln_g").then_inc(in_merge, 16)
            row(ln_b[:, :], "ln_b").then_inc(in_merge, 16)
            pool.dma_start(wst[:, :, :].rearrange("p g q -> p (g q)"), w_spatial).then_inc(in_merge, 16)
            pool.wait_ge(in_gate, 80)
            nc.gpsimd.tensor_tensor(lbr[:, :, 0, :], lbr[:, :, 0, :], lbr[:, :, 1, :], ALU.subtract).then_inc(lb_diff, 1)
            pool.wait_ge(gate_ready, 1)
            for g, dst in enumerate((gt1, gt2)):
                nc.gpsimd.tensor_tensor(dst[:, :], dst[:, :], gate_rows[:, g, :], ALU.add).then_inc(pool_step, 1)
                pool.wait_ge(pool_step, g + 1)
                nc.gpsimd.tensor_tensor(dst[:, :], dst[:, :], gate_rows[:, 2 + g, :], ALU.mult).then_inc(gates_done, 1)
            shifted_lo()
            shifted_lo()
            pool.wait_ge(ctx_state_ready, 2)
            nc.gpsimd.memset(ats[:, :, :], 0.0).then_inc(ats_zero, 1)
            pool.wait_ge(x_ready, XR_MIX)
            pool.dma_start(wr[:, :, :].rearrange("p k e -> p (k e)"), w_router).then_inc(in_router, 16)
            row(br[:, :], "b_router").then_inc(in_router, 16)
            shifted_lo()

        @block.tensor
        def _(pe):
            pos = Pos()

            def three(o, l_hi, l_lo, r_hi, r_lo, start, stop, shared=False):
                pe.matmul(o, l_hi, r_hi, start=start, stop=False, skip_group_check=shared)
                pe.matmul(o, l_hi, r_lo, start=False, stop=False, skip_group_check=shared)
                return pe.matmul(o, l_lo, r_hi, start=False, stop=stop, skip_group_check=shared)

            def two_threes(outs, l_hi, l_lo, r_hi, r_lo, stop=False):
                halves = [(outs[h], slice(h * 512, (h + 1) * 512)) for h in range(2)]
                for o, c in halves:
                    pe.matmul(o, l_hi, r_hi[:, c], start=False, stop=False, skip_group_check=True)
                    pe.matmul(o, l_hi, r_lo[:, c], start=False, stop=False, skip_group_check=True)
                for o, c in halves:
                    last = pe.matmul(o, l_lo, r_hi[:, c], start=False, stop=stop, skip_group_check=True)
                return last

            def piece():
                pe.wait_ge(lo_ready, pos("piece", 1))
                return pos.n.get("piece", 0) % RING

            def done(last):
                last.then_inc(piece_used, 1)
                pos.add("piece")

            def wait_h(k):
                pe.wait_ge(h_lo, pos("h", k + 1))

            def tok(k, t):
                return (slice(None), k, slice(t * P, (t + 1) * P))

            def free_fill():
                if pos.i is not None or pos.n.get("fill", 0) >= 2:
                    pe.wait_ge(g_free, pos("fill", -1))

            def chunk(hi, lo, kts=tuple(range(KD)), banks=None, waits=True):
                if banks is None:
                    free_fill()
                    b = pos.n.get("fill", 0) % 2
                    banks = (2 * b, 2 * b + 1)
                    pos.add("fill")
                for j in range(len(kts) // 2):
                    slot = piece()
                    for jj in range(2):
                        k = kts[2 * j + jj]
                        if waits:
                            wait_h(k)
                        for t in range(NT):
                            c = slice(jj * 512, (jj + 1) * 512)
                            last = three(ps[:, banks[t], :], hi[tok(k, t)], lo[tok(k, t)], w_hi[:, slot, c],
                                         w_lo[:, slot, c], k == kts[0], k == kts[-1])
                    done(last)

            def chunk_t(hi, lo):
                free_fill()
                b = pos.n["fill"] % 2
                pos.add("fill")
                for j in range(KD // 2):
                    slot = piece()
                    for jj in range(2):
                        k = 2 * j + jj
                        wait_h(k)
                        for m in range(4):
                            c = slice(jj * 512 + m * P, jj * 512 + (m + 1) * P)
                            o = ps[:, 2 * b + m // 2, (m % 2) * T:(m % 2 + 1) * T]
                            start = k == 0 and m % 2 == 0
                            pe.matmul(o, w_hi[:, slot, c], hi[:, k, :], start=start, stop=False, skip_group_check=True)
                            pe.matmul(o, w_hi[:, slot, c], lo[:, k, :], start=False, stop=False, skip_group_check=True)
                            last = pe.matmul(o, w_lo[:, slot, c], hi[:, k, :], start=False, stop=k == KD - 1,
                                             skip_group_check=True)
                    done(last)

            def norm_t(parts=1, version=None):
                src = xn if version is None else x_tok
                for j in range(4):
                    for kk in range(2):
                        for t in range(NT):
                            if version is not None and j == 0 and kk == 0:
                                pe.wait_ge(x_ready, version - 1 + t)
                            elif version is None and j % (4 // parts) == 0 and kk == 0:
                                pe.wait_ge(xn_ready, pos("xn", NT * (j * parts // 4) + t + 1))
                            k = 2 * j + kk
                            last = pe.transpose(ps[:, 4 + j, kk * T + t * P:kk * T + (t + 1) * P],
                                                src[:, t, k * P:(k + 1) * P], ident)
                    last.then_inc(t_done, 1)
                if version is None:
                    pos.add("xn", NT * parts)

            def gu(j):
                if j == 0:
                    free_fill()
                b = pos.n["fill"] % 2
                slot = piece()
                for jj in range(2):
                    k = 2 * j + jj
                    for t in range(NT):
                        c = slice(jj * 512, (jj + 1) * 512)
                        last = three(ps[:, 2 * b + t, :], x_hi[tok(k, t)], x_lo[tok(k, t)], w_hi[:, slot, c],
                                     w_lo[:, slot, c], k == 0, k == KD - 1)
                done(last)
                if j == 3:
                    pos.add("fill")

            def unit_t(b):
                pe.wait_ge(act_ready, pos("act", 2))
                pos.add("act", 2)
                for j in range(2):
                    for t in range(NT):
                        last = pe.transpose(ps[:, 2 * b, j * T + t * P:j * T + (t + 1) * P],
                                            a_tok[:, t, j * P:(j + 1) * P], ident)
                last.then_inc(act_t, 1)

            def last_down():
                slots = []
                for j in range(2):
                    slots.append(piece())
                    pos.add("piece")
                pe.wait_ge(g_free, pos("fill"))
                for t in range(NT):
                    for j in range(2):
                        last = two_threes((ps[:, 4 + 2 * t, :], ps[:, 5 + 2 * t, :]), a_hi[tok(j, t)],
                                          a_lo[tok(j, t)], w_hi[:, slots[j], :], w_lo[:, slots[j], :], j == 1)
                        if t == 0 and j == 1:
                            last.then_inc(sums_done, 1)
                        if t == 1:
                            last.then_inc(piece_used, 1)

            def down(fills):
                for j in range(2):
                    slot = piece()
                    pe.wait_ge(g_free, pos("fill", -fills))
                    for t in range(NT):
                        last = two_threes((ps[:, 4 + 2 * t, :], ps[:, 5 + 2 * t, :]), a_hi[tok(j, t)],
                                          a_lo[tok(j, t)], w_hi[:, slot, :], w_lo[:, slot, :])
                    done(last)

            def unit_step():
                for j in range(3):
                    gu(j)
                unit_t((pos.n["fill"] - 1) % 2)
                gu(3)
                down(1)

            def units(before, loops, scored=False):
                for k in range(KD):
                    wait_h(k)
                for j in range(4):
                    gu(j)
                if scored:
                    pe.wait_ge(scores_ready, 1)
                for b in range(4):
                    pe.matmul(ps[:, 4 + b, :], zero[:, :], x_hi[:, 0:2, :].rearrange("p k t -> p (k t)"),
                              start=True, stop=False, skip_group_check=True)
                for _ in range(before):
                    unit_step()
                with pos.loop(pe, loops, UNITS_PER | {"h": 0, "xn": 0}):
                    for _ in range(2):
                        unit_step()
                for _ in range(2):
                    unit_step()
                unit_t((pos.n["fill"] - 1) % 2)
                last_down()

            pe.wait_ge(in_first, 48)
            pe.wait_ge(zero_ready, 2)
            pm0 = pool_m[:, 0:4 * T].rearrange("p (w t) -> p w t", w=4)
            pm1 = pool_m[:, 4 * T:].rearrange("p (w t) -> p w t", w=4)
            pe.wait_ge(xn_ready, 2)
            for j in range(4):
                for kk in range(2):
                    k = 2 * j + kk
                    o = ps[:, 4 + j, kk * T:(kk + 1) * T]
                    pe.matmul(o, xn[:, 0, k * P:(k + 1) * P], pm0[:, j, :], start=True, stop=False)
                    last = pe.matmul(ps[:, 4 + j, kk * T + P:(kk + 1) * T], xn[:, 1, k * P:(k + 1) * P],
                                     pm1[:, j, :], start=False, stop=True)
                last.then_inc(t_done, 1)
            pos.add("xn", 2)
            for j in range(2):
                slot = piece()
                for g in range(2):
                    grp = 2 * j + g
                    for kk in range(2):
                        wait_h(2 * grp + kk)
                        for t in range(NT):
                            c = slice(g * 512 + kk * 256, g * 512 + (kk + 1) * 256)
                            last = three(ps[:, 2 * t + j, g * 256:(g + 1) * 256], x_hi[tok(2 * grp + kk, t)],
                                         x_lo[tok(2 * grp + kk, t)], w_hi[:, slot, c], w_lo[:, slot, c],
                                         kk == 0, kk == 1)
                done(last)
            pos.add("h", 8)
            pos.n["fill"] = 0
            pe.wait_ge(in_second, 64)
            pe.matmul(ps[0:HEADS, 4, 0:SPAN], rb[:, :], oneh[:, :], start=True, stop=True).then_inc(bias_mm, 1)
            pe.wait_ge(bias_rows, 1)
            norm_t(version=XR_POOL)
            units(2, 3)
            pos.add("h", 8)
            norm_t()
            for _ in range(2):
                chunk_t(h2_hi, h2_lo)
            for _ in range(2):
                chunk(h2_hi, h2_lo)
            pos.add("h", 8)
            for _ in range(2):
                chunk_t(x_hi, x_lo)
            pos.add("h", 8)
            pe.wait_ge(g_free, pos("fill"))

            pe.wait_ge(q_zero, 2)

            def scores(b):
                if b >= 2:
                    pe.wait_ge(pt0_ready, b - 1)
                    pe.wait_ge(pt1_ready, b - 1)
                base = 3 * (b % 2)
                for i in range(4):
                    h = 4 * b + i
                    q = (q_even, q_odd)[h % 2]
                    pe.matmul(ps[:, base, i * P:(i + 1) * P], q[:, h // 2, 0:P], kT[:, h // 2, 0:P],
                              start=True, stop=True)
                    last = pe.matmul(ps[:, base + 1 + i // 2, (i % 2) * T:(i % 2 + 1) * T], q[:, h // 2, P:T],
                                     kT[:, h // 2, :], start=True, stop=True)
                last.then_inc(s_done, 1)

            def transpose_probs(b):
                base = 3 * (b % 2)
                p0, p1 = probs(b)
                pe.wait_ge(p_ready, b + 1)
                for i in range(4):
                    o = base + 1 + i // 2
                    c = (i % 2) * T
                    pe.transpose(ps[:, o, c:c + P], p0[:, i, :], ident)
                    pe.transpose(ps[:, o, c + P:c + T], p1[:, i, 0:P], ident)
                    last = pe.transpose(ps[:, base, i * P:(i + 1) * P], p1[:, i, P:T], ident)
                last.then_inc(pt_done, 1)

            def attend(b):
                pe.wait_ge(pt0_ready, b + 1)
                pe.wait_ge(pt1_ready, b + 1)
                if b:
                    pe.wait_ge(o_lo, b)
                for i in range(4):
                    h = 4 * b + i
                    rows_ = slice(DH * (h % 2), DH * (h % 2) + DH)
                    c = (i // 2) * T
                    pe.matmul(ps[rows_, 6, c:c + T], v_tok[:, 0, h * DH:(h + 1) * DH], pt0[:, i, :],
                              start=True, stop=False)
                    last = pe.matmul(ps[rows_, 6, c + P:c + T], v_tok[:, 1, h * DH:(h + 1) * DH],
                                     pt1[:, i, :], start=False, stop=True)
                last.then_inc(pv_done, 1)

            def modulation(c):
                if c:
                    pe.wait_ge(ada_copied, c)
                for k in range(KD):
                    if k % 2 == 0:
                        slot = piece()
                    cols = slice((k % 2) * 512, (k % 2 + 1) * 512)
                    pe.matmul(ps[0:4, 7, :], ad[:, k, :], w_hi[:, slot, cols], start=k == 0, stop=False)
                    last = pe.matmul(ps[0:4, 7, :], ad[:, k, :], w_lo[:, slot, cols], start=False, stop=k == KD - 1)
                    if k % 2:
                        done(last)

            scores(0)
            scores(1)
            pe.wait_ge(ad_ready, 1)
            for b in range(4):
                modulation(3 * b)
                transpose_probs(b)
                modulation(3 * b + 1)
                attend(b)
                modulation(3 * b + 2)
                if b < 2:
                    scores(b + 2)
            pe.wait_ge(ada_copied, ADA_CHUNKS)
            for m in MOD_TILES:
                last = pe.transpose(ps[:, 7, 4 * m:4 * m + 4], ada_out[:, m * P:(m + 1) * P], ident[0:4, 0:4])
            last.then_inc(mod_mm, 1)
            for g, first in enumerate((2 * D, 5 * D)):
                for c in range(2):
                    last = pe.matmul(ps[:, 2 * g + c, :], const("sel_lat", 4),
                                     ada_out[:, first + c * 512:first + (c + 1) * 512], start=True, stop=True)
            last.then_inc(gate_mm, 1)
            pe.wait_ge(mod_ready, 1)
            pe.wait_ge(o_lo, 4)
            for c in range(2):
                chunk(x_hi, x_lo, banks=(4 + c, 6 + c), waits=False)
            norm_t(version=XR_WO)
            pe.wait_ge(gate_ready, 1)
            units(0, 4)
            pos.add("h", 8)
            pe.wait_ge(x_ready, XR_FFN1)
            norm_t()
            for _ in range(3):
                chunk(x_hi, x_lo)
            pos.add("h", 8)
            norm_t()
            for _ in range(2):
                chunk(x_hi, x_lo)
            pe.wait_ge(log_ready, 2)
            for d, near in enumerate(("after", "before")):
                for t in range(NT):
                    o = ps[:, 4 + 2 * d + t, :]
                    outer = t == d
                    last = pe.matmul(o, const(near), zf_c[:, d, t, :], start=True, stop=not outer)
                    if outer:
                        last = pe.matmul(o, const("ones"), zf_c[:, d, 1 - t, :], start=False, stop=True)
                last.then_inc(ctx_sums, 1)
            chunk(x_hi, x_lo)

            def flip(bank, src):
                for t in range(NT):
                    last = pe.matmul(ps[:, bank + 1 - t, :], const("flip"), src(t), start=True, stop=True)
                last.then_inc(flip_mm, 1)

            pe.wait_ge(ctx_keys_ready, 4)
            for d in range(2):
                for h in range(GLA_HEADS):
                    c = slice(h * P, (h + 1) * P)
                    for t in range(NT):
                        last = pe.matmul(ps[:, 4 + d, c], kc(d, t)[:, c], zv_c[:, t, c], start=t == 0, stop=t == 1)
                last.then_inc(ctx_state_mm, 1)
            pe.wait_ge(g_free, pos("fill", -1))
            flip(6, lambda t: xn[:, t, 0:512])
            chunk(x_hi, x_lo)
            pe.wait_ge(silu_g, 1)
            pe.wait_ge(flip_ready, 1)
            flip(6, lambda t: zq[:, 0, t, :])
            pe.wait_ge(g_free, pos("fill"))
            pe.wait_ge(ctx_state_ready, 2)
            flip(4, lambda t: zv[:, 0, t, :])
            for g in range(4):
                d, a = g // 2, g % 2
                if g:
                    pe.wait_ge(scan_tile_done, g)
                pe.wait_ge(log_ready, 3 + d)
                pe.wait_ge(k_ready, 3 + d)
                for h in range(GLA_HEADS):
                    if h >= 2:
                        pe.wait_ge(decays_ready, 9 * g + 2 * (h - 1))
                    pe.matmul(ps[:, 2 + h % 2, :], zf[:, d, a, h * P:(h + 1) * P], const("levels"), start=True,
                              stop=True).then_inc(decay_sums, 1)
                if g == 0:
                    pe.wait_ge(flip_ready, 3)
                for h in range(GLA_HEADS):
                    last = pe.matmul(ps[:, 6, h * P:(h + 1) * P], zf[:, d, a, h * P:(h + 1) * P], const("prefix"),
                                     start=True, stop=True)
                last.then_inc(decay_sums, 1)
                for h in range(GLA_HEADS):
                    c = slice(h * P, (h + 1) * P)
                    pe.transpose(ps[:, 0, c], zq[:, d, a, c], ident)
                    last = pe.transpose(ps[:, 1, c], zk[:, d, a, c], ident)
                last.then_inc(scan_transposed, 1)
                if g:
                    pe.wait_ge(side_free, g)
                chunk(x_hi, x_lo, banks=(4, 5))
                if a == 0:
                    pe.wait_ge(decays_ready, 9 * (g + 1))
                    pe.matmul(ps[:, 2, :], const("after"), zf[:, d, 0, :], start=True, stop=True).then_inc(rest_sums, 1)
                pe.wait_ge(decayed_ready, 9 * (g + 1))
                for h in range(GLA_HEADS):
                    c0 = h * P
                    last = pe.matmul(ps[:, 7, c0:c0 + P], ki[:, h, :], ex[:, 0, h, :], start=True, stop=True,
                                     skip_group_check=True)
                    for lev, half in enumerate((CHUNK, 2 * CHUNK, 4 * CHUNK), 1):
                        for s in range(0, P, 2 * half):
                            last = pe.matmul(ps[s:s + half, 7, c0 + s + half:c0 + s + 2 * half],
                                             ex[:, lev, h, s:s + half], ex[:, lev, h, s + half:s + 2 * half],
                                             start=True, stop=True, skip_group_check=True)
                last.then_inc(scan_weights_mm, 1)
                if a == 0:
                    pe.wait_ge(rest_keys_ready, d + 1)
                    for h in range(GLA_HEADS):
                        c = slice(h * P, (h + 1) * P)
                        last = pe.matmul(ps[:, 3, c], kh[:, c], zv[:, d, 0, c], start=True, stop=True)
                    last.then_inc(state_mm, 1)
                pe.wait_ge(scan_weights_ready, g + 1)
                for h in range(GLA_HEADS):
                    c = slice(h * P, (h + 1) * P)
                    pe.matmul(ps[:, 0, c], ats[:, h, :], zv[:, d, a, c], start=True, stop=False)
                    state = s0[:, d, c] if a == 0 else s1[:, h, :]
                    last = pe.matmul(ps[:, 0, c], qp[:, h, :], state, start=False, stop=True)
                last.then_inc(scan_out_mm, 1)
            pe.wait_ge(scan_tile_done, 4)
            for t in range(NT):
                last = pe.matmul(ps[:, 2 + 1 - t, :], const("flip"), o_dir[:, 1, t, :], start=True, stop=True)
            last.then_inc(back_mm, 1)
            pe.wait_ge(scan_sum_ready, 2)
            chunk(x_hi, x_lo)
            pe.wait_ge(in_merge, 48)
            pe.wait_ge(layer_norm_ready, 1)
            for t in range(NT):
                for g in range(GLA_HEADS):
                    c = slice(g * P, (g + 1) * P)
                    last = pe.matmul(ps[:, 6 + t, c], wst[:, g, :], vl[:, t, c], start=True, stop=True)
            last.then_inc(spatial_mm, 1)
            pe.wait_ge(branch_a_ready, 1)
            pe.wait_ge(side_free, 4)
            for t in range(NT):
                for h in range(GLA_HEADS):
                    last = pe.transpose(ps[:, 4 + h // 2, (h % 2) * T + t * P:(h % 2) * T + (t + 1) * P],
                                        o_dir[:, 0, t, h * P:(h + 1) * P], ident)
            last.then_inc(branch_a_t, 1)
            chunk(x_hi, x_lo)
            pe.wait_ge(branch_b_ready, 1)
            pe.wait_ge(branch_a_lo, 1)
            for t in range(NT):
                for h in range(GLA_HEADS):
                    last = pe.transpose(ps[:, 4 + h // 2, (h % 2) * T + t * P:(h % 2) * T + (t + 1) * P],
                                        u_tok[:, t, h * P:(h + 1) * P], ident)
            last.then_inc(branch_b_t, 1)
            chunk(x_hi, x_lo)
            pos.add("h", 8)
            pe.wait_ge(branch_b_lo, 1)
            for c in range(2):
                chunk(g_hi, g_lo, (0, 1, 2, 3), (4 + 2 * c, 5 + 2 * c), waits=False)
                if c == 0:
                    pe.wait_ge(g_free, pos("fill"))
                chunk(g_hi, g_lo, (4, 5, 6, 7), (c, 2 + c), waits=False)
            norm_t(2)
            for c in range(2):
                chunk(x_hi, x_lo, banks=(c, 2 + c))
            pos.add("h", 8)
            norm_t()
            pe.wait_ge(router_split, 1)
            for k in range(KD):
                wait_h(k)
            for t in range(NT):
                for k in range(KD):
                    pe.matmul(ps[:, 6 + t, 0:2 * EXPERTS], x_hi[tok(k, t)],
                              wr2[:, k, :, :].rearrange("p a e -> p (a e)"), start=k == 0, stop=False,
                              skip_group_check=True)
                    last = pe.matmul(ps[:, 6 + t, 0:EXPERTS], x_lo[tok(k, t)], wr2[:, k, 0, :], start=False,
                                     stop=k == KD - 1, skip_group_check=True)
            last.then_inc(router_mm, 1)
            units(0, EXPERTS // 2 - 1, scored=True)

        @block.scalar
        def _(act):
            pos = Pos()

            def step(ins):
                ins.then_inc(act_step, 1)
                pos.add("step")
                act.wait_ge(act_step, pos("step"))

            def prep(k):
                for _ in range(k):
                    n = pos.n.get("piece", 0)
                    if n % 2 == 0:
                        at = n // 2 % (RAW // 2)
                        times = n // RAW
                        full = 16 * (times + 1)
                        if pos.i is not None:
                            full = full + pos.i * 16
                        act.wait_ge(loaded[at], full)
                    if pos.i is not None or n >= RING:
                        act.wait_ge(piece_used, pos("piece", 1 - RING))
                    nc.scalar.activation(w_hi[:, n % RING, :], raw[:, n % RAW, :], ACT.Copy).then_inc(hi_ready, 1)
                    pos.add("piece")

            def ahead(hold=0):
                prep(min(pos.n.get("pe", 0) + RING, N_PIECES) - hold - pos.n.get("piece", 0))

            def load_sqrt():
                step(nc.scalar.activation(warm[:, :], eps[:, :], ACT.Sqrt))

            def root(parts, version=None):
                load_sqrt()
                for t in range(NT):
                    if version is not None:
                        act.wait_ge(x_ready, version - 1 + t)
                    step(nc.scalar.activation(xn[:, t, :], parts[t], ACT.Square, accum_out=ss[:, t:t + 1]))
                nc.scalar.activation(rms[:, :], ss[:, :], ACT.Sqrt, scale=1.0 / D, bias=eps[:, :]).then_inc(
                    rms_ready, 1)

            def root_sums(first, sums=None):
                load_sqrt()
                for t in range(NT):
                    if t == 0 and sums is not None:
                        act.wait_ge(sums_done, sums)
                    else:
                        act.wait_ge(piece_used, pos("pe"))
                    b = first + 2 * t
                    nc.scalar.activation(squares[:, :], ps[:, b:b + 2, :].rearrange("p a b -> p (a b)"),
                                         ACT.Square, accum_out=ss[:, t:t + 1]).then_inc(y_squared, 1)
                    pos.add("y")
                    act.wait_ge(y_squared, pos("y"))
                nc.scalar.activation(rms[:, :], ss[:, :], ACT.Sqrt, scale=1.0 / D, bias=eps[:, :]).then_inc(
                    rms_ready, 1)

            def norm_hi(dst, gain, shift, again=False):
                for j in range(4):
                    if not again:
                        act.wait_ge(t_done, pos("t_done", j + 1))
                    else:
                        act.wait_ge(h_lo, pos("h", -8 + 2 * j + 2))
                    for k in (2 * j, 2 * j + 1):
                        src = ps[:, 4 + j, (k % 2) * T:(k % 2 + 1) * T]
                        if gain is None:
                            ins = nc.scalar.activation(dst[:, k, :], src, ACT.Copy)
                        elif shift is None:
                            ins = nc.scalar.activation(dst[:, k, :], src, ACT.Copy, scale=gain[:, k:k + 1])
                        else:
                            ins = nc.scalar.activation(dst[:, k, :], src, ACT.Identity, scale=gain[:, k:k + 1],
                                                       bias=shift[:, k:k + 1])
                        ins.then_inc(h_hi, 1)
                pos.add("h", 8)
                if not again:
                    pos.add("t_done", 4)

            def unit_silu(b, routed, early=0):
                act.wait_ge(piece_used, pos("pe", -early))
                if pos.i is not None or pos.n.get("act", 0) > 0:
                    act.wait_ge(act_ready, pos("act"))
                for t in range(NT):
                    if routed:
                        ins = nc.scalar.activation(sg[:, t, :], ps[:, 2 * b + t, 0:HID], ACT.Silu)
                    else:
                        ins = nc.scalar.activation(sg[:, t, :], ps[:, 2 * b + t, 0:HID], ACT.Silu,
                                                   scale=rstd[:, t:t + 1])
                    ins.then_inc(silu_ready, 1)
                pos.add("act", 2)

            def unit_hi(b):
                act.wait_ge(act_t, pos("t", 1))
                pos.add("t")
                nc.scalar.activation(a_hi[:, :, :], ps[:, 2 * b, :].rearrange("p (j t) -> p j t", j=2),
                                     ACT.Copy).then_inc(act_hi, 1)

            def unit_step(routed, last=False):
                b = pos.n.get("fill", 0) % 2
                prep(2)
                unit_silu(b, routed)
                prep(3)
                unit_hi(b)
                pos.add("fill")
                pos.add("pe", 6)
                if last:
                    unit_silu(1 - b, routed, 2)
                prep(1)

            def units(before, loops, routed=False):
                if not routed:
                    act.wait_ge(rstd_ready, pos("rstd", 1))
                    pos.add("rstd")
                pos.add("pe", 4)
                for _ in range(before):
                    unit_step(routed)
                with pos.loop(act, loops, UNITS_PER):
                    for _ in range(2):
                        unit_step(routed)
                unit_step(routed)
                unit_step(routed, True)
                prep(2)
                unit_hi(pos.n["fill"] % 2)
                pos.add("fill")
                pos.add("pe", 2)

            def gates(zf, d, z):
                act.wait_ge(g_free, Z0 + z)
                step(nc.scalar.activation(zk[:, d, :, :], zf[:, d, :, :], ACT.Sigmoid, scale=-1.0))
                nc.scalar.activation(zf[:, d, :, :], zf[:, d, :, :], ACT.Sigmoid).then_inc(sig_ready, 1)

            def log(zf, d, n):
                act.wait_ge(f_ready, n)
                nc.scalar.activation(zf[:, d, :, :], zf[:, d, :, :], ACT.Ln).then_inc(log_ready, 1)

            act.wait_ge(in_x, 16)
            act.wait_ge(zero_ready, 2)
            root([x_tok[:, t, :] for t in range(NT)])
            ahead()
            act.wait_ge(in_first, 48)
            norm_hi(x_hi, vec("norm_mixer0"), None)
            pos.add("pe", 2)
            ahead()
            norm_hi(x_hi, vec("norm_ffn0"), None)
            root([x_tok[:, t, :] for t in range(NT)], XR_POOL)
            nc.scalar.activation(csil[:, :, :].rearrange("p k c -> p (k c)"), vec("c"), ACT.Silu).then_inc(c_silu, 1)
            units(2, 3)
            root([x_tok[:, t, :] for t in range(NT)], XR_FFN0)
            ahead(2)
            norm_hi(h2_hi, vec("kv_norm"), None)
            ahead()
            norm_hi(x_hi, vec("norm_mixer1"), None, again=True)

            def after_chunks(k):
                for _ in range(k):
                    pos.add("pe", 4)
                    ahead()

            after_chunks(6)

            def exps(b):
                p0, p1 = probs(b)
                act.wait_ge(p_raw, 2 * b + 2)
                for n, pr in enumerate((p0, p1)):
                    for i in range(4):
                        c = 4 * n + i
                        nc.scalar.activation(pr[:, i, :], pr[:, i, :], ACT.Exp, bias=mx[:, b % 2, c:c + 1],
                                             accum_out=rs[:, b % 2, c:c + 1]).then_inc(p_exp, 1)

            exps(0)
            for b in range(4):
                after_chunks(1)
                act.wait_ge(pt_done, b + 1)
                if b:
                    act.wait_ge(pv_done, b)
                base = 3 * (b % 2)
                nc.scalar.activation(pt0[:, :, :], ps[:, base + 1:base + 3, :].rearrange("p a (h q) -> p (a h) q", h=2),
                                     ACT.Copy).then_inc(pt0_ready, 1)
                after_chunks(1)
                if b < 3:
                    exps(b + 1)
                act.wait_ge(pv_done, b + 1)
                nc.scalar.activation(x_hi[:, 2 * b:2 * b + 2, :],
                                     ps[:, 6, :].rearrange("p (k t) -> p k t", k=2), ACT.Copy).then_inc(o_hi, 1)
                after_chunks(1)
            after_chunks(2)
            norm_hi(x_hi, vec("norm_ffn1"), None)
            root([x_tok[:, t, :] for t in range(NT)], XR_WO)
            units(0, 4)
            act.wait_ge(in_ctx, 16)
            root([ctx_tok[:, t, :] for t in range(NT)])
            ahead(2)
            norm_hi(x_hi, gains[:, 1, :], mod[:, :, 1])
            ahead()
            act.wait_ge(h_lo, pos("h"))
            root([x_tok[:, t, :] for t in range(NT)], XR_FFN1)
            act.wait_ge(lb_diff, 1)
            nc.scalar.activation(lb[:, :, :], lbr[:, :, 0, :], ACT.Sigmoid).then_inc(lb_ready, 1)
            after_chunks(1)
            root([x_tok[:, t, :] for t in range(NT)], XR_FIN)
            after_chunks(2)
            norm_hi(x_hi, gains[:, 0, :], mod[:, :, 0])
            gates(zf_c, 0, 2)
            gates(zf_c, 1, 2)
            after_chunks(1)
            log(zf_c, 0, 1)
            log(zf_c, 1, 2)
            act.wait_ge(g_free, Z0 + 4)
            nc.scalar.activation(zq[:, 0, :, :], zq[:, 0, :, :], ACT.Silu).then_inc(silu_g, 1)
            after_chunks(1)
            for d in range(2):
                act.wait_ge(ctx_sums, d + 1)
                for t in range(NT):
                    nc.scalar.activation(kc(d, t), ps[:, 4 + 2 * d + t, :], ACT.Exp).then_inc(ctx_decays, 1)
            after_chunks(1)
            gates(zf, 0, 6)
            act.wait_ge(flip_ready, 1)
            step(nc.scalar.activation(zk[:, 1, :, :], zf[:, 1, :, :], ACT.Sigmoid, scale=-1.0))
            nc.scalar.activation(zf[:, 1, :, :], zf[:, 1, :, :], ACT.Sigmoid).then_inc(sig_ready, 1)
            log(zf, 0, 3)
            log(zf, 1, 4)
            after_chunks(1)
            for g in range(4):
                d, a = g // 2, g % 2
                if g:
                    act.wait_ge(scan_tile_done, g)
                for h in range(GLA_HEADS):
                    act.wait_ge(decay_sums, 5 * g + h + 1)
                    nc.scalar.activation(ex[:, :, h, :], ps[:, 2 + h % 2, :].rearrange("p (l t) -> p l t", l=4),
                                         ACT.Exp).then_inc(decays_ready, 1)
                    nc.scalar.activation(ki[:, h, :], ps[:, 2 + h % 2, 0:P], ACT.Exp, scale=-1.0).then_inc(decays_ready, 1)
                act.wait_ge(decay_sums, 5 * g + 5)
                nc.scalar.activation(qp[:, :, :], ps[:, 6, :].rearrange("p (h t) -> p h t", h=4),
                                     ACT.Exp).then_inc(decays_ready, 1)
                after_chunks(1)
                if a == 0:
                    act.wait_ge(rest_sums, d + 1)
                    nc.scalar.activation(kh[:, :], ps[:, 2, :], ACT.Exp).then_inc(rest_decays, 1)
                dst, fn, ready = ((vl, ACT.Gelu_apprx_tanh, gelu_r), (u_tok, ACT.Gelu_apprx_tanh, gelu_r),
                                  (sgl, ACT.Silu, silu_g), (ga0, ACT.Sigmoid, gate_r))[g]
                act.wait_ge(side_free, g + 1)
                nc.scalar.activation(dst[:, :, :], dst[:, :, :], fn).then_inc(ready, 1)
                if g == 2:
                    act.wait_ge(merge_squares, 1)
                    nc.scalar.activation(rms[:, :], ss[:, :], ACT.Sqrt, scale=1.0 / CM, bias=eps[:, :]
                                         ).then_inc(merge_rms, 1)
            def function(c, dst):
                act.wait_ge(g_free, Z0 + 8 + c)
                nc.scalar.activation(dst[:, :, :], dst[:, :, :], ACT.Sigmoid).then_inc(gate_r, 1)

            act.wait_ge(merge_squares, 2)
            nc.scalar.activation(st8b[:, :], st8[:, :], ACT.Sqrt, scale=1.0 / P, bias=eps[:, :]).then_inc(merge_rms, 1)
            after_chunks(1)
            function(0, ga1)
            act.wait_ge(branch_a_t, 1)
            ga_, _ = FEAT["g_hgrn"]
            nc.scalar.activation(g_hi[:, 0:4, :], ps[:, 4:6, :].rearrange("p a (h t) -> p (a h) t", h=2), ACT.Copy,
                                 scale=ft[:, ga_:ga_ + 1]).then_inc(branch_a_hi, 1)
            after_chunks(1)
            function(1, gb0)
            act.wait_ge(branch_b_t, 1)
            nc.scalar.activation(g_hi[:, 4:8, :], ps[:, 4:6, :].rearrange("p a (h t) -> p (a h) t", h=2),
                                 ACT.Copy).then_inc(branch_b_hi, 1)
            after_chunks(1)
            function(2, gb1)
            for _ in range(4):
                pos.add("pe", 2)
                ahead()
            norm_hi(x_hi, None, None)
            after_chunks(1)
            pos.add("pe", 4)
            ahead(1)
            root_sums(0)
            root([x_tok[:, t, :] for t in range(NT)], XR_MIX)
            ahead()
            norm_hi(x_hi, gains[:, 2, :], mod[:, 24:, 0])
            act.wait_ge(logits_ready, 1)
            nc.scalar.activation(sc[:, :, :], sc[:, :, :], ACT.Sigmoid).then_inc(scores_ready, 1)
            units(0, EXPERTS // 2 - 1, routed=True)
            root_sums(4, 3)

        @block.vector
        def _(dve):
            pos = Pos()

            def step(ins):
                ins.then_inc(dve_step, 1)
                pos.add("step")
                dve.wait_ge(dve_step, pos("step"))

            def prep(k):
                for _ in range(k):
                    n = pos.n.get("piece", 0)
                    dve.wait_ge(hi_ready, pos("piece", 1))
                    nc.vector.tensor_tensor(w_lo[:, n % RING, :], raw[:, n % RAW, :],
                                            w_hi[:, n % RING, :].bitcast(f32), ALU.subtract).then_inc(lo_ready, 1)
                    pos.add("piece")

            def ahead(hold=0):
                prep(min(pos.n.get("pe", 0) + RING, N_PIECES) - hold - pos.n.get("piece", 0))

            def inverse():
                dve.wait_ge(rms_ready, pos("rms", 1))
                pos.add("rms")
                step(nc.vector.reciprocal(rstd[:, :], rms[:, :]))

            def inverse_shared():
                dve.wait_ge(rms_ready, pos("rms", 1))
                pos.add("rms")
                nc.vector.reciprocal(rstd[:, :], rms[:, :]).then_inc(rstd_ready, 1)
                pos.add("rstd")
                dve.wait_ge(rstd_ready, pos("rstd"))

            def norm_x(src):
                inverse()
                for t in range(NT):
                    nc.vector.tensor_scalar(xn[:, t, :], src[:, t, :], rstd[:, t:t + 1], None,
                                            ALU.mult).then_inc(xn_ready, 1)

            def norm_lo(targets):
                for dst_hi, dst, gain, shift in targets:
                    for k in range(KD):
                        dve.wait_ge(h_hi, pos("h", 2 * (k // 2) + 2))
                        src = ps[:, 4 + k // 2, (k % 2) * T:(k % 2 + 1) * T]
                        high = dst_hi[:, k, :].bitcast(f32)
                        if gain is None:
                            ins = nc.vector.tensor_tensor(dst[:, k, :], src, high, ALU.subtract)
                        elif shift is None:
                            ins = nc.vector.scalar_tensor_tensor(dst[:, k, :], src, gain[:, k:k + 1], high, ALU.mult,
                                                                 ALU.subtract)
                        else:
                            nc.vector.tensor_scalar(whole(k), src, gain[:, k:k + 1],
                                                    shift[:, k:k + 1], ALU.mult, ALU.add).then_inc(h_full, 1)
                            continue
                        ins.then_inc(h_lo, 1)
                    pos.add("h", 8)

            def wide(t, first=4):
                return ps[:, first + 2 * t:first + 2 * t + 2, :].rearrange("p a b -> p (a b)")

            def add_residual(sums=None):
                for t in range(NT):
                    if t == 0 and sums is not None:
                        dve.wait_ge(sums_done, sums)
                    else:
                        dve.wait_ge(piece_used, pos("pe"))
                    nc.vector.tensor_tensor(x_tok[:, t, :], x_tok[:, t, :], wide(t), ALU.add).then_inc(x_ready, 1)

            def unit_act(b, weight):
                for t in range(NT):
                    dve.wait_ge(silu_ready, pos("act", t + 1))
                    up = ps[:, 2 * b + t, HID:2 * HID]
                    factor = rstd[:, t:t + 1] if weight is None else comb[:, t, weight]
                    nc.vector.scalar_tensor_tensor(a_tok[:, t, :], sg[:, t, :], factor, up, ALU.mult,
                                                   ALU.mult).then_inc(act_ready, 1)
                pos.add("act", 2)

            def unit_lo(b):
                dve.wait_ge(act_hi, pos("t", 1))
                pos.add("t")
                nc.vector.tensor_tensor(a_lo[:, :, :], ps[:, 2 * b, :].rearrange("p (j t) -> p j t", j=2),
                                        a_hi[:, :, :].bitcast(f32), ALU.subtract).then_inc(g_free, 1)

            def unit_step(weight, last=None):
                b = pos.n.get("fill", 0) % 2
                prep(2)
                unit_act(b, weight)
                prep(3)
                unit_lo(b)
                pos.add("fill")
                pos.add("pe", 6)
                if last is not None:
                    unit_act(1 - b, *last)
                prep(1)

            def units(before, loops, routed=False):
                def weight(e):
                    return slice(e, e + 1) if routed else None

                pos.add("pe", 4)
                for _ in range(before):
                    unit_step(None)
                with pos.loop(dve, loops, UNITS_PER) as i:
                    for e in range(2):
                        unit_step(bass.ds(i * 2 + e, 1) if routed else None)
                unit_step(weight(2 * loops))
                unit_step(weight(2 * loops + 1), (weight(2 * loops + 2),))
                prep(2)
                unit_lo(pos.n["fill"] % 2)
                pos.add("fill")
                pos.add("pe", 2)

            def copy_queries(c):
                b = pos.n["fill"] % 2
                pos.add("fill")
                dve.wait_ge(piece_used, pos("pe"))
                k = slice(4 * c, 4 * c + 4)
                for r, dst in ((slice(0, DH), q_even), (slice(DH, P), q_odd)):
                    ins = nc.vector.tensor_copy(dst[r, k, :], ps[r, 2 * b:2 * b + 2, :].rearrange(
                        "p a (k t) -> p (a k) t", k=2))
                    if r.start:
                        ins.then_inc(g_free, 1)
                    else:
                        step(ins)

            def copy_fill(dst, transposed=False):
                b = pos.n["fill"] % 2
                pos.add("fill")
                dve.wait_ge(piece_used, pos("pe"))
                src = ps[:, 2 * b:2 * b + 2, :]
                if transposed:
                    src = src.rearrange("p a (k t) -> p (a k) t", k=2)
                nc.vector.tensor_copy(dst, src).then_inc(g_free, 1)

            dve.wait_ge(in_x, 16)
            norm_x(x_tok)
            ahead()
            dve.wait_ge(in_first, 48)
            norm_lo([(x_hi, x_lo, vec("norm_mixer0"), None)])
            pos.add("pe", 2)
            ahead()
            dve.wait_ge(in_second, 64)
            dve.wait_ge(piece_used, pos("pe"))
            for t in range(NT):
                step(nc.vector.tensor_tensor(xn[:, t, :], ps[:, 2 * t:2 * t + 2, :].rearrange("p a b -> p (a b)"),
                                             pool_s[:, :], ALU.mult))
                nc.vector.tensor_tensor(x_tok[:, t, :], x_tok[:, t, :], xn[:, t, :], ALU.add).then_inc(x_ready, 1)
            dve.wait_ge(bias_mm, 1)
            step(nc.vector.tensor_copy(rv[:, :], ps[0:HEADS, 4, 0:SPAN]))
            nc.vector.memset(rv[:, T:SPAN], -BIG).then_inc(bias_rows, 1)
            norm_lo([(x_hi, x_lo, vec("norm_ffn0"), None)])
            inverse_shared()
            dve.wait_ge(c_silu, 1)
            step(nc.vector.tensor_copy(ad[:, :, 0:2], csil[:, :, :]))
            nc.vector.tensor_tensor(ad[:, :, 2:4], csil[:, :, :], ad[:, :, 0:2].bitcast(f32),
                                    ALU.subtract).then_inc(ad_ready, 1)
            units(2, 3)
            add_residual(1)
            norm_x(x_tok)
            ahead(2)
            norm_lo([(h2_hi, h2_lo, vec("kv_norm"), None)])
            ahead()
            norm_lo([(x_hi, x_lo, vec("norm_mixer1"), None)])
            dve.wait_ge(bias_in, 16)
            for dst, transposed in ((kT[:, 0:4, :], True), (kT[:, 4:8, :], True), (v_tok[:, :, 0:512], False),
                                    (v_tok[:, :, 512:], False)):
                pos.add("pe", 4)
                ahead(1)
                copy_fill(dst, transposed=transposed)
                ahead()
            for c in range(2):
                pos.add("pe", 4)
                ahead(1)
                copy_queries(c)
                ahead()

            def raw_scores(b):
                p0, p1 = probs(b)
                base = 3 * (b % 2)
                dve.wait_ge(s_done, b + 1)
                if b >= 2:
                    dve.wait_ge(pt_done, b - 1)
                for n, (pr, src, rel) in enumerate((
                        (p0, ps[:, base, :].rearrange("p (h k) -> p h k", h=4), bias[:, 4 * b:4 * b + 4, P:T]),
                        (p1, ps[:, base + 1:base + 3, :].rearrange("p a (h k) -> p (a h) k", h=2),
                         bias[:, 4 * b:4 * b + 4, :]))):
                    step(nc.vector.scalar_tensor_tensor(pr, src, DH ** -0.5, rel, ALU.mult, ALU.add))
                    nc.vector.reduce_max(mx[:, b % 2, 4 * n:4 * n + 4], pr, AXX, negate=True).then_inc(p_raw, 1)

            def copy_modulation(c):
                pos.add("pe", 4)
                ahead(1)
                dve.wait_ge(piece_used, pos("pe"))
                nc.vector.tensor_copy(ada_out[:, c * 512:(c + 1) * 512], ps[0:4, 7, :]).then_inc(ada_copied, 1)
                ahead()

            raw_scores(0)
            for b in range(4):
                p0, p1 = probs(b)
                dve.wait_ge(p_exp, 8 * (b + 1))
                step(nc.vector.reciprocal(rr[:, :], rs[:, b % 2, :]))
                step(nc.vector.tensor_tensor(p0, p0, rr[:, 0:4].unsqueeze(2).to_broadcast([P, 4, P]), ALU.mult))
                nc.vector.tensor_tensor(p1, p1, rr[:, 4:8].unsqueeze(2).to_broadcast([P, 4, T]),
                                        ALU.mult).then_inc(p_ready, 1)
                copy_modulation(3 * b)
                dve.wait_ge(pt_done, b + 1)
                if b:
                    dve.wait_ge(pv_done, b)
                nc.vector.tensor_copy(pt1[:, :, :], ps[:, 3 * (b % 2), :].rearrange("p (h q) -> p h q", h=4)
                                      ).then_inc(pt1_ready, 1)
                if b < 3:
                    raw_scores(b + 1)
                copy_modulation(3 * b + 1)
                dve.wait_ge(o_hi, b + 1)
                nc.vector.tensor_tensor(x_lo[:, 2 * b:2 * b + 2, :],
                                        ps[:, 6, :].rearrange("p (k t) -> p k t", k=2),
                                        x_hi[:, 2 * b:2 * b + 2, :].bitcast(f32), ALU.subtract).then_inc(o_lo, 1)
                copy_modulation(3 * b + 2)
            dve.wait_ge(mod_mm, 1)
            a, b_ = FEAT["b_ada"]
            for m in (slice(0, 16), slice(24, 40)):
                parts = ps[:, 7, 4 * m.start:4 * m.stop].rearrange("p (m c) -> p m c", c=4)
                shape = [P, m.stop - m.start, 2]
                step(nc.vector.tensor_tensor(mod[:, m, :], parts[:, :, 0:2],
                                             ft[:, a + m.start:a + m.stop].unsqueeze(2).to_broadcast(shape), ALU.add))
                step(nc.vector.tensor_tensor(mod[:, m, :], mod[:, m, :], parts[:, :, 2:4], ALU.add))
            for n, (g, m, c) in enumerate((("g_pre_mix", 8, 0), ("g_pre_mix", 8, 1), ("g_pre_ffn", 32, 0))):
                ins = nc.vector.scalar_tensor_tensor(gains[:, n, :], mod[:, m:m + 8, c], 1.0, vec(g), ALU.add, ALU.mult)
                if n < 2:
                    step(ins)
                else:
                    ins.then_inc(mod_ready, 1)
            pos.add("pe", 4)
            ahead()
            dve.wait_ge(gate_mm, 1)
            step(nc.vector.tensor_copy(gt1[:, :], ps[:, 0:2, :].rearrange("p a b -> p (a b)")))
            nc.vector.tensor_copy(gt2[:, :], ps[:, 2:4, :].rearrange("p a b -> p (a b)")).then_inc(gate_ready, 1)
            pos.add("pe", 4)
            ahead(1)
            add_residual()
            ahead()
            norm_lo([(x_hi, x_lo, vec("norm_ffn1"), None)])
            inverse_shared()
            units(0, 4)
            norm_x(ctx_tok)
            add_residual(2)
            ahead(2)
            norm_lo([(x_hi, x_lo, gains[:, 1, :], mod[:, :, 1])])
            ahead()
            inverse()
            dve.wait_ge(in_fin, 16)
            for t in range(NT):
                nc.vector.scalar_tensor_tensor(x_tok[:, t, :], x_tok[:, t, :], rstd[:, t:t + 1], fin_g[:, :],
                                               ALU.mult, ALU.mult).then_inc(x_ready, 1)

            def take(dst):
                pos.add("pe", 4)
                ahead(1)
                b = pos.n["fill"] % 2
                pos.add("fill")
                dve.wait_ge(piece_used, pos("pe"))
                nc.vector.tensor_copy(dst, ps[:, 2 * b:2 * b + 2, :]).then_inc(g_free, 1)
                ahead()

            def forget(zf, d, n):
                dve.wait_ge(sig_ready, n)
                for t in range(NT):
                    nc_ = nc.vector.tensor_tensor(zk[:, d, t, :], zk[:, d, t, :], oml[:, d, :], ALU.mult)
                    if t == 0:
                        step(nc_)
                    else:
                        nc_.then_inc(k_ready, 1)
                    step(nc.vector.tensor_tensor(zf[:, d, t, :], zf[:, d, t, :], oml[:, d, :], ALU.mult))
                    f = nc.vector.tensor_tensor(zf[:, d, t, :], zf[:, d, t, :], lb[:, d, :], ALU.add)
                    if t == 0:
                        step(f)
                    else:
                        f.then_inc(f_ready, 1)

            take(zf_c[:, 0, :, :])
            norm_x(x_tok)
            take(zf_c[:, 1, :, :])
            dve.wait_ge(lb_ready, 1)
            step(nc.vector.tensor_scalar(oml[:, :, :], lb[:, :, :], -1.0, 1.0, ALU.mult, ALU.add))
            take(zv_c[:, :, :])
            norm_lo([(x_hi, x_lo, gains[:, 0, :], mod[:, :, 0])])
            forget(zf_c, 0, 1)
            dve.wait_ge(gates_done, 2)
            take(zq[:, 0, :, :])
            forget(zf_c, 1, 2)
            take(xn[:, :, 0:512])
            for d in range(2):
                for t in range(NT):
                    dve.wait_ge(ctx_decays, 2 * d + t + 1)
                    nc.vector.tensor_tensor(kc(d, t), kc(d, t), zk[:, d, t, :], ALU.mult).then_inc(ctx_keys_ready, 1)
            take(zf[:, 0, :, :])
            for d in range(2):
                dve.wait_ge(ctx_state_mm, d + 1)
                nc.vector.tensor_copy(s0[:, d, :], ps[:, 4 + d, :]).then_inc(ctx_state_ready, 1)

            def take_flipped(r, dst, bank):
                dve.wait_ge(flip_mm, r + 1)
                nc.vector.tensor_copy(dst[:, 1, :, :], ps[:, bank:bank + 2, :]).then_inc(flip_ready, 1)

            take_flipped(0, zf, 6)
            forget(zf, 0, 3)
            forget(zf, 1, 4)
            take(zv[:, 0, :, :])
            take_flipped(1, zq, 6)
            take_flipped(2, zv, 4)
            dve.wait_ge(ats_zero, 1)
            for g in range(4):
                d, a = g // 2, g % 2
                dve.wait_ge(scan_transposed, g + 1)
                dve.wait_ge(decays_ready, 9 * (g + 1))
                if a == 0:
                    step(nc.vector.tensor_copy(dt[:, :, :], qp[:, :, P - 1:P]))
                qt = ps[:, 0, :].rearrange("p (h t) -> p h t", h=4)
                kt = ps[:, 1, :].rearrange("p (h t) -> p h t", h=4)
                for dst, src in ((ex[:, 0, :, :], qt), (ki[:, :, :], kt), (qp[:, :, :], qt)):
                    nc.vector.tensor_tensor(dst, dst, src, ALU.mult).then_inc(decayed_ready, 1)
                for lev, half in enumerate((CHUNK, 2 * CHUNK, 4 * CHUNK), 1):
                    for side, src in ((1, qt), (0, kt)):
                        dst = ex[:, lev, :, :].rearrange("p h (b s u) -> p h b s u", s=2, u=half)[:, :, :, side, :]
                        part = src.rearrange("p h (b s u) -> p h b s u", s=2, u=half)[:, :, :, side, :]
                        nc.vector.tensor_tensor(dst, dst, part, ALU.mult).then_inc(decayed_ready, 1)
                pos.add("pe", 4)
                ahead(1)
                dve.wait_ge(piece_used, pos("pe"))
                nc.vector.tensor_copy((vl, u_tok, sgl, ga0)[g][:, :, :], ps[:, 4:6, :]).then_inc(side_free, 1)
                ahead()
                dve.wait_ge(scan_weights_mm, g + 1)
                nc.vector.copy_predicated(ats[:, :, :], causal[:, :, :],
                                          ps[:, 7, :].rearrange("p (h t) -> p h t", h=4)).then_inc(scan_weights_ready, 1)
                if a == 0:
                    dve.wait_ge(rest_decays, d + 1)
                    nc.vector.tensor_tensor(kh[:, :], kh[:, :], zk[:, d, 0, :], ALU.mult).then_inc(rest_keys_ready, 1)
                    dve.wait_ge(state_mm, d + 1)
                    for h in range(GLA_HEADS):
                        c = slice(h * P, (h + 1) * P)
                        step(nc.vector.scalar_tensor_tensor(s1[:, h, :], s0[:, d, c], dt[:, h, :], ps[:, 3, c],
                                                            ALU.mult, ALU.add))
                dve.wait_ge(scan_out_mm, g + 1)
                nc.vector.tensor_copy(o_dir[:, d, a, :], ps[:, 0, :]).then_inc(scan_tile_done, 1)
                if g == 1:
                    dve.wait_ge(gelu_r, 1)
                    step(nc.vector.reduce_sum(mean[:, :], vl[:, :, :], AXX))
                    step(nc.vector.tensor_scalar(mean[:, :], mean[:, :], -1.0 / CM, None, ALU.mult))
                    for t in range(NT):
                        step(nc.vector.tensor_scalar(vl[:, t, :], vl[:, t, :], mean[:, t:t + 1], None, ALU.add))
                    step(nc.vector.tensor_tensor(sq[:, :, :], vl[:, :, :], vl[:, :, :], ALU.mult))
                    nc.vector.reduce_sum(ss[:, :], sq[:, :, :], AXX).then_inc(merge_squares, 1)
                if g == 2:
                    dve.wait_ge(in_merge, 48)
                    dve.wait_ge(merge_rms, 1)
                    step(nc.vector.reciprocal(rstd[:, :], rms[:, :]))
                    for t in range(NT):
                        step(nc.vector.scalar_tensor_tensor(vl[:, t, :], vl[:, t, :], rstd[:, t:t + 1], ln_g[:, :],
                                                            ALU.mult, ALU.mult))
                        ins = nc.vector.tensor_tensor(vl[:, t, :], vl[:, t, :], ln_b[:, :], ALU.add)
                        if t == 0:
                            step(ins)
                        else:
                            ins.then_inc(layer_norm_ready, 1)
            dve.wait_ge(back_mm, 1)
            for t in range(NT):
                nc.vector.tensor_tensor(o_dir[:, 0, t, :], o_dir[:, 0, t, :], ps[:, 2 + t, :],
                                        ALU.add).then_inc(scan_sum_ready, 1)
            o = o_dir[:, 0, :, :]
            o8 = o.rearrange("p t (h n) -> p (t h) n", h=GLA_HEADS)
            sq8 = sq[:, :, :].rearrange("p t (h n) -> p (t h) n", h=GLA_HEADS)
            dve.wait_ge(scan_sum_ready, 2)
            step(nc.vector.tensor_tensor(sq[:, :, :], o, o, ALU.mult))
            nc.vector.reduce_sum(st8[:, :], sq8, AXX).then_inc(merge_squares, 1)
            dve.wait_ge(merge_rms, 2)
            step(nc.vector.reciprocal(st8b[:, :], st8b[:, :]))
            step(nc.vector.tensor_tensor(o8, o8, st8b[:, :].unsqueeze(2).to_broadcast([P, 8, P]), ALU.mult))
            dve.wait_ge(silu_g, 2)
            nc.vector.tensor_tensor(o, o, sgl[:, :, :], ALU.mult).then_inc(branch_a_ready, 1)
            take(ga1[:, :, :])
            gh, _ = FEAT["g_hgrn"]
            dve.wait_ge(branch_a_hi, 1)
            nc.vector.scalar_tensor_tensor(g_lo[:, 0:4, :], ps[:, 4:6, :].rearrange("p a (h t) -> p (a h) t", h=2),
                                           ft[:, gh:gh + 1], g_hi[:, 0:4, :].bitcast(f32), ALU.mult,
                                           ALU.subtract).then_inc(branch_a_lo, 1)
            dve.wait_ge(spatial_mm, 1)
            dve.wait_ge(gelu_r, 2)
            bs, _ = FEAT["b_spatial"]
            for t in range(NT):
                for g in range(GLA_HEADS):
                    c = slice(g * P, (g + 1) * P)
                    ins = nc.vector.scalar_tensor_tensor(u_tok[:, t, c], ps[:, 6 + t, c], ft[:, bs + g:bs + g + 1],
                                                         u_tok[:, t, c], ALU.add, ALU.mult)
                    if t == 1 and g == 3:
                        ins.then_inc(branch_b_ready, 1)
                    else:
                        step(ins)
            take(gb0[:, :, :])
            dve.wait_ge(branch_b_hi, 1)
            nc.vector.tensor_tensor(g_lo[:, 4:8, :], ps[:, 4:6, :].rearrange("p a (h t) -> p (a h) t", h=2),
                                    g_hi[:, 4:8, :].bitcast(f32), ALU.subtract).then_inc(branch_b_lo, 1)
            take(gb1[:, :, :])
            for c in range(2):
                cols = slice(c * 512, (c + 1) * 512)
                ga, gb = ((ga0, gb0), (ga1, gb1))[c]
                pos.add("pe", 2)
                ahead()
                dve.wait_ge(gate_r, 3 + c)
                dve.wait_ge(piece_used, pos("pe"))
                for t in range(NT):
                    step(nc.vector.tensor_tensor(ga[:, t, :], ga[:, t, :], ps[:, 4 + 2 * c + t, :], ALU.mult))
                pos.add("pe", 2)
                ahead(1)
                dve.wait_ge(piece_used, pos("pe"))
                for t in range(NT):
                    step(nc.vector.tensor_tensor(gb[:, t, :], gb[:, t, :], ps[:, c + 2 * t, :], ALU.mult))
                    nc.vector.tensor_tensor(xn[:, t, cols], ga[:, t, :], gb[:, t, :], ALU.add).then_inc(xn_ready, 1)
            ahead()
            norm_lo([(x_hi, x_lo, None, None)])
            pos.add("pe", 4)
            ahead()
            pos.add("pe", 4)
            ahead(1)

            def gated_residual(first, gate, ready):
                for t in range(NT):
                    dve.wait_ge(y_squared, pos("y", 1))
                    pos.add("y")
                    ins = nc.vector.tensor_tensor(xn[:, t, :], wide(t, first), gate[:, :], ALU.mult)
                    if t == 0:
                        step(ins)
                    else:
                        ins.then_inc(dve_step, 1)
                        pos.add("step")
                inverse()
                for t in range(NT):
                    nc.vector.scalar_tensor_tensor(x_tok[:, t, :], xn[:, t, :], rstd[:, t:t + 1], x_tok[:, t, :],
                                                   ALU.mult, ALU.add).then_inc(ready, 1)

            gated_residual(0, gt1, x_ready)
            norm_x(x_tok)
            ahead()
            dve.wait_ge(in_router, 32)
            step(nc.vector.tensor_copy(wr2[:, :, 0, :], wr[:, :, :]))
            nc.vector.tensor_tensor(wr2[:, :, 1, :], wr[:, :, :], wr2[:, :, 0, :].bitcast(f32), ALU.subtract
                                    ).then_inc(router_split, 1)
            norm_lo([(x_hi, x_lo, gains[:, 2, :], mod[:, 24:, 0])])
            dve.wait_ge(router_mm, 1)
            step(nc.vector.tensor_copy(t64[:, :, :], ps[:, 6:8, EXPERTS:2 * EXPERTS]))
            nc.vector.tensor_tensor(sc[:, :, :], t64[:, :, :], ps[:, 6:8, 0:EXPERTS], ALU.add).then_inc(logits_ready, 1)
            dve.wait_ge(scores_ready, 1)
            step(nc.vector.tensor_tensor(sel[:, :, :], sc[:, :, :], br[:, :].unsqueeze(1).to_broadcast([P, NT, EXPERTS]),
                                         ALU.add))
            for t in range(NT):
                for g in range(GROUPS):
                    step(nc.vector.max(best[:, t, g, :], sel[:, t, g * 8:(g + 1) * 8]))
            step(nc.vector.tensor_tensor(gsc[:, :, :], best[:, :, :, 0], best[:, :, :, 1], ALU.add))
            for t in range(NT):
                step(nc.vector.max(gm8[:, t, :], gsc[:, t, :]))
            step(nc.vector.memset(gm8[:, :, 4:8], BIG))
            for t in range(NT):
                step(nc.vector.match_replace(gkeep[:, t, :], gm8[:, t, :], gsc[:, t, :], BIG))
            step(nc.vector.tensor_scalar(gkeep2[:, :, :], gkeep[:, :, :], BIG, None, ALU.is_ge))
            step(nc.vector.tensor_scalar(gkeep2[:, :, :], gkeep2[:, :, :], BIG, -BIG, ALU.mult, ALU.add))
            step(nc.vector.tensor_tensor(
                sel[:, :, :].rearrange("p t (g e) -> p (t g) e", g=GROUPS),
                sel[:, :, :].rearrange("p t (g e) -> p (t g) e", g=GROUPS),
                gkeep2[:, :, :].rearrange("p t g -> p (t g)").unsqueeze(2).to_broadcast([P, NT * GROUPS, 8]), ALU.add))
            for t in range(NT):
                step(nc.vector.max(gm8[:, t, :], sel[:, t, :]))
                step(nc.vector.match_replace(t64[:, t, :], gm8[:, t, :], sel[:, t, :], BIG))
            step(nc.vector.tensor_scalar(t64[:, :, :], t64[:, :, :], BIG, None, ALU.is_ge))
            step(nc.vector.tensor_tensor(t64[:, :, :], t64[:, :, :], sc[:, :, :], ALU.mult))
            step(nc.vector.reduce_sum(wsum[:, :], t64[:, :, :], AXX))
            step(nc.vector.reciprocal(wsum[:, :], wsum[:, :]))
            for t in range(NT):
                step(nc.vector.tensor_scalar(comb[:, t, 0:EXPERTS], t64[:, t, :], wsum[:, t:t + 1], ROUTED_SCALE,
                                             ALU.mult, ALU.mult))
            step(nc.vector.memset(comb[:, :, EXPERTS:], 1.0))
            units(0, EXPERTS // 2 - 1, routed=True)
            gated_residual(4, gt2, res_ready)


def kernel(**inputs):
    import concourse.bacc as _bacc
    from concourse.bass_utils import run_bass_kernel_spmd as _run

    nc, arrays, _ = assemble(_bacc, inputs)
    r = _run(nc, [arrays], core_ids=[0])
    return r.results[0]["out_dram"].reshape(1, T, D)


def stream_of(a):
    pieces = []

    def cols(w, c0, width=512):
        k = w.shape[0] // P
        part = w[:, c0:c0 + width].reshape(k // 2, 2, P, width)
        pieces.extend(part.transpose(0, 2, 1, 3).reshape(k // 2, P, 2 * width))

    def unit_gu(w, c_gate, c_up):
        part = np.stack([w[:, c_gate:c_gate + HID], w[:, c_up:c_up + HID]], 1).reshape(KD // 2, 2, P, 2 * HID)
        pieces.extend(part.transpose(0, 2, 1, 3).reshape(KD // 2, P, 4 * HID))

    def unit_down(w, r0):
        pieces.extend(w[r0:r0 + HID].reshape(2, P, D))

    def units(gus, downs):
        unit_gu(*gus[0])
        for g, d in zip(gus[1:] + [None], downs):
            if g is not None:
                unit_gu(*g)
            unit_down(*d)

    def ffn(layer):
        gu, down = a["w_gate_up"][layer], a["w_down"][layer]
        units([(gu, u * HID, D_FF + u * HID) for u in range(FFN_UNITS)], [(down, u * HID) for u in range(FFN_UNITS)])

    pw = a["pool_w"][0].reshape(2, 2, 2, P, 256)
    pieces.extend(pw.transpose(0, 3, 1, 2, 4).reshape(2, P, 1024))
    ffn(0)
    for c in range(4):
        cols(a["w_kv"], c * 512)
    for c in range(2):
        cols(a["w_q"][0], c * 512)
    for c in range(ADA_CHUNKS):
        cols(a["w_ada_2"][0], c * 512)
    for c in range(2):
        cols(a["w_o"][0], c * 512)
    ffn(1)
    w_in = a["w_in_2"][0]
    for c in (1, 2, 3):
        cols(w_in, c * 512)
    for c in (0, 2, 1, 3, 6, 5, 4, 7, 8, 9, 10):
        cols(w_in, c * 512)
    for c in range(2):
        cols(a["w_branch_a_2"][0], c * 512)
        cols(a["w_branch_b_2"][0], c * 512)
    for c in range(2):
        cols(a["w_out_2"][0], c * 512)
    egu, edn = a["w_expert_gu_2"][0], a["w_expert_down_2"][0]
    units([(egu[e], 0, HID) for e in range(EXPERTS)] + [(a["w_shared_gu_2"][0], 0, HID)],
          [(edn[e], 0) for e in range(EXPERTS)] + [(a["w_shared_down_2"][0], 0)])
    out = np.empty((len(pieces) // 2, P, 2, PIECE), np.float32)
    for n, p in enumerate(pieces):
        out[n // 2, :, n % 2, :] = p
    return out.reshape(len(pieces) // 2, P, 2 * PIECE)


def layouts(a):
    consts, pool, causal, buckets = constants()
    feat = np.zeros((P, NFEAT), np.float32)

    def vec(name, v):
        lo, hi = FEAT[name]
        feat[:, lo:hi] = v.reshape(hi - lo, P).T

    vec("norm_mixer0", a["norm_mixer"][0])
    vec("norm_mixer1", a["norm_mixer"][1])
    vec("norm_ffn0", a["norm_ffn"][0])
    vec("norm_ffn1", a["norm_ffn"][1])
    vec("kv_norm", a["kv_norm"])
    vec("g_pre_mix", a["g_pre_mix_2"][0])
    vec("g_pre_ffn", a["g_pre_ffn_2"][0])
    vec("g_hgrn", a["g_hgrn_out_2"][0])
    vec("b_ada", a["b_ada_2"][0])
    lo, hi = FEAT["b_spatial"]
    feat[:, lo:hi] = a["b_spatial_2"][0]
    lo, hi = FEAT["c"]
    feat[:, lo:hi] = np.stack([a["c_2"][0].reshape(KD, P).T, a["c_ctx_2"].reshape(KD, P).T], 2).reshape(P, 2 * KD)
    rows = np.zeros((1, NROWS), np.float32)
    for name, v in (("pool_scale", a["pool_scale"]), ("final_norm", a["final_norm"]),
                    ("gt1_b", a["b_ada_2"][0, 2 * D:3 * D]), ("gt2_b", a["b_ada_2"][0, 5 * D:]),
                    ("g_post_mix", a["g_post_mix_2"]), ("g_post_ffn", a["g_post_ffn_2"]), ("ln_g", a["cm_ln_g_2"]),
                    ("ln_b", a["cm_ln_b_2"]), ("lb", a["lb_logits_2"]), ("b_router", a["b_router_2"])):
        lo, hi = ROWS[name]
        rows[0, lo:hi] = v.reshape(-1)
    return {
        "stream": stream_of(a), "x": a["x"][0], "ctx": a["ctx_2"][0], "feat": feat, "rows": rows, "consts": consts,
        "pool_c": pool, "causal_c": causal, "buckets_c": buckets, "rel_bias": a["rel_bias"],
        "w_router": a["w_router_2"][0].reshape(KD, P, EXPERTS).transpose(1, 0, 2).reshape(P, KD * EXPERTS),
        "w_spatial": a["w_spatial_2"][0].transpose(2, 0, 1).reshape(P, GLA_HEADS * P),
    }


def assemble(bacc, inputs):
    nc = bacc.Bacc("TRN2", target_bir_lowering=False, num_devices=1)
    arrays, args = {}, {}
    for name, v in layouts({k: np.asarray(v) for k, v in inputs.items()}).items():
        v = np.ascontiguousarray(v)
        arrays[name + "_dram"] = v
        args[name] = nc.dram_tensor(name + "_dram", v.shape, mybir.dt.from_np(v.dtype), kind="ExternalInput").ap()
    args["out"] = nc.dram_tensor("out_dram", (T, D), mybir.dt.float32, kind="ExternalOutput").ap()
    program(nc, **args)
    return nc, arrays, args
```
